# Optimizing a Trainium2 kernel written in Bass

```python
import jax, jax.numpy as jnp
from jax import lax
import numpy as np
import jax
import jax.numpy as jnp

D_MODEL = 1024
BATCH = 1
SEQ = 512
DEPTH = 2

EPS = 1e-6
GRID_W = 64
D_MIX = D_MODEL
HEAD_DIM = 64
ATT_HEADS = (D_MIX // 2) // HEAD_DIM
ATT_KV_HEADS = 2
ATT_GROUP = ATT_HEADS // ATT_KV_HEADS
ATT_WIDTH = ATT_HEADS * HEAD_DIM
KV_WIDTH = ATT_KV_HEADS * HEAD_DIM
ATT_SCALE = HEAD_DIM ** -0.5
Q_BLOCK = 128
ROPE_THETA = 10000.0
ROPE_AXIS_DIM = HEAD_DIM // 2
HGRN_WIDTH = D_MIX // 4
HGRN_DK = 64
HGRN_DV = 64
HGRN_HEADS = HGRN_WIDTH // HGRN_DV
HGRN_CHUNK = 16
CONV_WIDTH = D_MIX - ATT_WIDTH - HGRN_WIDTH
CONV_KERNEL = 31
CONV_PAD = (CONV_KERNEL - 1) // 2
D_FF = 4 * D_MODEL
IN_COLS = ATT_WIDTH + 2 * KV_WIDTH + 5 * HGRN_WIDTH + 2 * CONV_WIDTH


def _in_split_points():
    sizes = [ATT_WIDTH, KV_WIDTH, KV_WIDTH, HGRN_WIDTH, HGRN_WIDTH, HGRN_WIDTH,
             HGRN_WIDTH, HGRN_WIDTH, CONV_WIDTH, CONV_WIDTH]
    points, acc = [], 0
    for s in sizes[:-1]:
        acc += s
        points.append(acc)
    return points

def rms_norm(x, g):
    xf = x.astype(jnp.float32)
    y = xf * lax.rsqrt(jnp.mean(xf * xf, axis=-1, keepdims=True) + EPS)
    return (y * g.astype(jnp.float32)).astype(x.dtype)

def layer_norm(x, g, b):
    xf = x.astype(jnp.float32)
    mu = jnp.mean(xf, axis=-1, keepdims=True)
    xc = xf - mu
    y = xc * lax.rsqrt(jnp.mean(xc * xc, axis=-1, keepdims=True) + EPS)
    return (y * g.astype(jnp.float32) + b.astype(jnp.float32)).astype(x.dtype)

def _rope_angles(pos):
    inv_freq = ROPE_THETA ** (-jnp.arange(0, ROPE_AXIS_DIM, 2, dtype=jnp.float32) / ROPE_AXIS_DIM)
    ang = pos.astype(jnp.float32)[:, None] * inv_freq[None, :]
    return jnp.cos(ang), jnp.sin(ang)

def _rotate(x, cos, sin):
    half = x.shape[-1] // 2
    x1, x2 = x[..., :half], x[..., half:]
    c, s = cos[None, :, None, :], sin[None, :, None, :]
    return jnp.concatenate([x1 * c - x2 * s, x1 * s + x2 * c], axis=-1)

def apply_axial_rope(x, row_cs, col_cs):
    xf = x.astype(jnp.float32)
    out = jnp.concatenate([_rotate(xf[..., :ROPE_AXIS_DIM], *row_cs),
                           _rotate(xf[..., ROPE_AXIS_DIM:], *col_cs)], axis=-1)
    return out.astype(x.dtype)

def block_attention(q, k, v):
    B, L, H, D = q.shape
    nb = L // Q_BLOCK
    qb = q.reshape(B, nb, Q_BLOCK, ATT_KV_HEADS, ATT_GROUP, D).transpose(1, 0, 2, 3, 4, 5)

    def one_block(q_blk):
        s = jnp.einsum("bqhgd,bkhd->bhgqk", q_blk, k).astype(jnp.float32) * ATT_SCALE
        p = jax.nn.softmax(s, axis=-1)
        return jnp.einsum("bhgqk,bkhd->bqhgd", p.astype(v.dtype), v)

    o = lax.map(one_block, qb)
    return o.transpose(1, 0, 2, 3, 4, 5).reshape(B, L, H * D)

def chunk_gated_recurrence(q, k, v, log_f):
    B, L, H, K = q.shape
    V = v.shape[-1]
    C = HGRN_CHUNK
    N = L // C

    def to_chunks(a):
        return a.reshape(B, N, C, H, a.shape[-1]).transpose(0, 3, 1, 2, 4)

    q, k, v, log_f = (to_chunks(a) for a in (q, k, v, log_f))
    b = jnp.cumsum(log_f, axis=3)
    causal = jnp.tril(jnp.ones((C, C), dtype=bool))[:, :, None]
    diff = b[:, :, :, :, None, :] - b[:, :, :, None, :, :]
    decay = jnp.where(causal, jnp.exp(jnp.where(causal, diff, 0.0)), 0.0)
    scores = jnp.einsum("bhnik,bhnjk,bhnijk->bhnij", q, k, decay)
    o_intra = jnp.einsum("bhnij,bhnjv->bhniv", scores, v)
    b_last = b[:, :, :, -1:, :]
    u = jnp.einsum("bhnjk,bhnjv->bhnkv", k * jnp.exp(b_last - b), v)
    chunk_decay = jnp.exp(b_last[:, :, :, 0, :])

    def step(S, inp):
        dec, uu = inp
        return dec[..., None] * S + uu, S

    S0 = jnp.zeros((B, H, K, V), q.dtype)
    _, S_prev = lax.scan(step, S0, (jnp.moveaxis(chunk_decay, 2, 0), jnp.moveaxis(u, 2, 0)))
    S_prev = jnp.moveaxis(S_prev, 0, 2)
    o_inter = jnp.einsum("bhnik,bhnkv->bhniv", q * jnp.exp(b), S_prev)
    return (o_intra + o_inter).transpose(0, 2, 3, 1, 4).reshape(B, L, H, V)

def _layer_lower_bounds(lb_param):
    p = jax.nn.softmax(lb_param.astype(jnp.float32), axis=0)
    return jnp.cumsum(p, axis=0) - p[0:1]

def _forget_gate(z, lb):
    zf = z.astype(jnp.float32)
    log_f = jax.nn.log_sigmoid(zf) + jnp.log1p(lb * jnp.exp(-zf))
    k = (1.0 - lb) * jax.nn.sigmoid(-zf)
    return log_f, k

def hgrn2_bidirectional(q_h, i_h, f_fw, f_bw, g_h, lb_fw, lb_bw, norm_g):
    B, L, _ = q_h.shape
    heads = lambda a: a.astype(jnp.float32).reshape(B, L, HGRN_HEADS, -1)
    q, v = heads(q_h), heads(i_h)
    lb_fw = lb_fw.reshape(HGRN_HEADS, HGRN_DK)
    lb_bw = lb_bw.reshape(HGRN_HEADS, HGRN_DK)
    logf_fw, k_fw = _forget_gate(heads(f_fw), lb_fw)
    logf_bw, k_bw = _forget_gate(heads(f_bw), lb_bw)
    flip = lambda a: jnp.flip(a, axis=1)
    o_fw = chunk_gated_recurrence(q, k_fw, v, logf_fw)
    o_bw = flip(chunk_gated_recurrence(flip(q), flip(k_bw), flip(v), flip(logf_bw)))
    o = rms_norm(o_fw + o_bw, norm_g.reshape(HGRN_HEADS, HGRN_DV))
    o = o.reshape(B, L, HGRN_WIDTH) * jax.nn.silu(g_h.astype(jnp.float32))
    return o.astype(q_h.dtype)

def conformer_conv(a, gate, w_dw, b_dw, ln_g, ln_b):
    u = a * jax.nn.sigmoid(gate)
    y = lax.conv_general_dilated(u, w_dw[:, None, :], window_strides=(1,),
                                 padding=[(CONV_PAD, CONV_PAD)],
                                 dimension_numbers=("NWC", "WIO", "NWC"),
                                 feature_group_count=CONV_WIDTH)
    y = layer_norm(y + b_dw, ln_g, ln_b)
    return jax.nn.silu(y)

def first_inputs(seed: int = 0) -> dict:
    key = jax.random.key(seed)
    ks = jax.random.split(key, 16)
    n = lambda k, shape: jax.random.normal(k, shape, jnp.float32)
    return {
        "x": n(ks[0], (BATCH, SEQ, D_MODEL)),
        "w_in": n(ks[1], (DEPTH, D_MODEL, IN_COLS)) * D_MODEL ** -0.5,
        "w_out": n(ks[2], (DEPTH, D_MIX, D_MODEL)) * D_MIX ** -0.5,
        "norm_mix": 1.0 + 0.05 * n(ks[3], (DEPTH, D_MODEL)),
        "norm_mlp": 1.0 + 0.05 * n(ks[4], (DEPTH, D_MODEL)),
        "q_norm": 1.0 + 0.05 * n(ks[5], (DEPTH, HEAD_DIM)),
        "k_norm": 1.0 + 0.05 * n(ks[6], (DEPTH, HEAD_DIM)),
        "hgrn_lb_fwd": 0.5 * n(ks[7], (DEPTH, HGRN_WIDTH)),
        "hgrn_lb_bwd": 0.5 * n(ks[8], (DEPTH, HGRN_WIDTH)),
        "hgrn_norm": 1.0 + 0.05 * n(ks[9], (DEPTH, HGRN_WIDTH)),
        "conv_w": n(ks[10], (DEPTH, CONV_KERNEL, CONV_WIDTH)) * CONV_KERNEL ** -0.5,
        "conv_b": 0.02 * n(ks[11], (DEPTH, CONV_WIDTH)),
        "conv_ln_g": 1.0 + 0.05 * n(ks[12], (DEPTH, CONV_WIDTH)),
        "conv_ln_b": 0.02 * n(ks[13], (DEPTH, CONV_WIDTH)),
        "w_mlp_in": n(ks[14], (DEPTH, D_MODEL, D_FF)) * D_MODEL ** -0.5,
        "w_mlp_out": n(ks[15], (DEPTH, D_FF, D_MODEL)) * D_FF ** -0.5,
    }

def first_block(x, w_in, w_out, norm_mix, norm_mlp, q_norm, k_norm, hgrn_lb_fwd, hgrn_lb_bwd,
              hgrn_norm, conv_w, conv_b, conv_ln_g, conv_ln_b, w_mlp_in, w_mlp_out):
    B, L, _ = x.shape
    rows = L // GRID_W
    row_idx = jnp.broadcast_to(jnp.arange(rows)[:, None], (rows, GRID_W)).reshape(L)
    col_idx = jnp.broadcast_to(jnp.arange(GRID_W)[None, :], (rows, GRID_W)).reshape(L)
    row_cs, col_cs = _rope_angles(row_idx), _rope_angles(col_idx)
    lb_fwd = _layer_lower_bounds(hgrn_lb_fwd)
    lb_bwd = _layer_lower_bounds(hgrn_lb_bwd)
    splits = _in_split_points()

    for l in range(DEPTH):
        h = rms_norm(x, norm_mix[l])
        z = h @ w_in[l]
        (q_a, k_a, v_a, q_h, i_h, f_fw, f_bw, g_h, a_c, g_c) = jnp.split(z, splits, axis=-1)

        q_a = rms_norm(q_a.reshape(B, L, ATT_HEADS, HEAD_DIM), q_norm[l])
        k_a = rms_norm(k_a.reshape(B, L, ATT_KV_HEADS, HEAD_DIM), k_norm[l])
        q_a = apply_axial_rope(q_a, row_cs, col_cs)
        k_a = apply_axial_rope(k_a, row_cs, col_cs)
        v_a = v_a.reshape(B, L, ATT_KV_HEADS, HEAD_DIM)
        o_att = block_attention(q_a, k_a, v_a)

        o_hg = hgrn2_bidirectional(q_h, i_h, f_fw, f_bw, g_h,
                                   lb_fwd[l], lb_bwd[l], hgrn_norm[l])

        o_cv = conformer_conv(a_c, g_c, conv_w[l], conv_b[l],
                              conv_ln_g[l], conv_ln_b[l])

        mix = jnp.concatenate([o_att, o_hg.astype(x.dtype), o_cv], axis=-1)
        x = x + mix @ w_out[l]

        h = rms_norm(x, norm_mlp[l])
        x = x + jnp.square(jax.nn.relu(h @ w_mlp_in[l])) @ w_mlp_out[l]
    return x


ROT_DIM = HEAD_DIM // 4
ROPE_THETA_2 = 500000.0
NORM_EPS = 1e-6
NEG_INF = -1e30

NSA_HEADS = 8
NSA_GROUPS = 2
NSA_HPG = NSA_HEADS // NSA_GROUPS
CMP_LEN = 32
CMP_STRIDE = 16
CMP_HIDDEN = 256
SLC_LEN = 64
SLC_TOPN = 8
WINDOW = 256
SB_HEADS = 8
GLA_HEADS = 4
GLA_DK = 64
GLA_DV = 128
GLA_RANK = 16
GLA_TAU = 16.0
GLA_CHUNK = 64
FOX_HEADS = 8

BRANCH_WIDTH = 512
N_BRANCH = 4
D_FF_2 = 4 * D_MODEL

NSA_QW = NSA_HEADS * HEAD_DIM
NSA_KVW = NSA_GROUPS * HEAD_DIM
SB_W = SB_HEADS * HEAD_DIM
FOX_W = FOX_HEADS * HEAD_DIM
SPLITS = (NSA_QW, NSA_KVW, NSA_KVW, NSA_KVW, NSA_KVW, NSA_KVW, NSA_KVW, NSA_HEADS * 3,
          SB_W, SB_W, SB_W,
          GLA_HEADS * GLA_DK, GLA_HEADS * GLA_DK, GLA_HEADS * GLA_DV, GLA_RANK, GLA_HEADS * GLA_DV,
          FOX_W, FOX_W, FOX_W, FOX_HEADS,
          N_BRANCH * D_MODEL)
D_IN = sum(SPLITS)


def rms_norm_2(x, g):
    xf = x.astype(jnp.float32)
    xf = xf * lax.rsqrt(jnp.mean(xf * xf, axis=-1, keepdims=True) + NORM_EPS)
    return (xf * g.astype(jnp.float32)).astype(x.dtype)

def masked_softmax(logits, mask):
    logits = jnp.where(mask, logits.astype(jnp.float32), NEG_INF)
    return jax.nn.softmax(logits, axis=-1) * mask

def rope_partial(x, pos):
    half = ROT_DIM // 2
    inv = ROPE_THETA_2 ** (-jnp.arange(0, ROT_DIM, 2, dtype=jnp.float32) / ROT_DIM)
    ang = pos.astype(jnp.float32)[..., None] * inv
    ang = ang.reshape(ang.shape[:2] + (1,) * (x.ndim - 3) + (half,))
    cos = jnp.cos(ang).astype(x.dtype)
    sin = jnp.sin(ang).astype(x.dtype)
    x1, x2, xp = x[..., :half], x[..., half:ROT_DIM], x[..., ROT_DIM:]
    return jnp.concatenate([x1 * cos - x2 * sin, x2 * cos + x1 * sin, xp], axis=-1)

def nsa_mixer(q, k_cmp, v_cmp, k_slc, v_slc, k_win, v_win, gate_logits, pos,
              cmp_pos_k, cmp_pos_v, cmp_wk1, cmp_wk2, cmp_wv1, cmp_wv2):
    B, S = q.shape[:2]
    G, HPG, D = NSA_GROUPS, NSA_HPG, HEAD_DIM
    scale = D ** -0.5
    q = rope_partial(q.reshape(B, S, G, HPG, D), pos)
    k_cmp, v_cmp, k_slc, v_slc, k_win, v_win = [t.reshape(B, S, G, D) for t in (k_cmp, v_cmp, k_slc, v_slc, k_win, v_win)]
    k_slc = rope_partial(k_slc, pos)
    k_win = rope_partial(k_win, pos)
    tok = np.arange(S)

    n_cmp = (S - CMP_LEN) // CMP_STRIDE + 1
    cmp_start = np.arange(n_cmp) * CMP_STRIDE
    cmp_end = cmp_start + CMP_LEN - 1
    cmp_idx = cmp_start[:, None] + np.arange(CMP_LEN)[None, :]

    def compress(t, pe, w1, w2):
        blk = t[:, cmp_idx] + pe[:, None, :]
        blk = jnp.moveaxis(blk, 3, 2).reshape(B, n_cmp, G, CMP_LEN * D)
        return jax.nn.gelu(blk @ w1) @ w2

    kc = rope_partial(compress(k_cmp, cmp_pos_k, cmp_wk1, cmp_wk2), pos[:, cmp_end])
    vc = compress(v_cmp, cmp_pos_v, cmp_wv1, cmp_wv2)
    s_cmp = jnp.einsum('bsghd,bcgd->bghsc', q, kc) * scale
    p_cmp = masked_softmax(s_cmp, cmp_end[None, :] <= tok[:, None])
    o_cmp = jnp.einsum('bghsc,bcgd->bsghd', p_cmp.astype(vc.dtype), vc)

    n_sel = S // SLC_LEN
    top_n = min(SLC_TOPN, n_sel)
    sel_start = np.arange(n_sel) * SLC_LEN
    overlap = np.clip(np.minimum(cmp_start[:, None] + CMP_LEN, sel_start[None, :] + SLC_LEN)
                      - np.maximum(cmp_start[:, None], sel_start[None, :]), 0, None) / CMP_LEN
    imp = jnp.einsum('bghsc,cj->bgsj', p_cmp, jnp.asarray(overlap, jnp.float32))
    forced = (sel_start[None, :] == 0) | (np.arange(n_sel)[None, :] == (tok // SLC_LEN)[:, None])
    imp = jnp.where(forced, jnp.inf, jnp.where(sel_start[None, :] <= tok[:, None], imp, -jnp.inf))
    _, sel = lax.top_k(imp, top_n)
    n_qb = S // Q_BLOCK

    def to_blocks(t):
        return jnp.moveaxis(t.reshape(B, n_sel, SLC_LEN, G, D), 3, 1).reshape(B, G, n_sel, SLC_LEN * D)

    ks_blk = to_blocks(k_slc)
    vs_blk = to_blocks(v_slc)
    q_blk = jnp.moveaxis(q.reshape(B, n_qb, Q_BLOCK, G, HPG, D), 1, 0)
    sel_blk = jnp.moveaxis(sel.reshape(B, G, n_qb, Q_BLOCK, top_n), 2, 0)

    def select_block(args):
        qc, ic, t_start = args
        flat = ic.reshape(B, G, Q_BLOCK * top_n, 1)
        kg = jnp.take_along_axis(ks_blk, flat, axis=2).reshape(B, G, Q_BLOCK, top_n * SLC_LEN, D)
        vg = jnp.take_along_axis(vs_blk, flat, axis=2).reshape(B, G, Q_BLOCK, top_n * SLC_LEN, D)
        key_tok = (ic[..., None] * SLC_LEN + jnp.arange(SLC_LEN)).reshape(B, G, Q_BLOCK, top_n * SLC_LEN)
        t = t_start + jnp.arange(Q_BLOCK)
        s = jnp.einsum('bqghd,bgqkd->bghqk', qc, kg) * scale
        p = masked_softmax(s, (key_tok <= t[:, None])[:, :, None])
        return jnp.einsum('bghqk,bgqkd->bqghd', p.astype(vg.dtype), vg)

    o_slc = lax.map(select_block, (q_blk, sel_blk, jnp.arange(n_qb) * Q_BLOCK))
    o_slc = jnp.moveaxis(o_slc, 0, 1).reshape(B, S, G, HPG, D)

    n_band = Q_BLOCK + WINDOW
    band_idx = np.arange(n_qb)[:, None] * Q_BLOCK + np.arange(n_band)[None, :]
    band_tok = band_idx - WINDOW
    pad = ((0, 0), (WINDOW, 0), (0, 0), (0, 0))
    kb = jnp.pad(k_win, pad)[:, band_idx]
    vb = jnp.pad(v_win, pad)[:, band_idx]
    tq = tok.reshape(n_qb, Q_BLOCK)
    win_mask = ((band_tok[:, None, :] <= tq[:, :, None]) & (band_tok[:, None, :] > tq[:, :, None] - WINDOW)
                & (band_tok[:, None, :] >= 0))
    s_win = jnp.einsum('bnqghd,bnkgd->bnghqk', q.reshape(B, n_qb, Q_BLOCK, G, HPG, D), kb) * scale
    p_win = masked_softmax(s_win, win_mask[None, :, None, None])
    o_win = jnp.einsum('bnghqk,bnkgd->bnqghd', p_win.astype(vb.dtype), vb).reshape(B, S, G, HPG, D)

    g = jax.nn.sigmoid(gate_logits.astype(jnp.float32)).reshape(B, S, G, HPG, 3).astype(q.dtype)
    o = g[..., 0:1] * o_cmp + g[..., 1:2] * o_slc + g[..., 2:3] * o_win
    return o.reshape(B, S, NSA_HEADS * D)

def stick_breaking_mixer(q, k, v):
    B, S = q.shape[:2]
    H, D = SB_HEADS, HEAD_DIM
    scale = D ** -0.5
    n_qb = S // Q_BLOCK
    kT = jnp.moveaxis(k.reshape(B, S, H, D), 1, 2)
    vT = jnp.moveaxis(v.reshape(B, S, H, D), 1, 2)
    qb = q.reshape(B, n_qb, Q_BLOCK, H, D).transpose(1, 0, 3, 2, 4)
    key_pos = jnp.arange(S)

    def block(args):
        qc, t_start = args
        z = jnp.einsum('bhqd,bhkd->bhqk', qc, kT).astype(jnp.float32) * scale
        t = t_start + jnp.arange(Q_BLOCK)
        valid = key_pos[None, :] < t[:, None]
        sp = jnp.where(valid, jax.nn.softplus(z), 0.0)
        later = lax.cumsum(sp, axis=3, reverse=True) - sp
        a = jnp.where(valid, jnp.exp(jax.nn.log_sigmoid(z) - later), 0.0)
        return jnp.einsum('bhqk,bhkd->bhqd', a.astype(vT.dtype), vT)

    o = lax.map(block, (qb, jnp.arange(n_qb) * Q_BLOCK))
    return o.transpose(1, 0, 3, 2, 4).reshape(B, S, H * D)

def gla_mixer(q, k, v, a_lr, gate, w_alpha, b_alpha, norm_g):
    B, S = q.shape[:2]
    H, DK, DV, C = GLA_HEADS, GLA_DK, GLA_DV, GLA_CHUNK
    n_ch = S // C
    log_a = jax.nn.log_sigmoid((a_lr @ w_alpha + b_alpha).astype(jnp.float32)) / GLA_TAU

    def chunks(t, f):
        return t.reshape(B, n_ch, C, H, f).transpose(1, 0, 3, 2, 4)

    qc_all = chunks(q * DK ** -0.5, DK)
    kc_all = chunks(k, DK)
    vc_all = chunks(v, DV)
    la_all = chunks(log_a, DK)
    causal = np.tril(np.ones((C, C), dtype=bool))

    def step(state, inp):
        qc, kc, vc, lac = inp
        b = jnp.cumsum(lac, axis=2)
        o_inter = jnp.einsum('bhtk,bhkv->bhtv', qc * jnp.exp(b), state)
        diff = jnp.where(causal[:, :, None], b[:, :, :, None, :] - b[:, :, None, :, :], -jnp.inf)
        att = jnp.einsum('bhtk,bhsk,bhtsk->bhts', qc, kc, jnp.exp(diff))
        o_intra = jnp.einsum('bhts,bhsv->bhtv', att, vc)
        b_last = b[:, :, -1:, :]
        state = (jnp.exp(b_last[:, :, 0])[..., None] * state
                 + jnp.einsum('bhsk,bhsv->bhkv', kc * jnp.exp(b_last - b), vc))
        return state, o_inter + o_intra

    state0 = jnp.zeros((B, H, DK, DV), jnp.float32)
    _, o = lax.scan(step, state0, (qc_all, kc_all, vc_all, la_all))
    o = o.transpose(1, 0, 3, 2, 4).reshape(B, S, H, DV)
    o = o * lax.rsqrt(jnp.mean(o * o, axis=-1, keepdims=True) + NORM_EPS) * norm_g.astype(jnp.float32)
    y = o.astype(v.dtype) * jax.nn.silu(gate).reshape(B, S, H, DV)
    return y.reshape(B, S, H * DV)

def forgetting_mixer(q, k, v, f_logit, b_f):
    B, S = q.shape[:2]
    H, D = FOX_HEADS, HEAD_DIM
    scale = D ** -0.5
    n_qb = S // Q_BLOCK
    log_f = jax.nn.log_sigmoid(f_logit.astype(jnp.float32) + b_f.astype(jnp.float32))
    cumT = jnp.moveaxis(jnp.cumsum(log_f, axis=1), 1, 2)
    kT = jnp.moveaxis(k.reshape(B, S, H, D), 1, 2)
    vT = jnp.moveaxis(v.reshape(B, S, H, D), 1, 2)
    qb = q.reshape(B, n_qb, Q_BLOCK, H, D).transpose(1, 0, 3, 2, 4)
    cb = cumT.reshape(B, H, n_qb, Q_BLOCK).transpose(2, 0, 1, 3)
    key_pos = jnp.arange(S)

    def block(args):
        qc, ct, t_start = args
        s = jnp.einsum('bhqd,bhkd->bhqk', qc, kT).astype(jnp.float32) * scale
        s = s + ct[..., None] - cumT[:, :, None, :]
        t = t_start + jnp.arange(Q_BLOCK)
        p = masked_softmax(s, key_pos[None, :] <= t[:, None])
        return jnp.einsum('bhqk,bhkd->bhqd', p.astype(vT.dtype), vT)

    o = lax.map(block, (qb, cb, jnp.arange(n_qb) * Q_BLOCK))
    return o.transpose(1, 0, 3, 2, 4).reshape(B, S, H * D)

def hybrid_layer(x, positions, norm_mix, w_in, b_gate, cmp_pos_k, cmp_pos_v, cmp_wk1, cmp_wk2,
                 cmp_wv1, cmp_wv2, gla_w_alpha, gla_b_alpha, gla_norm, fox_b_f, w_branch, w_out,
                 norm_ff, w_ff1, w_ff2):
    B, S, _ = x.shape
    h = rms_norm_2(x, norm_mix)
    proj = h @ w_in
    offsets = np.cumsum(SPLITS)[:-1].tolist()
    (nsa_q, nsa_kc, nsa_vc, nsa_ks, nsa_vs, nsa_kw, nsa_vw, nsa_g,
     sb_q, sb_k, sb_v,
     gla_q, gla_k, gla_v, gla_a, gla_g,
     fox_q, fox_k, fox_v, fox_f,
     gate_logits) = jnp.split(proj, offsets, axis=-1)

    y_nsa = nsa_mixer(nsa_q, nsa_kc, nsa_vc, nsa_ks, nsa_vs, nsa_kw, nsa_vw, nsa_g, positions,
                      cmp_pos_k, cmp_pos_v, cmp_wk1, cmp_wk2, cmp_wv1, cmp_wv2)
    y_sb = stick_breaking_mixer(sb_q, sb_k, sb_v)
    y_gla = gla_mixer(gla_q.reshape(B, S, GLA_HEADS, GLA_DK), gla_k.reshape(B, S, GLA_HEADS, GLA_DK),
                      gla_v.reshape(B, S, GLA_HEADS, GLA_DV), gla_a, gla_g, gla_w_alpha, gla_b_alpha, gla_norm)
    y_fox = forgetting_mixer(fox_q, fox_k, fox_v, fox_f, fox_b_f)

    ys = jnp.stack([y_nsa, y_sb, y_gla, y_fox], axis=2)
    branch = jnp.einsum('bsnc,ncd->bsnd', ys, w_branch)
    gates = jax.nn.sigmoid((gate_logits + b_gate).astype(jnp.float32)).astype(x.dtype)
    mixed = jnp.sum(gates.reshape(B, S, N_BRANCH, D_MODEL) * branch, axis=2)
    x = x + mixed @ w_out
    h2 = rms_norm_2(x, norm_ff)
    return x + jnp.square(jax.nn.relu(h2 @ w_ff1)) @ w_ff2

def second_inputs(seed: int = 0) -> dict:
    key = jax.random.key(seed)
    ks = jax.random.split(key, 21)
    L = DEPTH

    def nrm(k, shape, scale):
        return jax.random.normal(k, shape, jnp.float32) * scale

    x = nrm(ks[0], (BATCH, SEQ, D_MODEL), 1.0)
    offset = jax.random.randint(ks[1], (BATCH, 1), 0, 4096, dtype=jnp.int32)
    positions = jnp.arange(SEQ, dtype=jnp.int32)[None, :] + offset
    return {
        'x': x,
        'positions': positions,
        'norm_mix': 1.0 + nrm(ks[2], (L, D_MODEL), 0.02),
        'w_in': nrm(ks[3], (L, D_MODEL, D_IN), D_MODEL ** -0.5),
        'b_gate': nrm(ks[4], (L, N_BRANCH * D_MODEL), 0.02),
        'nsa_cmp_pos_k': nrm(ks[5], (L, CMP_LEN, HEAD_DIM), 0.1),
        'nsa_cmp_pos_v': nrm(ks[6], (L, CMP_LEN, HEAD_DIM), 0.1),
        'nsa_cmp_wk1': nrm(ks[7], (L, CMP_LEN * HEAD_DIM, CMP_HIDDEN), (CMP_LEN * HEAD_DIM) ** -0.5),
        'nsa_cmp_wk2': nrm(ks[8], (L, CMP_HIDDEN, HEAD_DIM), CMP_HIDDEN ** -0.5),
        'nsa_cmp_wv1': nrm(ks[9], (L, CMP_LEN * HEAD_DIM, CMP_HIDDEN), (CMP_LEN * HEAD_DIM) ** -0.5),
        'nsa_cmp_wv2': nrm(ks[10], (L, CMP_HIDDEN, HEAD_DIM), CMP_HIDDEN ** -0.5),
        'gla_w_alpha': nrm(ks[11], (L, GLA_RANK, GLA_HEADS * GLA_DK), GLA_RANK ** -0.5),
        'gla_b_alpha': nrm(ks[12], (L, GLA_HEADS * GLA_DK), 0.1),
        'gla_norm': 1.0 + nrm(ks[13], (L, GLA_DV), 0.02),
        'fox_b_f': 2.0 + nrm(ks[14], (L, FOX_HEADS), 0.1),
        'w_branch': nrm(ks[15], (L, N_BRANCH, BRANCH_WIDTH, D_MODEL), BRANCH_WIDTH ** -0.5),
        'w_out': nrm(ks[16], (L, D_MODEL, D_MODEL), D_MODEL ** -0.5),
        'norm_ff': 1.0 + nrm(ks[17], (L, D_MODEL), 0.02),
        'w_ff1': nrm(ks[18], (L, D_MODEL, D_FF_2), D_MODEL ** -0.5),
        'w_ff2': nrm(ks[19], (L, D_FF_2, D_MODEL), D_FF_2 ** -0.5),
        'norm_final': 1.0 + nrm(ks[20], (D_MODEL,), 0.02),
    }

def second_block(x, positions, norm_mix, w_in, b_gate, nsa_cmp_pos_k, nsa_cmp_pos_v, nsa_cmp_wk1,
              nsa_cmp_wk2, nsa_cmp_wv1, nsa_cmp_wv2, gla_w_alpha, gla_b_alpha, gla_norm, fox_b_f,
              w_branch, w_out, norm_ff, w_ff1, w_ff2, norm_final):
    for l in range(DEPTH):
        x = hybrid_layer(x, positions, norm_mix[l], w_in[l], b_gate[l], nsa_cmp_pos_k[l], nsa_cmp_pos_v[l],
                         nsa_cmp_wk1[l], nsa_cmp_wk2[l], nsa_cmp_wv1[l], nsa_cmp_wv2[l], gla_w_alpha[l],
                         gla_b_alpha[l], gla_norm[l], fox_b_f[l], w_branch[l], w_out[l], norm_ff[l],
                         w_ff1[l], w_ff2[l])
    return rms_norm_2(x, norm_final)


def setup_inputs(seed=0):
    out = dict(first_inputs(seed))
    for name, value in second_inputs(seed + 1).items():
        if name != "x":
            out[name + "_2"] = value
    return out


def reference(
    x, w_in, w_out, norm_mix, norm_mlp, q_norm, k_norm, hgrn_lb_fwd, hgrn_lb_bwd, hgrn_norm,
    conv_w, conv_b, conv_ln_g, conv_ln_b, w_mlp_in, w_mlp_out, positions_2, norm_mix_2, w_in_2,
    b_gate_2, nsa_cmp_pos_k_2, nsa_cmp_pos_v_2, nsa_cmp_wk1_2, nsa_cmp_wk2_2, nsa_cmp_wv1_2,
    nsa_cmp_wv2_2, gla_w_alpha_2, gla_b_alpha_2, gla_norm_2, fox_b_f_2, w_branch_2, w_out_2,
    norm_ff_2, w_ff1_2, w_ff2_2, norm_final_2,
):
    x = first_block(
        x, w_in, w_out, norm_mix, norm_mlp, q_norm, k_norm, hgrn_lb_fwd, hgrn_lb_bwd, hgrn_norm,
        conv_w, conv_b, conv_ln_g, conv_ln_b, w_mlp_in, w_mlp_out,
    )
    return second_block(
        x, positions_2, norm_mix_2, w_in_2, b_gate_2, nsa_cmp_pos_k_2, nsa_cmp_pos_v_2,
        nsa_cmp_wk1_2, nsa_cmp_wk2_2, nsa_cmp_wv1_2, nsa_cmp_wv2_2, gla_w_alpha_2,
        gla_b_alpha_2, gla_norm_2, fox_b_f_2, w_branch_2, w_out_2, norm_ff_2, w_ff1_2, w_ff2_2,
        norm_final_2,
    )


_drawn_inputs = setup_inputs


def setup_inputs(seed=0):
    import zlib

    import numpy as np

    out = dict(_drawn_inputs(seed))
    spreads = {}
    factors = {'q_norm': 8.0,
     'k_norm': 8.0,
     'conv_b': 3.014,
     'conv_ln_b': 5.975,
     'norm_mix_2': 4.705,
     'b_gate_2': 8.0,
     'nsa_cmp_pos_k_2': 8.0,
     'nsa_cmp_pos_v_2': 17.612,
     'nsa_cmp_wk1_2': 3.882,
     'nsa_cmp_wk2_2': 3.671,
     'gla_b_alpha_2': 4.363,
     'gla_norm_2': 8.0,
     'fox_b_f_2': 46.613,
     'norm_ff_2': 3.64,
     'norm_final_2': 7.995}
    for name, (base, spread) in spreads.items():
        noise = np.random.default_rng([zlib.crc32(name.encode()), seed]).standard_normal(out[name].shape)
        drawn = base * np.exp(spread * noise) if base else spread * noise
        out[name] = jnp.asarray(drawn.astype(out[name].dtype))
    for name, factor in factors.items():
        out[name] = (out[name] * factor).astype(out[name].dtype)
    return out
```

```python
from contextlib import ExitStack

import numpy as np

import concourse.bass as bass
from concourse import mybir

F32 = mybir.dt.float32
F32R = mybir.dt.float32r
BF16 = mybir.dt.bfloat16
I32 = mybir.dt.int32
U8 = mybir.dt.uint8
ALU = mybir.AluOpType
ACT = mybir.ActivationFunctionType
AX_X = mybir.AxisListType.X

P = 128
T = 512
NT = T // P
D = 1024
NK = D // P
DEPTH = 2
HD = 64
EPS = 1e-6
UNIT = 2048
FF = 4 * D
FB = FF // D
SCALE = float(HD) ** -0.5
NEG = -1e30

CONSTS = ["ident", "ones", "pair_ones", "rot1", "rot2", "neg_tri", "neg_ones",
          "causal_neg", "window_neg", "later_neg", "later_one"]
LEVELS = [64, 32, 16, 8, 4, 2, 1]
V1 = {}
_at = 0
for _name, _n in (("norm_mix", 8), ("norm_mlp", 8), ("q_norm", 1), ("k_norm", 1), ("lb_f0", 2), ("lb_f1", 2),
                  ("lb_b0", 2), ("lb_b1", 2), ("hgrn_norm", 2), ("conv_b", 2), ("ln_g", 2), ("ln_b", 2),
                  ("conv_w", 62)):
    V1[_name] = _at
    _at += _n
NV1 = _at
V2 = {}
_at = 0
for _name, _n in (("norm_mix", 8), ("norm_ff", 8), ("b_gate", 32), ("pe_k", 16), ("pe_v", 16), ("b_alpha", 2),
                  ("gla_norm", 1), ("fox_b", 1), ("final", 8)):
    V2[_name] = _at
    _at += _n
NV2 = _at


def plan_units(groups):
    units, first_unit, first_tile, n = [], {}, {}, 0
    for group, operand, shapes in groups:
        first_unit[group], first_tile[group] = len(units), n
        for nk, ntile in shapes:
            units.append((group, nk, ntile, operand, n))
            n += ntile
    return units, first_unit, first_tile


FF_GROUPS = [g for b in range(FB) for g in ((f"up{b}", "h", [(8, 2)] * 4), (f"down{b}", "mid", [(8, 2)] * 4))]
GROUPS1 = [("in", "h", [(8, 2)] * 10), ("out", "h", [(8, 2)] * 4)] + FF_GROUPS
BRANCH = [(8, 2), (8, 2), (4, 4)] * 2
GROUPS2 = [("nsa", "h", [(8, 2)] * 5 + [(8, 1)]), ("mix0", "h", BRANCH), ("sb", "h", [(8, 2)] * 6), ("mix1", "h", BRANCH),
           ("gla", "h", [(8, 2)] * 6), ("mix2", "h", BRANCH), ("fox", "h", [(8, 2)] * 6), ("mix3", "h", BRANCH),
           ("out", "h", [(8, 2)] * 4)] + FF_GROUPS
STAGES1 = ["norm0", "in", "prep", "att", "hgrn", "conv", "out", "norm1"] + [g[0] for g in FF_GROUPS]
STAGES2 = ["norm0", "nsa", "prep", "cmp", "att", "mix0", "sb", "stick", "mix1", "gla", "recur", "mix2", "fox", "forget",
           "mix3", "out", "norm1"] + [g[0] for g in FF_GROUPS]


def ranges(kind, qt):
    return {"full": (0, NT), "causal": (0, qt + 1), "window": (max(0, qt - 2), qt + 1), "cmp": (0, 1),
            "fox": (0, qt + 1)}[kind]


def program(nc, given, out, probes=None, blocks=(1, 2), layers=DEPTH):
    x_in, consts_in, masks_in, rope_in, cmpmask_in, sel_in, freq_in = (
        given[n] for n in ("x", "consts", "masks", "rope", "cmpmask", "sel", "freq"))
    vec1_in, vec2_in, w1_in, w2_in, pos_in, cmpw_in, cmpw2_in, alpha_in = (
        given[n] for n in ("vec1", "vec2", "stream1", "stream2", "positions", "cmpw", "cmpw2", "alpha"))
    ctx = ExitStack()
    with ctx:
        def sb(name, shape, dt=F32, scope=ctx):
            return scope.enter_context(nc.sbuf_tensor(name, shape, dt))

        sems = []

        def sem(name):
            s = ctx.enter_context(nc.semaphore(name))
            sems.append(s)
            return s

        xT = sb("xT", [P, NK, T])
        hH = sb("hH", [P, NK, T], F32R)
        hL = sb("hL", [P, NK, T], F32R)
        w_raw = sb("w_raw", [P, 2, UNIT])
        w_hi = sb("w_hi", [P, 2, UNIT], F32R)
        w_lo = sb("w_lo", [P, 2, UNIT], F32R)
        C = sb("C", [P, len(CONSTS), P])
        ident, ones, pair_ones, rot1, rot2, neg_tri, neg_ones = (C[:, i, :] for i in range(7))
        later_one = C[:, 10, :]
        Cb = sb("Cb", [P, 4, P], BF16)
        identb, causal_neg, window_neg, later_neg = (Cb[:, i, :] for i in range(4))
        masks = sb("masks", [P, 2 * len(LEVELS) + 1, P], U8)
        cosT = sb("cosT", [P, T])
        sinT = sb("sinT", [P, T])
        vec = sb("vec", [P, max(NV1, NV2)])
        acc = [ctx.enter_context(nc.psum_tensor(f"acc{i}", [P, T], F32)) for i in range(2)]
        B = [ctx.enter_context(nc.psum_tensor(f"bank{i}", [P, T], F32)) for i in range(6)]

        pe_finished, act_finished, dve_finished = sem("pe_finished"), sem("act_finished"), sem("dve_finished")
        dve_chain, act_chain = sem("dve_chain"), sem("act_chain")
        consts_loaded, vec_loaded, x_loaded, stored = sem("consts_loaded"), sem("vec_loaded"), sem("x_loaded"), sem("stored")
        w_loaded = [sem(f"w_loaded{i}") for i in range(2)]
        hi_split, lo_split = sem("hi_split"), sem("lo_split")
        acc_ready = [sem(f"acc_ready{i}") for i in range(2)]
        acc_free = [sem(f"acc_free{i}") for i in range(2)]
        relu_used = sem("relu_used")
        sq_ready, sq_summed, rstd_ready = sem("sq_ready"), sem("sq_summed"), sem("rstd_ready")
        attention_sems = [[sem(f"{n}_{i}") for n in ("s_ready", "max_ready", "exp_done", "p_normed", "pt_turned", "pt_ready",
                                                     "pv_done", "o_free", "bias_turned", "bias_ready")] for i in range(2)]
        v_turned, v_ready = sem("v_turned"), sem("v_ready")
        softplus_ready, rate_ready, key_ready, decay_summed = (sem("softplus_ready"), sem("rate_ready"), sem("key_ready"),
                                                               sem("decay_summed"))
        gap_ready, decay_ready, terms_ready, level_scored, level_kept = (
            sem("gap_ready"), sem("decay_ready"), sem("terms_ready"), sem("level_scored"), sem("level_kept"))
        o_ready, o_taken, o_squared, o_summed, o_rstd, gate_ready = (
            sem("o_ready"), sem("o_taken"), sem("o_squared"), sem("o_summed"), sem("o_rstd"), sem("gate_ready"))
        z_squared, z_summed, z_rstd, z_normed, z_rotated, z_done = (
            sem("z_squared"), sem("z_summed"), sem("z_rstd"), sem("z_normed"), sem("z_rotated"), sem("z_done"))
        conv_ready, conv_summed, conv_mean, conv_squared, conv_var, conv_rstd, conv_gate, conv_pre = (
            sem("conv_ready"), sem("conv_summed"), sem("conv_mean"), sem("conv_squared"), sem("conv_var"),
            sem("conv_rstd"), sem("conv_gate"), sem("conv_pre"))

        counts = {}

        def link(eng, ins):
            s = dve_chain if eng is nc.vector else act_chain
            key = "dve" if eng is nc.vector else "act"
            counts[key] += 1
            ins.then_inc(s, 1)
            eng.wait_ge(s, counts[key])

        def new_layer():
            counts.update(dve=0, act=0)

        def clear():
            nc.all_engine_barrier()
            nums = sorted(s.num for s in sems)
            assert nums == list(range(nums[0], nums[0] + len(nums)))
            nc.sync.sem_clear(range(nums[0], nums[-1] + 1))
            nc.all_engine_barrier()

        pe, act, dve, pool, sp = nc.tensor, nc.scalar, nc.vector, nc.gpsimd, nc.sync

        def split_hi(units, u):
            if u >= len(units):
                return
            _, nk, ntile, _, _ = units[u]
            w = nk * ntile * P
            act.wait_ge(w_loaded[u % 2], 16 * (u // 2 + 1))
            if u >= 2:
                n = units[u - 2][4] + units[u - 2][2] - 1
                act.wait_ge(acc_ready[n % 2], n // 2 + 1)
            act.activation(w_hi[:, u % 2, 0:w], w_raw[:, u % 2, 0:w], ACT.Copy).then_inc(hi_split, 1)

        def load_weights(units, source, L):
            for u, (_, nk, ntile, _, _) in enumerate(units):
                w = nk * ntile * P
                if u >= 2:
                    sp.wait_ge(lo_split, u - 1)
                sp.dma_start(w_raw[:, u % 2, 0:w], source[bass.ds(L, 1), u, :, 0:w].rearrange("a p n -> (a p) n"))\
                    .then_inc(w_loaded[u % 2], 16)

        def split_lo(units):
            for u, (_, nk, ntile, _, _) in enumerate(units):
                w = nk * ntile * P
                pool.wait_ge(hi_split, u + 1)
                pool.tensor_tensor(w_lo[:, u % 2, 0:w], w_raw[:, u % 2, 0:w], w_hi[:, u % 2, 0:w], ALU.subtract)\
                    .then_inc(lo_split, 1)

        def products(units, group, operands):
            for u, (g, nk, ntile, _, n0) in enumerate(units):
                if g != group:
                    continue
                H, Lo = operands(nk)
                pe.wait_ge(lo_split, u + 1)
                for t in range(ntile):
                    n = n0 + t
                    if n >= 2:
                        pe.wait_ge(acc_free[n % 2], n // 2)
                    for k in range(nk):
                        c = k * ntile * P + t * P
                        wh, wl = w_hi[:, u % 2, c:c + P], w_lo[:, u % 2, c:c + P]
                        pe.matmul(acc[n % 2][:, :], wh, H[:, k, :], start=(k == 0), stop=False)
                        pe.matmul(acc[n % 2][:, :], wl, H[:, k, :], start=False, stop=False)
                        last = pe.matmul(acc[n % 2][:, :], wh, Lo[:, k, :], start=False, stop=(k == nk - 1))
                    last.then_inc(acc_ready[n % 2], 1)

        def group_units(units, group):
            return [(u, x) for u, x in enumerate(units) if x[0] == group]

        def act_group(units, group, evacuate=None):
            for u, (_, nk, ntile, _, n0) in group_units(units, group):
                for t in range(ntile):
                    if evacuate:
                        n = n0 + t
                        act.wait_ge(acc_ready[n % 2], n // 2 + 1)
                        evacuate(n, n - units_first(units, group), acc[n % 2])
                split_hi(units, u + 2)

        def units_first(units, group):
            return next(x[4] for x in units if x[0] == group)

        def dve_group(units, group, evacuate):
            for u, (_, nk, ntile, _, n0) in group_units(units, group):
                for t in range(ntile):
                    n = n0 + t
                    dve.wait_ge(acc_ready[n % 2], n // 2 + 1)
                    evacuate(n, n - units_first(units, group), acc[n % 2])

        def add_to_x(n, t, a):
            dve.tensor_tensor(xT[:, t % NK, :], a[:, :], xT[:, t % NK, :], ALU.add).then_inc(acc_free[n % 2], 1)

        def norm_act(r, sq, tmp):
            for k in range(NK):
                i = NK * r + k
                if k >= 2:
                    act.wait_ge(sq_summed, i - 1)
                act.activation(sq[:, k % 2, :], xT[:, k, :], ACT.Square).then_inc(sq_ready, 1)
            act.wait_ge(sq_summed, NK * r + NK)
            link(act, act.activation(tmp[:, :], B[0][:, :], ACT.Ln, bias=EPS, scale=1.0 / D))
            act.activation(tmp[:, :], tmp[:, :], ACT.Exp, scale=-0.5).then_inc(rstd_ready, 1)

        def norm_pe(r, sq):
            for k in range(NK):
                i = NK * r + k
                pe.wait_ge(sq_ready, i + 1)
                pe.matmul(B[0][:, :], ones, sq[:, k % 2, :], start=(k == 0), stop=(k == NK - 1)).then_inc(sq_summed, 1)

        def norm_dve(r, gcol, tmp, y):
            dve.wait_ge(rstd_ready, r + 1)
            for k in range(NK):
                link(dve, dve.scalar_tensor_tensor(y[:, k % 2, :], xT[:, k, :], vec[:, gcol + k:gcol + k + 1], tmp[:, :],
                                                   ALU.mult, ALU.mult))
                split_dve(hH[:, k, :], hL[:, k, :], y[:, k % 2, :])

        def split_dve(hi, lo, src):
            link(dve, dve.tensor_copy(hi, src))
            link(dve, dve.tensor_tensor(lo, src, hi, ALU.subtract))

        def mlp(units, stage, engine, midH, midL, r_sb):
            for b in range(FB):
                up, down = f"up{b}", f"down{b}"
                if engine == "pe":
                    after(pe, stage, "norm1" if b == 0 else f"down{b - 1}", dve_finished)
                    products(units, up, lambda nk: (hH, hL))
                    finish(pe, up)
                    after(pe, stage, up, dve_finished)
                    products(units, down, lambda nk: (midH, midL))
                    finish(pe, down)
                if engine == "act":
                    if b:
                        after(act, stage, f"up{b - 1}", dve_finished)

                    def relu(n, t, a):
                        i = NK * b + t
                        if i >= 2:
                            act.wait_ge(relu_used, i - 1)
                        act.activation(r_sb[:, i % 2, :], a[:, :], ACT.Relu).then_inc(acc_free[n % 2], 1)
                    act_group(units, up, relu)
                    finish(act, up)
                    act_group(units, down)
                    finish(act, down)
                if engine == "dve":
                    if b:
                        after(dve, stage, f"down{b - 1}", pe_finished)
                    for t in range(NK):
                        i = NK * b + t
                        n = units_first(units, up) + t
                        dve.wait_ge(acc_free[n % 2], n // 2 + 1)
                        link(dve, dve.tensor_tensor(r_sb[:, i % 2, :], r_sb[:, i % 2, :], r_sb[:, i % 2, :], ALU.mult))
                        link(dve, dve.tensor_copy(midH[:, t, :], r_sb[:, i % 2, :]))
                        dve.tensor_tensor(midL[:, t, :], r_sb[:, i % 2, :], midH[:, t, :], ALU.subtract)\
                            .then_inc(relu_used, 1)
                    finish(dve, up)
                    dve_group(units, down, add_to_x)
                    finish(dve, down)

        def finish(eng, name):
            s = {id(pe): pe_finished, id(act): act_finished, id(dve): dve_finished}[id(eng)]
            eng.drain().then_inc(s, 1)

        def after(eng, stages, name, *who):
            for s in who:
                eng.wait_ge(s, stages.index(name) + 1)

        class Attention:

            def __init__(self, sems_of, passes, P_sb, PT_sb, S_sb, stat, y, extra, gate, out_tile):
                (self.s_ready, self.max_ready, self.exp_done, self.p_normed, self.pt_turned, self.pt_ready, self.pv_done,
                 self.o_free, self.bias_turned, self.bias_ready) = sems_of
                self.passes, self.P, self.PT, self.S, self.stat, self.y = passes, P_sb, PT_sb, S_sb, stat, y
                self.extra, self.gate, self.out_tile = extra, gate, out_tile
                self.base = []
                n = 0
                for p in passes:
                    self.base.append(n)
                    n += self.key_tiles(p)
                self.base.append(n)

            @staticmethod
            def key_tiles(p):
                return 1 if p["kind"] == "cmp" else NT

            @staticmethod
            def width(p, qt):
                lo, hi = ranges(p["kind"], qt)
                return 31 if p["kind"] == "cmp" else (hi - lo) * P

            @staticmethod
            def queries(p, kt):
                return [qt for qt in range(NT) if ranges(p["kind"], qt)[0] <= kt < ranges(p["kind"], qt)[1]]

            def pe(self):
                n = len(self.passes)
                for p in range(n + 1):
                    if p < n:
                        self.pe_scores(p)
                    if p >= 1:
                        self.pe_values(p - 1)

            def pe_scores(self, p):
                w = self.passes[p]
                kind = w["kind"]
                if kind == "fox":
                    pe.wait_ge(self.bias_ready, p) if p else None
                    pe.matmul(B[5][:, :], w["sel"], w["bias"], start=True, stop=True).then_inc(self.bias_turned, 1)
                for qt in range(NT):
                    g = NT * p + qt
                    if g >= 2:
                        pe.wait_ge(self.exp_done, g - 1)
                    lo, hi = ranges(kind, qt)
                    m = self.width(w, qt)
                    keys = w["k"][:, 0:31] if kind == "cmp" else w["k"][:, lo * P:hi * P]
                    masked = []
                    if kind in ("causal", "window", "fox"):
                        masked.append((causal_neg, (qt - lo) * P))
                    if kind == "window" and qt >= 2:
                        masked.append((window_neg, 0))
                    last = pe.matmul(B[g % 2][:, 0:m], w["q"][:, qt * P:(qt + 1) * P], keys, start=True, stop=True,
                                     skip_group_check=True)
                    for j, (mask, at) in enumerate(masked):
                        last = pe.matmul(B[g % 2][:, at:at + P], identb, mask, start=False, stop=True,
                                         skip_group_check=True)
                    last.then_inc(self.s_ready, 1)

            def pe_values(self, p):
                w = self.passes[p]
                nkt = self.key_tiles(w)
                ob = B[4]
                pe.wait_ge(self.p_normed, NT * (p + 1))
                for kt in range(nkt + 1):
                    if kt < nkt:
                        c = self.base[p] + kt
                        if c >= 2:
                            pe.wait_ge(self.pt_ready, c - 1)
                        rows = 31 if w["kind"] == "cmp" else P
                        for qt in self.queries(w, kt):
                            at = 0 if w["kind"] == "cmp" else (kt - ranges(w["kind"], qt)[0]) * P
                            last = pe.transpose(B[2 + c % 2][0:rows, qt * P:(qt + 1) * P],
                                                self.P[:, p % 2, qt, at:at + rows], ident)
                        last.then_inc(self.pt_turned, 1)
                    if kt >= 1:
                        c = self.base[p] + kt - 1
                        pe.wait_ge(self.pt_ready, c + 1)
                        if kt == 1 and w["opens"] and w["pair"]:
                            pe.wait_ge(self.o_free, w["pair"])
                        qs = self.queries(w, kt - 1)
                        rows = 31 if w["kind"] == "cmp" else P
                        half = HD * w["half"]
                        pe.matmul(ob[half:half + HD, qs[0] * P:(qs[-1] + 1) * P], w["v"](kt - 1),
                                  self.PT[0:rows, c % 2, qs[0] * P:(qs[-1] + 1) * P],
                                  start=(w["opens_head"] and kt == 1), stop=True,
                                  skip_group_check=True).then_inc(self.pv_done, 1)

            def act(self):
                n = len(self.passes)
                for p in range(n + 1):
                    if p < n:
                        for qt in range(NT):
                            self.act_exp(p, qt)
                    if p >= 1:
                        self.act_turn(p - 1)

            def act_exp(self, p, qt):
                w = self.passes[p]
                g = NT * p + qt
                m = self.width(w, qt)
                act.wait_ge(self.max_ready, g + 1)
                if p >= 2 and qt == 0:
                    act.wait_ge(self.pt_turned, self.base[p - 1])
                src = self.S[:, g % 2, 0:m] if w["kind"] in ("fox", "cmp") else B[g % 2][:, 0:m]
                col = (p % 2) * NT + qt
                act.activation(self.P[:, p % 2, qt, 0:m], src, ACT.Exp, scale=SCALE, bias=self.stat[:, 1, col:col + 1],
                               accum_out=self.stat[:, 2, col:col + 1]).then_inc(self.exp_done, 1)

            def act_turn(self, p):
                w = self.passes[p]
                for kt in range(self.key_tiles(w)):
                    c = self.base[p] + kt
                    act.wait_ge(self.pt_turned, c + 1)
                    if c >= 2:
                        act.wait_ge(self.pv_done, c - 1)
                    qs = self.queries(w, kt)
                    rows = 31 if w["kind"] == "cmp" else P
                    a, b = qs[0] * P, (qs[-1] + 1) * P
                    act.activation(self.PT[0:rows, c % 2, a:b], B[2 + c % 2][0:rows, a:b], ACT.Copy).then_inc(self.pt_ready, 1)

            def dve(self):
                n = len(self.passes)
                for p in range(n + 1):
                    if p < n and self.passes[p]["kind"] == "fox":
                        dve.wait_ge(self.bias_turned, p + 1)
                        ins = dve.tensor_copy(self.extra[:, p % 2, :], B[5][:, :])
                        ins.then_inc(self.bias_ready, 1)
                        dve.wait_ge(self.bias_ready, p + 1)
                    for qt in range(NT):
                        if qt == 2 and p >= 1:
                            self.dve_normalise(p - 1)
                        if p < n:
                            self.dve_max(p, qt)
                    if p >= 1 and self.passes[p - 1]["closes"]:
                        self.dve_output(p - 1)

            def dve_max(self, p, qt):
                w = self.passes[p]
                g = NT * p + qt
                m = self.width(w, qt)
                col = (p % 2) * NT + qt
                dve.wait_ge(self.s_ready, g + 1)
                if w["kind"] in ("fox", "cmp"):
                    bias = self.extra[:, p % 2, 0:m] if w["kind"] == "fox" else w["bias"][:, qt, 0:m]
                    if g >= 2:
                        dve.wait_ge(self.exp_done, g - 1)
                    link(dve, dve.tensor_tensor_reduce(self.S[:, g % 2, 0:m], B[g % 2][:, 0:m], bias, 1.0, -3e38, ALU.add,
                                                       ALU.max, self.stat[:, 0, col:col + 1]))
                else:
                    link(dve, dve.reduce_max(self.stat[:, 0, col:col + 1], B[g % 2][:, 0:m], AX_X))
                dve.tensor_scalar(self.stat[:, 1, col:col + 1], self.stat[:, 0, col:col + 1], -SCALE, None, ALU.mult)\
                    .then_inc(self.max_ready, 1)

            def dve_normalise(self, p):
                w = self.passes[p]
                a, b = (p % 2) * NT, (p % 2) * NT + NT
                dve.wait_ge(self.exp_done, NT * (p + 1))
                link(dve, dve.reciprocal(self.stat[:, 3, a:b], self.stat[:, 2, a:b]))
                if self.gate is not None:
                    link(dve, dve.tensor_tensor(self.stat[:, 3, a:b], self.stat[:, 3, a:b], self.gate[:, :, w["gate"]],
                                                ALU.mult))
                for qt in range(NT):
                    m = self.width(w, qt)
                    pr = self.P[:, p % 2, qt, 0:m]
                    if w["kind"] == "cmp":
                        dve.scalar_tensor_tensor(pr, pr, self.stat[:, 3, a + qt:a + qt + 1], w["keep"][:, qt, 0:m],
                                                 ALU.mult, ALU.mult).then_inc(self.p_normed, 1)
                    else:
                        dve.tensor_scalar(pr, pr, self.stat[:, 3, a + qt:a + qt + 1], None, ALU.mult).then_inc(self.p_normed, 1)

            def dve_output(self, p):
                w = self.passes[p]
                dve.wait_ge(self.pv_done, self.base[p + 1])
                ins = dve.tensor_copy(self.y[:, :], B[4][:, :])
                ins.then_inc(self.o_free, 1)
                dve.wait_ge(self.o_free, w["pair"] + 1)
                hi, lo = self.out_tile(w["pair"])
                split_dve(hi, lo, self.y[:, :])

        def make_passes(per_head):
            passes = []
            for h, ps in enumerate(per_head):
                for j, p in enumerate(ps):
                    passes.append(dict(p, pair=h // 2, half=h % 2, opens=(h % 2 == 0 and j == 0),
                                       opens_head=(j == 0), closes_head=(j == len(ps) - 1),
                                       closes=(h % 2 == 1 and j == len(ps) - 1)))
            return passes

        def turn_pe(tiles, base):
            for i, t in enumerate(tiles):
                n = base + i
                if n >= 2:
                    pe.wait_ge(v_ready, n - 1)
                for tt in range(NT):
                    last = pe.transpose(B[n % 2][:, tt * P:(tt + 1) * P], t[:, tt * P:(tt + 1) * P], ident)
                last.then_inc(v_turned, 1)

        def turn_act(outs, base):
            for i, o in enumerate(outs):
                n = base + i
                act.wait_ge(v_turned, n + 1)
                act.activation(o, B[n % 2][:, :].rearrange("p (t f) -> p t f", t=NT), ACT.Copy).then_inc(v_ready, 1)

        class Recurrence:

            def __init__(self, dirs, BB, gap, decay, QL, KL, SS):
                self.dirs, self.BB, self.gap, self.decay, self.QL, self.KL, self.SS = dirs, BB, gap, decay, QL, KL, SS
                self.steps = [(d, h) for d in range(dirs) for h in [T // 2, T // 4] + LEVELS] + [(0, 0)]
                self.n = len(self.steps)

            def scores_of(self, d, h):
                if h == T // 2:
                    return [(0, 2, 2), (1, 2, 2)] if d == 0 else [(2, 0, 2), (3, 0, 2)]
                if h == T // 4:
                    return [(0, 1, 1), (2, 3, 1)] if d == 0 else [(1, 0, 1), (3, 2, 1)]
                return [(t, t, 1) for t in range(NT)]

            @staticmethod
            def block_of(jt, it):
                if jt == it:
                    return jt
                far = (jt < 2) != (it < 2)
                if jt < it:
                    return 4 + 2 * jt + it - 2 if far else 8 + jt // 2
                return 10 + 2 * (jt - 2) + it if far else 14 + it // 2

            def dve(self, run, q, ks, both):
                for s in range(self.n + 2):
                    if s < self.n and self.steps[s][1]:
                        d, h = self.steps[s]
                        i = self.n * run + s
                        nb = T // (2 * h)
                        X = self.BB[:, d, 1 - d:1 - d + T].rearrange("p (b w) -> p b w", w=2 * h)
                        ref = self.BB[:, d, 0:T].rearrange("p (b w) -> p b w", w=2 * h)[:, :, h:h + 1]\
                            .to_broadcast([P, nb, h])
                        G = self.gap[:, s % 2, :].rearrange("p (b w) -> p b w", w=2 * h)
                        if s >= 2:
                            dve.wait_ge(decay_ready, (self.n - 1) * run + s - 1)
                        dve.tensor_tensor(G[:, :, 0:h], ref, X[:, :, 0:h], ALU.subtract)
                        dve.tensor_tensor(G[:, :, h:2 * h], X[:, :, h:2 * h], ref, ALU.subtract).then_inc(gap_ready, 1)
                    if 1 <= s <= self.n:
                        d, h = self.steps[s - 1]
                        if h:
                            dve.wait_ge(decay_ready, (self.n - 1) * run + s)
                            if s >= 3:
                                dve.wait_ge(level_scored, self.n * run + s - 2)
                            E = self.decay[:, (s - 1) % 2, :]
                            dve.tensor_tensor(self.QL[:, (s - 1) % 2, :], q, E, ALU.mult)
                            dve.tensor_tensor(self.KL[:, (s - 1) % 2, :], ks[d], E, ALU.mult).then_inc(terms_ready, 1)
                        elif self.dirs == 2:
                            dve.tensor_tensor(both, ks[0], ks[1], ALU.add).then_inc(terms_ready, 1)
                        else:
                            dve.drain().then_inc(terms_ready, 1)
                    if s >= 2:
                        d, h = self.steps[s - 2]
                        i = self.n * run + s - 2
                        dve.wait_ge(level_scored, i + 1)
                        if i:
                            dve.wait_ge(level_kept, i)
                        for a in range(2):
                            bank = B[2 * (i % 2) + a]
                            if h == T // 2:
                                b = 4 if d == 0 else 10
                                last = dve.tensor_copy(self.SS[:, a, b:b + 4, :],
                                                       bank[:, :].rearrange("p (b f) -> p b f", f=P))
                            elif h == T // 4:
                                b = 8 if d == 0 else 14
                                last = dve.tensor_copy(self.SS[:, a, b:b + 2, :],
                                                       bank[:, 0:2 * P].rearrange("p (b f) -> p b f", f=P))
                            else:
                                m = LEVELS.index(h) + d * len(LEVELS) if h else 2 * len(LEVELS)
                                last = dve.copy_predicated(self.SS[:, a, 0:4, :],
                                                           masks[:, m:m + 1, :].to_broadcast([P, NT, P]),
                                                           bank[:, :].rearrange("p (b f) -> p b f", f=P))
                        last.then_inc(level_kept, 1)

            def act(self, run):
                for s in range(self.n - 1):
                    i = (self.n - 1) * run + s
                    act.wait_ge(gap_ready, i + 1)
                    if s >= 2:
                        act.wait_ge(terms_ready, self.n * run + s - 1)
                    act.activation(self.decay[:, s % 2, :], self.gap[:, s % 2, :], ACT.Exp).then_inc(decay_ready, 1)

            def pe(self, run, q, both):
                for s in range(self.n):
                    d, h = self.steps[s]
                    i = self.n * run + s
                    pe.wait_ge(terms_ready, i + 1)
                    if s >= 2:
                        pe.wait_ge(level_kept, i - 1)
                    QQ, KK = (self.QL[:, s % 2, :], self.KL[:, s % 2, :]) if h else (q, both)
                    for a in range(2):
                        r = slice(HD * a, HD * a + HD)
                        at = 0
                        todo = self.scores_of(d, h)
                        for j, (jt, it, w) in enumerate(todo):
                            last = pe.matmul(B[2 * (i % 2) + a][:, at:at + w * P], KK[r, jt * P:(jt + 1) * P],
                                             QQ[r, it * P:(it + w) * P], start=(j == 0), stop=True,
                                             skip_group_check=True)
                            at += w * P
                    last.then_inc(level_scored, 1)

            def pe_values(self, run, a, v, bank, rows):
                pe.wait_ge(level_kept, self.n * (run + 1))
                pairs = [(jt, it) for it in range(NT) for jt in range(NT) if jt <= it or self.dirs == 2]
                for j, (jt, it) in enumerate(pairs):
                    last = pe.matmul(bank[rows, it * P:(it + 1) * P], v(jt), self.SS[:, a, self.block_of(jt, it), :],
                                     start=(j == 0), stop=True, skip_group_check=True)
                return last

        def softplus_of_minus(dst, src, **kw):
            link(act, act.activation(dst, src, ACT.Abs, **kw))
            link(act, act.activation(dst, dst, ACT.Exp, scale=-1.0))
            return act.activation(dst, dst, ACT.Ln, bias=1.0)

        def load_start():
            scope = ExitStack()
            with scope:
                x_tok = sb("x_tok", [P, NT, D], F32, scope)
                masks_f = sb("masks_f", [P, 2 * len(LEVELS) + 1, P], F32, scope)
                with nc.Block() as block:
                    @block.sync
                    def _(sp):
                        sp.dma_start(C[:, :, :], consts_in).then_inc(consts_loaded, 16)
                        sp.dma_start(x_tok[:, :, :], x_in[0].rearrange("(t p) d -> p t d", p=P)).then_inc(x_loaded, 16)
                        sp.dma_start(masks_f[:, :, :], masks_in).then_inc(consts_loaded, 16)
                        sp.dma_start(cosT[:, :], rope_in[0]).then_inc(consts_loaded, 16)
                        sp.dma_start(sinT[:, :], rope_in[1]).then_inc(consts_loaded, 16)

                    @block.tensor
                    def _(pe):
                        pe.wait_ge(consts_loaded, 64)
                        pe.wait_ge(x_loaded, 16)
                        for k in range(NK):
                            if k >= 2:
                                pe.wait_ge(v_ready, k - 1)
                            for t in range(NT):
                                last = pe.transpose(B[k % 2][:, t * P:(t + 1) * P], x_tok[:, t, k * P:(k + 1) * P], ident)
                            last.then_inc(v_turned, 1)

                    @block.scalar
                    def _(act):
                        for k in range(NK):
                            act.wait_ge(v_turned, k + 1)
                            act.activation(xT[:, k, :], B[k % 2][:, :], ACT.Copy).then_inc(v_ready, 1)

                    @block.vector
                    def _(dve):
                        dve.wait_ge(consts_loaded, 64)
                        dve.tensor_copy(masks[:, :, :], masks_f[:, :, :])
                        dve.tensor_copy(Cb[:, 0, :], C[:, 0, :])
                        dve.tensor_copy(Cb[:, 1:4, :], C[:, 7:10, :])
                        dve.memset(lb_now[:, :, 0], NEG)
                        dve.memset(lb_now[:, :, 1], 0.0)
            clear()

        lb_now = sb("lb_now", [P, 4, 2])
        lb_gap = sb("lb_gap", [P, 2, 4])
        bound_gap, bound_softplus = sem("bound_gap"), sem("bound_softplus")

        def next_bounds_act():
            act.wait_ge(bound_gap, 1)
            softplus_of_minus(lb_gap[:, 1, :], lb_gap[:, 0, :]).then_inc(bound_softplus, 1)

        def next_bounds_dve():
            for d, (first, second) in enumerate((("lb_f0", "lb_f1"), ("lb_b0", "lb_b1"))):
                last = dve.tensor_tensor(lb_gap[:, 0, 2 * d:2 * d + 2], vec[:, V1[second]:V1[second] + 2],
                                         vec[:, V1[first]:V1[first] + 2], ALU.subtract)
            last.then_inc(bound_gap, 1)
            dve.wait_ge(bound_softplus, 1)
            link(dve, dve.scalar_tensor_tensor(lb_now[:, :, 0], lb_gap[:, 0, :], 0.0, lb_gap[:, 1, :],
                                               ALU.min, ALU.subtract))
            dve.tensor_tensor(lb_now[:, :, 1], lb_now[:, :, 0], lb_gap[:, 0, :], ALU.subtract)

        def first_layer(L):
            units, first_unit, first_tile = plan_units(GROUPS1)
            stages = STAGES1
            new_layer()
            scope = ExitStack()
            with scope:
                tmp = sb("tmp", [P, T], F32, scope)
                pair = sb("pair", [P, 2, T], F32, scope)
                yt = sb("yt", [P, 2, T], F32, scope)
                with ExitStack() as mlp_scope:
                    midH = sb("midH", [P, NK, T], F32R, mlp_scope)
                    midL = sb("midL", [P, NK, T], F32R, mlp_scope)
                Z = sb("Z", [P, 20, T], F32, scope)
                phases = {}
                with ExitStack() as s1:
                    phases["att"] = dict(P=sb("probs", [P, 2, NT, T], F32, s1), PT=sb("probsT", [P, 2, T], F32, s1),
                                         stat=sb("stat", [P, 4, 8], F32, s1))
                with ExitStack() as s1:
                    phases["hgrn"] = dict(BB=sb("cum", [P, 2, T + 1], F32, s1), gap=sb("gap", [P, 2, T], F32, s1),
                                          decay=sb("decay", [P, 2, T], F32, s1), QL=sb("QL", [P, 2, T], F32, s1),
                                          KL=sb("KL", [P, 2, T], F32, s1), SS=sb("SS", [P, 2, 16, P], F32, s1),
                                          keys=sb("keys", [P, 3, T], F32, s1), t=sb("terms", [P, 3, T], F32, s1))
                with ExitStack() as s1:
                    phases["conv"] = dict(u=sb("conv_u", [P, 2, T + 30], F32, s1), c=sb("conv_c", [P, 2, T], F32, s1),
                                          s=sb("conv_s", [P, 2, T], F32, s1), m=sb("conv_m", [P, T], F32, s1))
                v_tok = [Z[:, t, :].rearrange("p (t f) -> p t f", t=NT) for t in (5, 8, 9)]
                A, Hg, Cv = phases["att"], phases["hgrn"], phases["conv"]

                def y_tile(t):
                    return hH[:, t, :], hL[:, t, :]

                passes = make_passes([[dict(kind="full", q=Z[HD * (h // 4):HD * (h // 4) + HD, h % 4, :],
                                            k=Z[HD * (h // 4):HD * (h // 4) + HD, 4, :],
                                            v=(lambda kt, g=h // 4: v_tok[0][:, kt, HD * g:HD * g + HD]))]
                                      for h in range(8)])
                att = Attention(attention_sems[0], passes, A["P"], A["PT"], None, A["stat"], yt[:, 0, :], None, None, y_tile)
                rec = Recurrence(2, Hg["BB"], Hg["gap"], Hg["decay"], Hg["QL"], Hg["KL"], Hg["SS"])

                with nc.Block() as block:
                    @block.sync
                    def _(sp):
                        sp.dma_start(vec[:, 0:NV1], vec1_in[bass.ds(L, 1)].rearrange("a p n -> (a p) n"))\
                            .then_inc(vec_loaded, 16)
                        load_weights(units, w1_in, L)

                    @block.gpsimd
                    def _(pool):
                        split_lo(units)

                    @block.tensor
                    def _(pe):
                        norm_pe(0, pair)
                        finish(pe, "norm0")
                        after(pe, stages, "norm0", dve_finished)
                        products(units, "in", lambda nk: (hH, hL))
                        finish(pe, "in")
                        after(pe, stages, "in", act_finished)
                        for t in range(5):
                            pe.wait_ge(z_squared, t + 1)
                            pe.matmul(B[0][:, :], pair_ones, pair[:, t % 2, :], start=True, stop=True).then_inc(z_summed, 1)
                            pe.wait_ge(z_normed, t + 1)
                            pe.matmul(B[1][:, :], rot1, Z[:, t, :], start=True, stop=True).then_inc(z_rotated, 1)
                        finish(pe, "prep")
                        after(pe, stages, "prep", act_finished, dve_finished)
                        turn_pe([Z[:, 5, :]], 0)
                        pe.wait_ge(v_ready, 1)
                        att.pe()
                        finish(pe, "att")
                        after(pe, stages, "att", act_finished, dve_finished)
                        for r in range(2):
                            turn_pe([Z[:, 8 + r, :]], 1 + r)
                            pe.wait_ge(v_ready, 2 + r)
                            rec.pe(r, Z[:, 6 + r, :], Hg["keys"][:, 2, :])
                            for a in range(2):
                                last = rec.pe_values(r, a, lambda jt: v_tok[1 + r][:, jt, HD * a:HD * a + HD], B[4],
                                                     slice(HD * a, HD * a + HD))
                            last.then_inc(o_ready, 1)
                            pe.wait_ge(o_squared, r + 1)
                            pe.matmul(B[5][:, :], pair_ones, pair[:, 0, :], start=True, stop=True).then_inc(o_summed, 1)
                        finish(pe, "hgrn")
                        after(pe, stages, "hgrn", act_finished, dve_finished)
                        for j in range(2):
                            pe.wait_ge(conv_ready, j + 1)
                            last = pe.matmul(B[0][:, :], ones, Cv["c"][:, j, :], start=(j == 0), stop=(j == 1))
                        last.then_inc(conv_summed, 1)
                        for j in range(2):
                            pe.wait_ge(conv_squared, j + 1)
                            last = pe.matmul(B[1][:, :], ones, Cv["s"][:, j, :], start=(j == 0), stop=(j == 1))
                        last.then_inc(conv_var, 1)
                        finish(pe, "conv")
                        after(pe, stages, "conv", dve_finished)
                        products(units, "out", lambda nk: (hH, hL))
                        finish(pe, "out")
                        norm_pe(1, pair)
                        finish(pe, "norm1")
                        mlp(units, stages, "pe", midH, midL, None)

                    @block.scalar
                    def _(act):
                        split_hi(units, 0)
                        split_hi(units, 1)
                        norm_act(0, pair, tmp)
                        finish(act, "norm0")

                        def to_Z(n, t, a):
                            act.activation(Z[:, t, :], a[:, :], ACT.Copy).then_inc(acc_free[n % 2], 1)
                        act_group(units, "in", to_Z)
                        finish(act, "in")
                        for t in range(5):
                            if t >= 2:
                                act.wait_ge(z_summed, t - 1)
                            act.activation(pair[:, t % 2, :], Z[:, t, :], ACT.Square).then_inc(z_squared, 1)
                            act.wait_ge(z_summed, t + 1)
                            if t:
                                act.wait_ge(z_normed, t)
                            link(act, act.activation(tmp[:, :], B[0][:, :], ACT.Ln, bias=EPS, scale=1.0 / HD))
                            act.activation(tmp[:, :], tmp[:, :], ACT.Exp, scale=-0.5).then_inc(z_rstd, 1)
                        finish(act, "prep")
                        after(act, stages, "prep", pe_finished, dve_finished)
                        turn_act([v_tok[0]], 0)
                        att.act()
                        finish(act, "att")
                        after(act, stages, "att", pe_finished, dve_finished)
                        for r in range(2):
                            turn_act([v_tok[1 + r]], 1 + r)
                            for d in range(2):
                                f = Z[:, 10 + 2 * d + r, :]
                                i = 2 * r + d
                                if i:
                                    act.wait_ge(key_ready, i)
                                link(act, softplus_of_minus(Hg["t"][:, 0, :], f))
                                softplus_of_minus(Hg["t"][:, 1, :], f, scale=-1.0, bias=lb_now[:, 2 * d + r, 0:1])\
                                    .then_inc(softplus_ready, 1)
                                act.wait_ge(rate_ready, i + 1)
                                act.activation(Hg["keys"][:, d, :], Hg["t"][:, 0, :], ACT.Exp,
                                               bias=lb_now[:, 2 * d + r, 1:2]).then_inc(key_ready, 1)
                            rec.act(r)
                            act.wait_ge(o_taken, r + 1)
                            act.activation(pair[:, 0, :], yt[:, 0, :], ACT.Square).then_inc(o_squared, 1)
                            act.wait_ge(o_summed, r + 1)
                            link(act, act.activation(tmp[:, :], B[5][:, :], ACT.Ln, bias=EPS, scale=1.0 / HD))
                            act.activation(tmp[:, :], tmp[:, :], ACT.Exp, scale=-0.5).then_inc(o_rstd, 1)
                            act.activation(pair[:, 1, :], Z[:, 14 + r, :], ACT.Sigmoid).then_inc(gate_ready, 1)
                        finish(act, "hgrn")
                        after(act, stages, "hgrn", pe_finished, dve_finished)
                        for j in range(2):
                            act.activation(Cv["c"][:, j, :], Z[:, 18 + j, :], ACT.Sigmoid).then_inc(conv_gate, 1)
                        for j in range(2):
                            act.wait_ge(conv_mean, j + 1)
                            act.activation(Cv["s"][:, j, :], Cv["c"][:, j, :], ACT.Square).then_inc(conv_squared, 1)
                        act.wait_ge(conv_var, 1)
                        link(act, act.activation(tmp[:, :], B[1][:, :], ACT.Ln, bias=EPS, scale=1.0 / (2 * P)))
                        act.activation(tmp[:, :], tmp[:, :], ACT.Exp, scale=-0.5).then_inc(conv_rstd, 1)
                        for j in range(2):
                            act.wait_ge(conv_pre, j + 1)
                            act.activation(Cv["s"][:, j, :], Cv["c"][:, j, :], ACT.Sigmoid).then_inc(conv_gate, 1)
                        finish(act, "conv")
                        act_group(units, "out")
                        next_bounds_act()
                        finish(act, "out")
                        after(act, stages, "out", dve_finished)
                        norm_act(1, pair, tmp)
                        finish(act, "norm1")
                        mlp(units, stages, "act", midH, midL, pair)

                    @block.vector
                    def _(dve):
                        dve.wait_ge(vec_loaded, 16)
                        norm_dve(0, V1["norm_mix"], tmp, yt)
                        finish(dve, "norm0")
                        finish(dve, "in")
                        after(dve, stages, "in", act_finished)
                        for t in range(5):
                            col = V1["q_norm"] if t < 4 else V1["k_norm"]
                            dve.wait_ge(z_rstd, t + 1)
                            ins = dve.scalar_tensor_tensor(Z[:, t, :], Z[:, t, :], vec[:, col:col + 1], tmp[:, :],
                                                           ALU.mult, ALU.mult)
                            ins.then_inc(z_normed, 1)
                            dve.wait_ge(z_normed, t + 1)
                            dve.wait_ge(z_rotated, t + 1)
                            link(dve, dve.tensor_tensor(yt[:, 0, :], B[1][:, :], sinT[:, :], ALU.mult))
                            link(dve, dve.tensor_tensor(yt[:, 1, :], Z[:, t, :], cosT[:, :], ALU.mult))
                            link(dve, dve.tensor_tensor(Z[:, t, :], yt[:, 0, :], yt[:, 1, :], ALU.add))
                        finish(dve, "prep")
                        after(dve, stages, "prep", pe_finished, act_finished)
                        att.dve()
                        finish(dve, "att")
                        after(dve, stages, "att", pe_finished, act_finished)
                        t_, BB, keys = Hg["t"], Hg["BB"], Hg["keys"]
                        dve.memset(BB[:, :, 0:1], 0.0)
                        dve.memset(Hg["SS"][:, :, :, :], 0.0)
                        for r in range(2):
                            for d in range(2):
                                f = Z[:, 10 + 2 * d + r, :]
                                i = 2 * r + d
                                dve.wait_ge(softplus_ready, i + 1)
                                link(dve, dve.tensor_scalar(t_[:, 2, :], f, -1.0, lb_now[:, 2 * d + r, 0:1], ALU.mult, ALU.add))
                                link(dve, dve.scalar_tensor_tensor(t_[:, 2, :], t_[:, 2, :], 0.0, t_[:, 1, :],
                                                                   ALU.max, ALU.add))
                                link(dve, dve.scalar_tensor_tensor(t_[:, 0, :], f, 0.0, t_[:, 0, :], ALU.min, ALU.subtract))
                                link(dve, dve.tensor_tensor(t_[:, 2, :], t_[:, 2, :], t_[:, 0, :], ALU.add))
                                link(dve, dve.tensor_tensor_scan(BB[:, d, 1:T + 1], ones[:, 0:1].to_broadcast([P, T]),
                                                                 t_[:, 2, :], 0.0, ALU.mult, ALU.add))
                                dve.tensor_tensor(t_[:, 0, :], t_[:, 0, :], f, ALU.subtract).then_inc(rate_ready, 1)
                            dve.wait_ge(key_ready, 2 * r + 2)
                            rec.dve(r, Z[:, 6 + r, :], [keys[:, 0, :], keys[:, 1, :]], keys[:, 2, :])
                            dve.wait_ge(o_ready, r + 1)
                            dve.tensor_copy(yt[:, 0, :], B[4][:, :]).then_inc(o_taken, 1)
                            dve.wait_ge(gate_ready, r + 1)
                            link(dve, dve.tensor_tensor(pair[:, 1, :], pair[:, 1, :], Z[:, 14 + r, :], ALU.mult))
                            dve.wait_ge(o_rstd, r + 1)
                            col = V1["hgrn_norm"] + r
                            link(dve, dve.scalar_tensor_tensor(yt[:, 0, :], yt[:, 0, :], vec[:, col:col + 1], tmp[:, :],
                                                               ALU.mult, ALU.mult))
                            link(dve, dve.tensor_tensor(yt[:, 0, :], yt[:, 0, :], pair[:, 1, :], ALU.mult))
                            split_dve(hH[:, 4 + r, :], hL[:, 4 + r, :], yt[:, 0, :])
                        finish(dve, "hgrn")
                        after(dve, stages, "hgrn", pe_finished, act_finished)
                        U, c, s_ = Cv["u"], Cv["c"], Cv["s"]
                        for j in range(2):
                            dve.memset(U[:, j, 0:15], 0.0)
                            dve.memset(U[:, j, T + 15:T + 30], 0.0)
                            dve.wait_ge(conv_gate, j + 1)
                            link(dve, dve.tensor_tensor(U[:, j, 15:T + 15], Z[:, 16 + j, :], c[:, j, :], ALU.mult))
                            for tap in range(31):
                                w = V1["conv_w"] + 2 * tap + j
                                src = U[:, j, tap:tap + T]
                                if tap == 0:
                                    b = V1["conv_b"] + j
                                    ins = dve.tensor_scalar(c[:, j, :], src, vec[:, w:w + 1], vec[:, b:b + 1], ALU.mult, ALU.add)
                                else:
                                    ins = dve.scalar_tensor_tensor(c[:, j, :], src, vec[:, w:w + 1], c[:, j, :],
                                                                   ALU.mult, ALU.add)
                                if tap < 30:
                                    link(dve, ins)
                            ins.then_inc(conv_ready, 1)
                        dve.wait_ge(conv_summed, 1)
                        link(dve, dve.tensor_scalar(Cv["m"][:, :], B[0][:, :], 1.0 / (2 * P), None, ALU.mult))
                        for j in range(2):
                            dve.tensor_tensor(c[:, j, :], c[:, j, :], Cv["m"][:, :], ALU.subtract).then_inc(conv_mean, 1)
                        dve.wait_ge(conv_rstd, 1)
                        for j in range(2):
                            g, b = V1["ln_g"] + j, V1["ln_b"] + j
                            link(dve, dve.tensor_tensor(c[:, j, :], c[:, j, :], tmp[:, :], ALU.mult))
                            dve.tensor_scalar(c[:, j, :], c[:, j, :], vec[:, g:g + 1], vec[:, b:b + 1], ALU.mult, ALU.add)\
                                .then_inc(conv_pre, 1)
                        for j in range(2):
                            dve.wait_ge(conv_gate, 3 + j)
                            link(dve, dve.tensor_tensor(c[:, j, :], c[:, j, :], s_[:, j, :], ALU.mult))
                            split_dve(hH[:, 6 + j, :], hL[:, 6 + j, :], c[:, j, :])
                        finish(dve, "conv")
                        dve_group(units, "out", add_to_x)
                        next_bounds_dve()
                        finish(dve, "out")
                        norm_dve(1, V1["norm_mlp"], tmp, yt)
                        finish(dve, "norm1")
                        mlp(units, stages, "dve", midH, midL, pair)
            clear()

        stacked, cmp_loaded, cmp_used, blocks_ready, hidden_ready, hidden_gelu, cmp_made, cmp_taken, cmp_turned = (
            sem(n) for n in ("stacked", "cmp_loaded", "cmp_used", "blocks_ready", "hidden_ready", "hidden_gelu", "cmp_made",
                             "cmp_taken", "cmp_turned"))
        mask_loaded = sem("mask_loaded")
        alpha_loaded, branch_mixed, z_made, sp_part, sp_ready, logit_ready, a_ready, stick_done, stick_taken = (
            sem(n) for n in ("alpha_loaded", "branch_mixed", "z_made", "sp_part", "sp_ready", "logit_ready", "a_ready",
                             "stick_done", "stick_taken"))
        gate_turned, angle_ready, sine_ready, alpha_made, alpha_biased = (
            sem(n) for n in ("gate_turned", "angle_ready", "sine_ready", "alpha_made", "alpha_biased"))

        def start_second():
            new_layer()
            turn = 2 * np.pi
            parts = [6.28125]
            parts.append(float(np.float32(round((turn - parts[0]) * 2 ** 20) / 2 ** 20)))
            parts.append(turn - parts[0] - parts[1])
            to_whole = 1.5 * 2 ** 23
            edge = 3.1415925
            scope = ExitStack()
            with scope:
                pos = sb("pos", [P, T], I32, scope)
                freq = sb("freq", [P, 2], F32, scope)
                ang, n, s2 = (sb(x, [P, T], F32, scope) for x in ("ang", "turns", "s2"))
                with nc.Block() as block:
                    @block.sync
                    def _(sp):
                        sp.dma_start(pos[:, :], pos_in[0:1, :].to_broadcast([P, T])).then_inc(x_loaded, 16)
                        sp.dma_start(freq[:, :], freq_in).then_inc(x_loaded, 16)

                    @block.vector
                    def _(dve):
                        dve.wait_ge(x_loaded, 32)
                        link(dve, dve.tensor_copy(ang[:, :], pos[:, :]))
                        link(dve, dve.tensor_scalar(ang[:, :], ang[:, :], freq[:, 0:1], None, ALU.mult))
                        link(dve, dve.tensor_scalar(n[:, :], ang[:, :], 1.0 / turn, to_whole, ALU.mult, ALU.add))
                        link(dve, dve.tensor_scalar(n[:, :], n[:, :], -to_whole, None, ALU.add))
                        for part in parts:
                            link(dve, dve.scalar_tensor_tensor(ang[:, :], n[:, :], -part, ang[:, :], ALU.mult, ALU.add))
                        dve.tensor_scalar(ang[:, :], ang[:, :], -edge, edge, ALU.max, ALU.min).then_inc(angle_ready, 1)
                        dve.wait_ge(sine_ready, 1)
                        link(dve, dve.tensor_tensor(s2[:, :], s2[:, :], s2[:, :], ALU.mult))
                        dve.tensor_scalar(cosT[:, :], s2[:, :], -2.0, 1.0, ALU.mult, ALU.add)

                    @block.scalar
                    def _(act):
                        act.wait_ge(angle_ready, 1)
                        act.activation(sinT[:, :], ang[:, :], ACT.Sin)
                        act.activation(s2[:, :], ang[:, :], ACT.Sin, scale=0.5).then_inc(sine_ready, 1)
            clear()

        def second_layer(L):
            units, first_unit, first_tile = plan_units(GROUPS2)
            stages = STAGES2
            new_layer()
            scope = ExitStack()
            with scope:
                tmp = sb("tmp2", [P, T], F32, scope)
                pair = sb("pair2", [P, 2, T], F32, scope)
                yt = sb("yt2", [P, 2, T], F32, scope)
                with ExitStack() as s1:
                    midH = sb("midH2", [P, NK, T], F32R, s1)
                    midL = sb("midL2", [P, NK, T], F32R, s1)
                mixed = sb("mixed", [P, NK, T], F32, scope)
                yH = sb("yH", [P, 4, T], F32R, scope)
                yL = sb("yL", [P, 4, T], F32R, scope)
                small = sb("small", [P, T], F32, scope)
                with ExitStack() as s1:
                    sig = sb("sig", [P, 4, T], F32, s1)
                Z = sb("Z2", [P, 12, T], F32, scope)
                with ExitStack() as s1:
                    stack = sb("stack", [P, 4, T], F32, s1)
                    blocks_sb = sb("cblocks", [P, 16, 62], F32, s1)
                    cw1 = sb("cw1", [P, 16, 256], F32, s1)
                kc = Z[:, 10, 0:31]
                vc = Z[0:31, 10, 32:160]
                hid = Z[:, 10, 160:284].rearrange("p (m c) -> p m c", m=2)
                kraw = Z[:, 10, 288:319]
                cw2 = Z[:, 10, 320:448].rearrange("p (m c) -> p m c", m=2)
                kt2 = Z[:, 10, 448:510]
                gate = Z[:, 11, 0:96].rearrange("p (t c) -> p t c", t=NT)
                cm = Z[:, 11, 96:344].rearrange("p (m t c) -> p m t c", m=2, t=NT)
                with ExitStack() as s1:
                    probs = sb("probs2", [P, 2, NT, T], F32, s1)
                    probsT = sb("probsT2", [P, 2, T], F32, s1)
                    S_sb = sb("S_sb", [P, 2, T], F32, s1)
                    stat = sb("stat2", [P, 4, 8], F32, s1)
                    bias_sb = sb("bias_sb", [P, 2, T], F32, s1)
                with ExitStack() as s1:
                    part = sb("sp_part_sb", [P, NT, T], F32, s1)
                    soft = sb("soft_sb", [P, NT, T], F32, s1)
                    aT = sb("aT", [P, NT, T], F32, s1)
                with ExitStack() as s1:
                    BB = sb("cum2", [P, 1, T + 1], F32, s1)
                    gap, decay = sb("gap2", [P, 2, T], F32, s1), sb("decay2", [P, 2, T], F32, s1)
                    QL, KL = sb("QL2", [P, 2, T], F32, s1), sb("KL2", [P, 2, T], F32, s1)
                    SS = sb("SS2", [P, 2, 10, P], F32, s1)
                    alpha = sb("alpha", [P, 256], F32, s1)
                turned = [Z[:, t, :].rearrange("p (t f) -> p t f", t=NT) for t in range(12)]

                def y_tile(t):
                    return yH[:, t, :], yL[:, t, :]

                nsa = []
                for h in range(8):
                    g = h // 4
                    r = slice(HD * g, HD * g + HD)
                    q = Z[r, h % 4, :]
                    nsa.append([
                        dict(kind="causal", q=q, k=Z[r, 6, :], v=lambda kt, r=r: turned[7][:, kt, r], gate=3 * h + 1),
                        dict(kind="window", q=q, k=Z[r, 8, :], v=lambda kt, r=r: turned[9][:, kt, r], gate=3 * h + 2),
                        dict(kind="cmp", q=q, k=kc[r, :], v=lambda kt, r=r: vc[:, r], gate=3 * h, bias=cm[:, 0],
                             keep=cm[:, 1])])
                att = Attention(attention_sems[0], make_passes(nsa), probs, probsT, S_sb, stat, yt[:, 0, :], None, gate, y_tile)
                forget = []
                for h in range(8):
                    r = slice(HD * (h % 2), HD * (h % 2) + HD)
                    forget.append([dict(kind="fox", q=Z[r, h // 2, :], k=Z[r, 4 + h // 2, :],
                                        v=lambda kt, r=r, t=8 + h // 2: turned[t][:, kt, r],
                                        sel=ident[64:96, 64 + h:65 + h].to_broadcast([32, P]), bias=small[64:96, :])])
                fox = Attention(attention_sems[1], make_passes(forget), probs, probsT, S_sb, stat, yt[:, 0, :], bias_sb, None, y_tile)
                rec = Recurrence(1, BB, gap, decay, QL, KL, SS)

                with nc.Block() as block:
                    @block.sync
                    def _(sp):
                        sp.dma_start(vec[:, 0:NV2], vec2_in[bass.ds(L, 1)].rearrange("a p n -> (a p) n"))\
                            .then_inc(vec_loaded, 16)
                        load_weights(units, w2_in, L)

                    @block.gpsimd
                    def _(pool):
                        split_lo(units)

                    def operands(nk):
                        return (hH, hL) if nk == NK else (yH, yL)

                    @block.tensor
                    def _(pe):
                        norm_pe(0, pair)
                        finish(pe, "norm0")
                        after(pe, stages, "norm0", dve_finished)
                        products(units, "nsa", operands)
                        finish(pe, "nsa")
                        after(pe, stages, "nsa", act_finished)
                        for i, t in enumerate((0, 1, 2, 3, 6, 8)):
                            if i:
                                pe.wait_ge(z_done, i)
                            pe.matmul(B[0][:, :], rot2, Z[:, t, :], start=True, stop=True).then_inc(z_rotated, 1)
                        for t in range(NT):
                            last = pe.transpose(B[1][:, t * P:(t + 1) * P], small[:, t * P:(t + 1) * P], ident)
                        last.then_inc(gate_turned, 1)
                        finish(pe, "prep")
                        after(pe, stages, "prep", act_finished, dve_finished)
                        for kv in range(2):
                            pe.wait_ge(blocks_ready, kv + 1)
                            pe.wait_ge(cmp_loaded, 32 * (kv + 1))
                            for m in range(2):
                                for j in range(16):
                                    last = pe.matmul(B[0][:, m * 62:m * 62 + 62], cw1[:, j, m * P:(m + 1) * P],
                                                     blocks_sb[:, j, :], start=(j == 0 and m == 0), stop=(j == 15 and m == 1),
                                                     skip_group_check=True)
                            last.then_inc(hidden_ready, 1)
                            pe.wait_ge(hidden_gelu, kv + 1)
                            for g in range(2):
                                r = slice(HD * g, HD * g + HD)
                                for m in range(2):
                                    h_ = hid[:, m, 31 * g:31 * g + 31]
                                    if kv == 0:
                                        last = pe.matmul(B[1][r, 0:31], cw2[:, m, :], h_, start=(m == 0), stop=(m == 1))
                                    else:
                                        last = pe.matmul(B[2][0:31, r], h_, cw2[:, m, :], start=(m == 0 and g == 0),
                                                         stop=(m == 1 and g == 1), skip_group_check=True)
                            last.then_inc(cmp_made, 1)
                            if kv == 0:
                                pe.wait_ge(cmp_taken, 1)
                                pe.matmul(B[3][:, 0:31], rot2, kraw, start=True, stop=True).then_inc(cmp_turned, 1)
                        finish(pe, "cmp")
                        after(pe, stages, "cmp", act_finished, dve_finished)
                        turn_pe([Z[:, 7, :], Z[:, 9, :]], 0)
                        pe.wait_ge(v_ready, 2)
                        att.pe()
                        finish(pe, "att")
                        after(pe, stages, "att", act_finished, dve_finished)
                        products(units, "mix0", operands)
                        finish(pe, "mix0")
                        products(units, "sb", operands)
                        finish(pe, "sb")
                        after(pe, stages, "sb", act_finished, dve_finished)
                        turn_pe([Z[:, 8 + t, :] for t in range(4)], 2)
                        pe.wait_ge(v_ready, 6)
                        for h in range(8):
                            r = slice(HD * (h % 2), HD * (h % 2) + HD)
                            if h:
                                pe.wait_ge(a_ready, NT * h)
                            for j in reversed(range(NT)):
                                pe.matmul(B[j][:, 0:T - j * P], Z[r, 4 + h // 2, j * P:(j + 1) * P], Z[r, h // 2, j * P:T],
                                          start=True, stop=True).then_inc(z_made, 1)
                            for j in reversed(range(NT)):
                                pe.wait_ge(sp_ready, NT * h + NT - j)
                                pe.matmul(B[j][:, 0:T - j * P], neg_tri, soft[:, j, 0:T - j * P], start=False, stop=True,
                                          skip_group_check=True)
                                for i in range(j + 1, NT):
                                    pe.matmul(B[j][:, (i - j) * P:T - j * P], neg_ones, soft[:, i, 0:T - i * P],
                                              start=False, stop=True, skip_group_check=True)
                                pe.matmul(B[j][:, 0:P], identb, later_neg, start=False, stop=True,
                                          skip_group_check=True).then_inc(logit_ready, 1)
                            if h % 2 == 0 and h:
                                pe.wait_ge(stick_taken, h // 2)
                            pe.wait_ge(a_ready, NT * h + NT)
                            for j in range(NT):
                                last = pe.matmul(B[4][r, j * P:T], turned[8 + h // 2][:, j, r], aT[:, j, 0:T - j * P],
                                                 start=(j == 0), stop=True, skip_group_check=True)
                            last.then_inc(stick_done, 1)
                        finish(pe, "stick")
                        after(pe, stages, "stick", act_finished, dve_finished)
                        products(units, "mix1", operands)
                        finish(pe, "mix1")
                        products(units, "gla", operands)
                        finish(pe, "gla")
                        after(pe, stages, "gla", act_finished, dve_finished)
                        pe.wait_ge(alpha_loaded, 16)
                        for run in range(2):
                            if run:
                                pe.wait_ge(o_rstd, 2)
                            pe.matmul(B[5][:, :], alpha[32:48, run * P:(run + 1) * P], small[32:48, :], start=True, stop=True)\
                                .then_inc(alpha_made, 1)
                            turn_pe([Z[:, 4 + 2 * run + a, :] for a in range(2)], 6 + 2 * run)
                            pe.wait_ge(v_ready, 8 + 2 * run)
                            rec.pe(run, Z[:, run, :], Z[:, 2 + run, :])
                            for a in range(2):
                                rec.pe_values(run, a, lambda jt: turned[4 + 2 * run + a][:, jt, :], B[4], slice(0, P))\
                                    .then_inc(o_ready, 1)
                                pe.wait_ge(o_squared, 2 * run + a + 1)
                                pe.wait_ge(alpha_biased, run + 1)
                                if a:
                                    pe.wait_ge(o_rstd, 2 * run + 1)
                                pe.matmul(B[5][:, :], ones, pair[:, 0, :], start=True, stop=True).then_inc(o_summed, 1)
                        finish(pe, "recur")
                        after(pe, stages, "recur", act_finished, dve_finished)
                        products(units, "mix2", operands)
                        finish(pe, "mix2")
                        products(units, "fox", operands)
                        finish(pe, "fox")
                        after(pe, stages, "fox", act_finished, dve_finished)
                        turn_pe([Z[:, 8 + t, :] for t in range(4)], 10)
                        pe.wait_ge(v_ready, 14)
                        pe.wait_ge(decay_summed, 1)
                        fox.pe()
                        finish(pe, "forget")
                        after(pe, stages, "forget", act_finished, dve_finished)
                        products(units, "mix3", operands)
                        finish(pe, "mix3")
                        after(pe, stages, "mix3", dve_finished)
                        products(units, "out", operands)
                        finish(pe, "out")
                        norm_pe(1, pair)
                        finish(pe, "norm1")
                        mlp(units, stages, "pe", midH, midL, None)

                    @block.scalar
                    def _(act):
                        act.wait_ge(vec_loaded, 16)
                        split_hi(units, 0)
                        split_hi(units, 1)
                        norm_act(0, pair, tmp)
                        finish(act, "norm0")

                        def to_Z(scaled):
                            def evacuate(n, t, a):
                                dst = small[:, :] if t == 10 and scaled == () else Z[:, t, :]
                                act.activation(dst, a[:, :], ACT.Copy, scale=SCALE if t in scaled else 1.0)\
                                    .then_inc(acc_free[n % 2], 1)
                            return evacuate

                        def gates(branch):
                            def evacuate(n, t, a):
                                if t % 8 >= 4:
                                    return
                                if t == 8:
                                    act.wait_ge(branch_mixed, NK * branch + 4)
                                col = V2["b_gate"] + NK * branch + 4 * (t // 8) + t % 8
                                act.activation(sig[:, t % 4, :], a[:, :], ACT.Sigmoid, bias=vec[:, col:col + 1])\
                                    .then_inc(acc_free[n % 2], 1)
                            return evacuate

                        act_group(units, "nsa", to_Z(()))
                        finish(act, "nsa")
                        act.wait_ge(gate_turned, 1)
                        act.dma_start(cm.rearrange("p m t c -> p (m t c)"), cmpmask_in.rearrange("p m t c -> p (m t c)"))\
                            .then_inc(mask_loaded, 16)
                        act.activation(gate, B[1][:, :].rearrange("p (t f) -> p t f", t=NT)[:, :, 0:24], ACT.Sigmoid)
                        finish(act, "prep")
                        after(act, stages, "prep", pe_finished, dve_finished)
                        for kv in range(2):
                            for g in range(2):
                                r = slice(HD * g, HD * g + HD)
                                act.dma_start(stack[0:HD, 2 * kv + g, :], Z[r, 4 + kv, :]).then_inc(stacked, 16)
                                act.dma_start(stack[HD:P, 2 * kv + g, 0:T - 1], Z[r, 4 + kv, 1:T]).then_inc(stacked, 16)
                        for kv in range(2):
                            if kv:
                                act.wait_ge(cmp_made, 1)
                            act.dma_start(cw1[:, :, :].rearrange("p j c -> p (j c)"),
                                          cmpw_in[bass.ds(L, 1), kv].rearrange("a p n -> (a p) n")).then_inc(cmp_loaded, 16)
                            act.dma_start(cw2.rearrange("p m c -> p (m c)"),
                                          cmpw2_in[bass.ds(L, 1), kv].rearrange("a p n -> (a p) n")).then_inc(cmp_loaded, 16)
                            act.wait_ge(hidden_ready, kv + 1)
                            act.activation(hid, B[0][:, 0:124].rearrange("p (m c) -> p m c", m=2), ACT.Gelu_apprx_tanh)\
                                .then_inc(hidden_gelu, 1)
                        finish(act, "cmp")
                        after(act, stages, "cmp", pe_finished, dve_finished)
                        turn_act([turned[7], turned[9]], 0)
                        att.act()
                        finish(act, "att")
                        after(act, stages, "att", pe_finished, dve_finished)
                        act_group(units, "mix0", gates(0))
                        finish(act, "mix0")
                        after(act, stages, "mix0", dve_finished)
                        act_group(units, "sb", to_Z((0, 1, 2, 3)))
                        finish(act, "sb")
                        after(act, stages, "sb", pe_finished, dve_finished)
                        turn_act([turned[8 + t] for t in range(4)], 2)
                        for h in range(8):
                            for j in reversed(range(NT)):
                                n = NT * h + NT - 1 - j
                                act.wait_ge(z_made, n + 1)
                                if h:
                                    act.wait_ge(sp_ready, n + 1 - NT)
                                softplus_of_minus(part[:, j, 0:T - j * P], B[j][:, 0:T - j * P]).then_inc(sp_part, 1)
                            if h:
                                act.wait_ge(stick_done, h)
                            for j in reversed(range(NT)):
                                act.wait_ge(logit_ready, NT * h + NT - j)
                                act.activation(aT[:, j, 0:T - j * P], B[j][:, 0:T - j * P], ACT.Exp).then_inc(a_ready, 1)
                        finish(act, "stick")
                        after(act, stages, "stick", pe_finished, dve_finished)
                        act_group(units, "mix1", gates(1))
                        finish(act, "mix1")
                        after(act, stages, "mix1", dve_finished)
                        act_group(units, "gla", to_Z((0, 1)))
                        act.dma_start(alpha[32:48, :], alpha_in[bass.ds(L, 1)].rearrange("a p n -> (a p) n"))\
                            .then_inc(alpha_loaded, 16)
                        finish(act, "gla")
                        after(act, stages, "gla", pe_finished, dve_finished)
                        for run in range(2):
                            turn_act([turned[4 + 2 * run + a] for a in range(2)], 6 + 2 * run)
                            act.wait_ge(alpha_biased, run + 1)
                            softplus_of_minus(tmp[:, :], yt[:, 0, :]).then_inc(softplus_ready, 1)
                            rec.act(run)
                            for a in range(2):
                                i = 2 * run + a
                                act.wait_ge(o_taken, i + 1)
                                act.activation(pair[:, 0, :], yt[:, 0, :], ACT.Square).then_inc(o_squared, 1)
                                act.wait_ge(o_summed, i + 1)
                                link(act, act.activation(tmp[:, :], B[5][:, :], ACT.Ln, bias=EPS, scale=1.0 / P))
                                act.activation(tmp[:, :], tmp[:, :], ACT.Exp, scale=-0.5).then_inc(o_rstd, 1)
                                act.activation(pair[:, 1, :], Z[:, 8 + i, :], ACT.Sigmoid).then_inc(gate_ready, 1)
                        finish(act, "recur")
                        after(act, stages, "recur", pe_finished, dve_finished)
                        act_group(units, "mix2", gates(2))
                        finish(act, "mix2")
                        after(act, stages, "mix2", dve_finished)
                        act_group(units, "fox", to_Z((99,)))
                        finish(act, "fox")
                        after(act, stages, "fox", pe_finished, dve_finished)
                        act.wait_ge(alpha_biased, 3)
                        softplus_of_minus(tmp[64:96, :], yt[64:96, 0, :]).then_inc(softplus_ready, 1)
                        turn_act([turned[8 + t] for t in range(4)], 10)
                        fox.act()
                        finish(act, "forget")
                        after(act, stages, "forget", pe_finished, dve_finished)
                        act_group(units, "mix3", gates(3))
                        finish(act, "mix3")
                        act_group(units, "out")
                        finish(act, "out")
                        after(act, stages, "out", dve_finished)
                        norm_act(1, pair, tmp)
                        finish(act, "norm1")
                        mlp(units, stages, "act", midH, midL, pair)

                    @block.vector
                    def _(dve):
                        dve.wait_ge(vec_loaded, 16)
                        norm_dve(0, V2["norm_mix"], tmp, yt)
                        finish(dve, "norm0")
                        finish(dve, "nsa")
                        after(dve, stages, "nsa", act_finished)
                        for i, t in enumerate((0, 1, 2, 3, 6, 8)):
                            dve.wait_ge(z_rotated, i + 1)
                            link(dve, dve.tensor_tensor(yt[:, 0, :], B[0][:, :], sinT[:, :], ALU.mult))
                            link(dve, dve.tensor_tensor(yt[:, 1, :], Z[:, t, :], cosT[:, :], ALU.mult))
                            dve.tensor_tensor(Z[:, t, :], yt[:, 0, :], yt[:, 1, :], ALU.add).then_inc(z_done, 1)
                        finish(dve, "prep")
                        after(dve, stages, "prep", pe_finished, act_finished)
                        dve.wait_ge(mask_loaded, 16)
                        for kv in range(2):
                            dve.wait_ge(stacked, 128)
                            if kv:
                                dve.wait_ge(hidden_ready, 1)
                            for j in range(16):
                                col = V2["pe_v" if kv else "pe_k"] + j
                                last = dve.tensor_scalar(blocks_sb[:, j, :].rearrange("p (g c) -> p g c", g=2),
                                                         stack[:, 2 * kv:2 * kv + 2, 2 * j:2 * j + 481:16],
                                                         vec[:, col:col + 1], None, ALU.add)
                            last.then_inc(blocks_ready, 1)
                            dve.wait_ge(cmp_made, kv + 1)
                            if kv == 0:
                                ins = dve.tensor_copy(kraw, B[1][:, 0:31])
                                ins.then_inc(cmp_taken, 1)
                                dve.wait_ge(cmp_taken, 1)
                                dve.wait_ge(cmp_turned, 1)
                                dve.tensor_tensor(kt2[:, 0:31], kraw, cosT[:, 31:T:16], ALU.mult)
                                link(dve, dve.tensor_tensor(kt2[:, 31:62], B[3][:, 0:31], sinT[:, 31:T:16], ALU.mult))
                                link(dve, dve.tensor_tensor(kc, kt2[:, 0:31], kt2[:, 31:62], ALU.add))
                            else:
                                dve.tensor_copy(vc, B[2][0:31, 0:P])
                        finish(dve, "cmp")
                        after(dve, stages, "cmp", pe_finished, act_finished)
                        att.dve()
                        finish(dve, "att")
                        after(dve, stages, "att", pe_finished, act_finished)

                        def mix(branch):
                            def evacuate(n, t, a):
                                if t % 8 < 4:
                                    return
                                f = 4 * (t // 8) + t % 4
                                ng = units_first(units, f"mix{branch}") + 8 * (t // 8) + t % 4
                                dve.wait_ge(acc_free[ng % 2], ng // 2 + 1)
                                if branch == 0:
                                    dve.tensor_tensor(mixed[:, f, :], a[:, :], sig[:, t % 4, :], ALU.mult)\
                                        .then_inc(acc_free[n % 2], 1)
                                    dve.wait_ge(acc_free[n % 2], n // 2 + 1)
                                    dve.drain().then_inc(branch_mixed, 1)
                                else:
                                    dve.tensor_tensor(yt[:, t % 2, :], a[:, :], sig[:, t % 4, :], ALU.mult)\
                                        .then_inc(acc_free[n % 2], 1)
                                    dve.wait_ge(acc_free[n % 2], n // 2 + 1)
                                    dve.tensor_tensor(mixed[:, f, :], mixed[:, f, :], yt[:, t % 2, :], ALU.add)\
                                        .then_inc(branch_mixed, 1)
                            dve_group(units, f"mix{branch}", evacuate)
                            if branch < 3:
                                finish(dve, f"mix{branch}")

                        mix(0)
                        finish(dve, "sb")
                        after(dve, stages, "sb", pe_finished, act_finished)
                        for h in range(8):
                            for j in reversed(range(NT)):
                                n = NT * h + NT - 1 - j
                                w = T - j * P
                                dve.wait_ge(sp_part, n + 1)
                                if h:
                                    dve.wait_ge(logit_ready, NT * h)
                                if True:
                                    link(dve, dve.scalar_tensor_tensor(soft[:, j, 0:w], B[j][:, 0:w], 0.0, part[:, j, 0:w],
                                                                       ALU.max, ALU.add))
                                dve.tensor_tensor(soft[:, j, 0:P], soft[:, j, 0:P], later_one, ALU.mult).then_inc(sp_ready, 1)
                            if h % 2:
                                dve.wait_ge(stick_done, h + 1)
                                ins = dve.tensor_copy(yt[:, 0, :], B[4][:, :])
                                ins.then_inc(stick_taken, 1)
                                dve.wait_ge(stick_taken, h // 2 + 1)
                                split_dve(yH[:, h // 2, :], yL[:, h // 2, :], yt[:, 0, :])
                        finish(dve, "stick")
                        after(dve, stages, "stick", pe_finished, act_finished)
                        mix(1)
                        finish(dve, "gla")
                        after(dve, stages, "gla", pe_finished, act_finished)
                        dve.memset(BB[:, :, 0:1], 0.0)
                        dve.memset(SS[:, :, :, :], 0.0)
                        for run in range(2):
                            col = V2["b_alpha"] + run
                            dve.wait_ge(alpha_made, run + 1)
                            dve.tensor_scalar(yt[:, 0, :], B[5][:, :], vec[:, col:col + 1], None, ALU.add)\
                                .then_inc(alpha_biased, 1)
                            dve.wait_ge(softplus_ready, run + 1)
                            link(dve, dve.scalar_tensor_tensor(yt[:, 1, :], yt[:, 0, :], 0.0, tmp[:, :], ALU.min, ALU.subtract))
                            link(dve, dve.tensor_scalar(yt[:, 1, :], yt[:, 1, :], 1.0 / 16, None, ALU.mult))
                            link(dve, dve.tensor_tensor_scan(BB[:, 0, 1:T + 1], ones[:, 0:1].to_broadcast([P, T]),
                                                             yt[:, 1, :], 0.0, ALU.mult, ALU.add))
                            rec.dve(run, Z[:, run, :], [Z[:, 2 + run, :]], None)
                            for a in range(2):
                                i = 2 * run + a
                                dve.wait_ge(o_ready, i + 1)
                                dve.tensor_copy(yt[:, 0, :], B[4][:, :]).then_inc(o_taken, 1)
                                dve.wait_ge(gate_ready, i + 1)
                                link(dve, dve.tensor_tensor(pair[:, 1, :], pair[:, 1, :], Z[:, 8 + i, :], ALU.mult))
                                dve.wait_ge(o_rstd, i + 1)
                                col = V2["gla_norm"]
                                link(dve, dve.scalar_tensor_tensor(yt[:, 0, :], yt[:, 0, :], vec[:, col:col + 1], tmp[:, :],
                                                                   ALU.mult, ALU.mult))
                                link(dve, dve.tensor_tensor(yt[:, 0, :], yt[:, 0, :], pair[:, 1, :], ALU.mult))
                                split_dve(yH[:, i, :], yL[:, i, :], yt[:, 0, :])
                        finish(dve, "recur")
                        after(dve, stages, "recur", pe_finished, act_finished)
                        mix(2)
                        finish(dve, "fox")
                        after(dve, stages, "fox", pe_finished, act_finished)
                        r = slice(64, 96)
                        col = V2["fox_b"]
                        dve.tensor_scalar(yt[r, 0, :], small[r, :], vec[r, col:col + 1], None, ALU.add)\
                            .then_inc(alpha_biased, 1)
                        dve.wait_ge(softplus_ready, 3)
                        link(dve, dve.scalar_tensor_tensor(yt[r, 1, :], yt[r, 0, :], 0.0, tmp[r, :], ALU.min, ALU.subtract))
                        link(dve, dve.tensor_tensor_scan(yt[r, 0, :], ones[r, 0:1].to_broadcast([32, T]), yt[r, 1, :], 0.0,
                                                         ALU.mult, ALU.add))
                        dve.tensor_scalar(small[r, :], yt[r, 0, :], -1.0 / SCALE, None, ALU.mult).then_inc(decay_summed, 1)
                        fox.dve()
                        finish(dve, "forget")
                        after(dve, stages, "forget", pe_finished, act_finished)
                        mix(3)
                        for k in range(NK):
                            split_dve(hH[:, k, :], hL[:, k, :], mixed[:, k, :])
                        finish(dve, "mix3")
                        dve_group(units, "out", add_to_x)
                        finish(dve, "out")
                        norm_dve(1, V2["norm_ff"], tmp, yt)
                        finish(dve, "norm1")
                        mlp(units, stages, "dve", midH, midL, pair)
            clear()

        def store_result(gcol=None):
            new_layer()
            scope = ExitStack()
            with scope:
                tmp = sb("f_tmp", [P, T], F32, scope)
                pair = sb("f_pair", [P, 2, T], F32, scope)
                y = sb("f_y", [P, NK, T], F32, scope)
                x_tok = sb("f_tok", [P, NT, D], F32, scope)
                with nc.Block() as block:
                    @block.tensor
                    def _(pe):
                        norm_pe(0, pair)
                        for t in range(NT):
                            for half in range(2):
                                n = 2 * t + half
                                if n == 0:
                                    pe.wait_ge(key_ready, 1)
                                if n >= 2:
                                    pe.wait_ge(v_ready, n - 1)
                                for k in range(4):
                                    last = pe.transpose(B[1 + n % 2][:, k * P:(k + 1) * P],
                                                        y[:, 4 * half + k, t * P:(t + 1) * P], ident)
                                last.then_inc(v_turned, 1)

                    @block.scalar
                    def _(act):
                        norm_act(0, pair, tmp)
                        for n in range(2 * NT):
                            act.wait_ge(v_turned, n + 1)
                            act.activation(x_tok[:, n // 2, (n % 2) * T:(n % 2) * T + T], B[1 + n % 2][:, :], ACT.Copy)\
                                .then_inc(v_ready, 1)

                    @block.vector
                    def _(dve):
                        dve.wait_ge(rstd_ready, 1)
                        for k in range(NK):
                            g = V2["final"] + k
                            last = dve.scalar_tensor_tensor(y[:, k, :], xT[:, k, :], vec[:, g:g + 1], tmp[:, :],
                                                            ALU.mult, ALU.mult)
                        last.then_inc(key_ready, 1)

                    @block.sync
                    def _(sp):
                        for t in range(NT):
                            sp.wait_ge(v_ready, 2 * t + 2)
                            sp.dma_start(out[0, t * P:(t + 1) * P, :], x_tok[:, t, :]).then_inc(stored, 16)
                        sp.wait_ge(stored, 16 * NT)
            clear()

        def probe(i):
            with nc.Block() as block:
                @block.sync
                def _(sp):
                    sp.dma_start(probes[i], xT[:, :, :]).then_inc(stored, 16)
                    sp.wait_ge(stored, 16)
            clear()

        load_start()
        if 1 in blocks:
            with nc.Fori(0, layers) as L:
                first_layer(L)
            if probes is not None:
                probe(0)
        if 2 in blocks:
            start_second()
            with nc.Fori(0, layers) as L:
                second_layer(L)
        if 2 in blocks:
            store_result()


def constants():
    f = np.float32
    i = np.arange(P)
    row, col = i[:, None], i[None, :]
    c = {"ident": np.eye(P), "ones": np.ones((P, P)), "pair_ones": (row // HD == col // HD),
         "neg_tri": -(row >= col).astype(f), "neg_ones": -np.ones((P, P)),
         "causal_neg": np.where(col > row, NEG, 0), "window_neg": np.where(col <= row, NEG, 0),
         "later_neg": np.where(col <= row, NEG, 0), "later_one": col > row}
    for name, half, width, n in (("rot1", 16, 32, HD), ("rot2", 8, 16, 16)):
        R = np.zeros((P, P), f)
        for base in range(0, P, HD):
            for start in range(0, n, width):
                for j in range(half):
                    a, b = base + start + j, base + start + half + j
                    R[b, a], R[a, b] = -1, 1
        c[name] = R
    consts = np.stack([np.asarray(c[k], f) for k in CONSTS], axis=1)
    m = []
    for h in LEVELS:
        m.append((row // (2 * h) == col // (2 * h)) & (row % (2 * h) < h) & (col % (2 * h) >= h))
    m += [x.T for x in m] + [np.eye(P, dtype=bool)]
    t = np.arange(T)
    axis = HD // 2
    inv = (10000.0 ** (-np.arange(0, axis, 2, dtype=f) / axis)).astype(f)
    ang = np.stack([(t // 64).astype(f)[:, None] * inv, (t % 64).astype(f)[:, None] * inv])
    rope = np.zeros((2, P, T), f)
    for p in range(P):
        d = p % HD
        a = ang[d // axis][:, d % (axis // 2)]
        rope[0, p], rope[1, p] = np.cos(a), np.sin(a)
    end = np.arange(31) * 16 + 31
    tok = t.reshape(NT, P).T
    keep = (end[None, None, :] <= tok[:, :, None])
    cmpmask = np.stack([np.where(keep, 0, NEG), keep], axis=1).astype(f)
    sel = np.zeros((32, 8, P), f)
    for h in range(8):
        sel[h, h, :] = 1
    freq = np.zeros((P, 2), f)
    inv2 = (500000.0 ** (-np.arange(0, 16, 2, dtype=f) / 16)).astype(f)
    for p in range(P):
        if p % HD < 16:
            freq[p, 0] = inv2[p % HD % 8]
    return (consts, np.stack(m, axis=1).astype(f), rope, cmpmask, sel, freq)


def columns(a):
    return a.reshape(a.shape[0], -1, P).transpose(0, 2, 1)


def tiles(w, nk, cols):
    return w.reshape(w.shape[0], nk, P, cols).transpose(0, 2, 1, 3).reshape(w.shape[0], P, nk * cols)


def mlp_units(up, down):
    u = []
    for b in range(FB):
        u += [tiles(up[:, :, b * D + j * 256:b * D + j * 256 + 256], NK, 256) for j in range(4)]
        u += [tiles(down[:, b * D:(b + 1) * D, j * 256:j * 256 + 256], NK, 256) for j in range(4)]
    return u


def head_order(w):
    return w.reshape(w.shape[0], w.shape[1], 2, 4, HD).transpose(0, 1, 3, 2, 4).reshape(w.shape)


def stream1(w_in, w_out, up, down):
    w = np.concatenate([head_order(w_in[:, :, 0:512]), w_in[:, :, 512:]], axis=2)
    units = [tiles(w[:, :, j * 256:(j + 1) * 256], NK, 256) for j in range(10)]
    units += [tiles(w_out[:, :, j * 256:(j + 1) * 256], NK, 256) for j in range(4)]
    return np.stack(units + mlp_units(up, down), axis=1)


def stream2(w_in, w_branch, w_out, up, down):
    q, rest = head_order(w_in[:, :, 0:512]), w_in[:, :, 512:1280]
    g, sb_w, gla, lowrank, gla_g = (w_in[:, :, a:b] for a, b in ((1280, 1304), (1304, 2840), (2840, 3864), (3864, 3880),
                                                              (3880, 4392)))
    fox, fox_f, gates = w_in[:, :, 4392:5928], w_in[:, :, 5928:5936], w_in[:, :, 5936:]
    z = lambda n: np.zeros(w_in.shape[:2] + (n,), w_in.dtype)
    small = np.concatenate([g, z(8), lowrank, z(16), fox_f, z(56)], axis=2)
    cut = lambda w: [tiles(w[:, :, j * 256:(j + 1) * 256], NK, 256) for j in range(w.shape[2] // 256)]
    one = np.concatenate([tiles(small, NK, P), np.zeros((w_in.shape[0], P, UNIT // 2), w_in.dtype)], axis=2)
    units = cut(q) + cut(rest) + [one]
    groups = [[], cut(sb_w), cut(np.concatenate([gla, gla_g], axis=2)), cut(fox)]
    for n in range(4):
        units += groups[n]
        for half in range(2):
            c = n * D + half * 512
            units += cut(gates[:, :, c:c + 512]) + [tiles(w_branch[:, n, :, half * 512:half * 512 + 512], 4, 512)]
    return np.stack(units + cut(w_out) + mlp_units(up, down), axis=1)


def kernel(x, w_in, w_out, norm_mix, norm_mlp, q_norm, k_norm, hgrn_lb_fwd, hgrn_lb_bwd, hgrn_norm, conv_w, conv_b,
           conv_ln_g, conv_ln_b, w_mlp_in, w_mlp_out, positions_2, norm_mix_2, w_in_2, b_gate_2, nsa_cmp_pos_k_2,
           nsa_cmp_pos_v_2, nsa_cmp_wk1_2, nsa_cmp_wk2_2, nsa_cmp_wv1_2, nsa_cmp_wv2_2, gla_w_alpha_2, gla_b_alpha_2,
           gla_norm_2, fox_b_f_2, w_branch_2, w_out_2, norm_ff_2, w_ff1_2, w_ff2_2, norm_final_2):
    import concourse.bacc as bacc
    from concourse.bass_utils import run_bass_kernel_spmd

    a = np.asarray
    both = lambda v: np.concatenate([a(v), a(v)], axis=1)
    lb_f = np.broadcast_to(a(hgrn_lb_fwd).reshape(1, 1, -1), (DEPTH, 1, 2 * 256)).reshape(DEPTH, -1)
    lb_b = np.broadcast_to(a(hgrn_lb_bwd).reshape(1, 1, -1), (DEPTH, 1, 2 * 256)).reshape(DEPTH, -1)
    vec1 = np.concatenate([columns(v) for v in (
        a(norm_mix), a(norm_mlp), both(q_norm), both(k_norm), lb_f, lb_b, a(hgrn_norm), a(conv_b), a(conv_ln_g),
        a(conv_ln_b), a(conv_w).reshape(DEPTH, -1))], axis=2)
    fox_b = np.zeros((DEPTH, P), np.float32)
    fox_b[:, 64:72] = a(fox_b_f_2)
    final = np.broadcast_to(a(norm_final_2)[None], (DEPTH, D))
    vec2 = np.concatenate([columns(v) for v in (
        a(norm_mix_2), a(norm_ff_2), a(b_gate_2), a(nsa_cmp_pos_k_2).reshape(DEPTH, -1),
        a(nsa_cmp_pos_v_2).reshape(DEPTH, -1), a(gla_b_alpha_2), a(gla_norm_2), fox_b, final)], axis=2)
    consts, masks, rope, cmpmask, sel, freq = constants()
    cmpw = np.stack([tiles(a(w), 16, 256) for w in (nsa_cmp_wk1_2, nsa_cmp_wv1_2)], axis=1)
    cmpw2 = np.stack([tiles(a(w), 2, HD) for w in (nsa_cmp_wk2_2, nsa_cmp_wv2_2)], axis=1)
    arrays = {
        "x": a(x), "consts": consts, "masks": masks, "rope": rope, "cmpmask": cmpmask, "sel": sel, "freq": freq,
        "vec1": vec1, "vec2": vec2,
        "stream1": stream1(a(w_in), a(w_out), a(w_mlp_in), a(w_mlp_out)),
        "stream2": stream2(a(w_in_2), a(w_branch_2), a(w_out_2), a(w_ff1_2), a(w_ff2_2)),
        "positions": a(positions_2), "cmpw": cmpw, "cmpw2": cmpw2, "alpha": a(gla_w_alpha_2),
    }
    arrays = {k: np.ascontiguousarray(v) for k, v in arrays.items()}
    nc = bacc.Bacc("TRN2", target_bir_lowering=False, num_devices=1)
    t = {k: nc.dram_tensor(f"in_{k}", v.shape, mybir.dt.from_np(v.dtype), kind="ExternalInput").ap()
         for k, v in arrays.items()}
    out = nc.dram_tensor("out", (1, T, D), F32, kind="ExternalOutput").ap()
    program(nc, t, out)
    r = run_bass_kernel_spmd(nc, [{f"in_{k}": v for k, v in arrays.items()}], core_ids=[0])
    return r.results[0]["out"]
```

```python
from contextlib import ExitStack

import numpy as np

import concourse.bass as bass
from concourse import mybir

F32 = mybir.dt.float32
F32R = mybir.dt.float32r
BF16 = mybir.dt.bfloat16
I32 = mybir.dt.int32
U8 = mybir.dt.uint8
ALU = mybir.AluOpType
ACT = mybir.ActivationFunctionType
AX_X = mybir.AxisListType.X

P = 128
T = 512
NT = T // P
D = 1024
NK = D // P
DEPTH = 2
HD = 64
EPS = 1e-6
UNIT = 1024
FF = 4 * D
CONV_AT = 12
FB = FF // D
SCALE = float(HD) ** -0.5
NEG = -1e30

CONSTS = ["ident", "ones", "pair_ones", "rot1", "rot2", "neg_tri", "neg_ones",
          "causal_neg", "window_neg", "later_neg", "later_one"]
LEVELS = [64, 32, 16, 8, 4, 2, 1]
V1 = {}
_at = 0
for _name, _n in (("norm_mix", 8), ("norm_mlp", 8), ("q_norm", 1), ("k_norm", 1), ("lb_f0", 2), ("lb_f1", 2),
                  ("lb_b0", 2), ("lb_b1", 2), ("hgrn_norm", 2), ("conv_b", 2), ("ln_g", 2), ("ln_b", 2),
                  ("conv_w", 62)):
    V1[_name] = _at
    _at += _n
NV1 = _at
V2 = {}
_at = 0
for _name, _n in (("norm_mix", 8), ("norm_ff", 8), ("b_gate", 32), ("pe_k", 16), ("pe_v", 16), ("b_alpha", 2),
                  ("gla_norm", 1), ("fox_b", 1), ("final", 8)):
    V2[_name] = _at
    _at += _n
NV2 = _at


def plan_units(groups):
    units, first_unit, first_tile, n = [], {}, {}, 0
    for group, operand, shapes in groups:
        first_unit[group], first_tile[group] = len(units), n
        for nk, ntile in shapes:
            units.append((group, nk, ntile, operand, n))
            n += ntile
    return units, first_unit, first_tile


FF_GROUPS = [g for b in range(FB) for g in ((f"up{b}", "h", [(8, 1)] * 8), (f"down{b}", "mid", [(8, 1)] * 8))]
GROUPS1 = [("att_in", "h", [(8, 1)] * 6), ("rest_in", "h", [(8, 1)] * 14), ("out", "h", [(8, 1)] * 8)] + FF_GROUPS
MIX = ([(8, 1)] * 4 + [(4, 2)] * 2) * 2
GROUPS2 = [("nsa_in", "h", [(8, 1)] * 11), ("stick_in", "h", [(8, 1)] * 12), ("mix0", "h", MIX),
           ("gla_in", "h", [(8, 1)] * 12), ("mix1", "h", MIX), ("fox_in", "h", [(8, 1)] * 12), ("mix2", "h", MIX),
           ("gate3", "h", [(8, 1)] * 8), ("mix3", "h", [(4, 2)] * 4), ("out", "h", [(8, 1)] * 8)] + FF_GROUPS
STAGES1 = ["start", "att_in", "prep", "att", "hgrn", "conv", "out"] + [g[0] for g in FF_GROUPS]
STAGES2 = ["start", "nsa_in", "prep", "cmp", "att", "mix0", "stick", "mix1", "recur", "mix2", "forget", "mix3",
           "out"] + [g[0] for g in FF_GROUPS]


def ranges(kind, qt):
    return {"full": (0, NT), "causal": (0, qt + 1), "window": (max(0, qt - 2), qt + 1), "cmp": (0, 1),
            "fox": (0, qt + 1)}[kind]


def program(nc, given, out, probes=None, blocks=(1, 2), layers=DEPTH):
    x_in, consts_in, masks_in, rope_in, cmpmask_in, sel_in, freq_in = (
        given[n] for n in ("x", "consts", "masks", "rope", "cmpmask", "sel", "freq"))
    vec1_in, vec2_in, w1_in, w2_in, pos_in, cmpw_in, cmpw2_in, alpha_in = (
        given[n] for n in ("vec1", "vec2", "stream1", "stream2", "positions", "cmpw", "cmpw2", "alpha"))
    ctx = ExitStack()
    with ctx:
        def sb(name, shape, dt=F32, scope=ctx):
            return scope.enter_context(nc.sbuf_tensor(name, shape, dt))

        sems = []

        def sem(name):
            s = ctx.enter_context(nc.semaphore(name))
            sems.append(s)
            return s

        xT = sb("xT", [P, NK, T])
        hH = sb("hH", [P, NK, T], F32R)
        hL = sb("hL", [P, NK, T], F32R)
        rstd = sb("rstd", [P, T])
        w_raw = sb("w_raw", [P, 2, UNIT])
        w_hi = sb("w_hi", [P, 2, UNIT], F32R)
        w_lo = sb("w_lo", [P, 2, UNIT], F32R)
        C = sb("C", [P, len(CONSTS), P])
        ident, ones, pair_ones, rot1, rot2, neg_tri, neg_ones = (C[:, i, :] for i in range(7))
        later_one = C[:, 10, :]
        Cb = sb("Cb", [P, 4, P], BF16)
        identb, causal_neg, window_neg, later_neg = (Cb[:, i, :] for i in range(4))
        masks = sb("masks", [P, 2 * len(LEVELS) + 1, P], U8)
        cosT = sb("cosT", [P, T])
        sinT = sb("sinT", [P, T])
        vec = sb("vec", [P, max(NV1, NV2)])
        acc = [ctx.enter_context(nc.psum_tensor(f"acc{i}", [P, T], F32)) for i in range(2)]
        B = [ctx.enter_context(nc.psum_tensor(f"bank{i}", [P, T], F32)) for i in range(6)]

        pe_finished, act_finished, dve_finished = sem("pe_finished"), sem("act_finished"), sem("dve_finished")
        dve_chain, act_chain = sem("dve_chain"), sem("act_chain")
        consts_loaded, vec_loaded, x_loaded, stored = sem("consts_loaded"), sem("vec_loaded"), sem("x_loaded"), sem("stored")
        w_loaded = [sem(f"w_loaded{i}") for i in range(2)]
        hi_split, lo_split = sem("hi_split"), sem("lo_split")
        acc_ready = [sem(f"acc_ready{i}") for i in range(2)]
        acc_free = [sem(f"acc_free{i}") for i in range(2)]
        sq_ready, sq_summed, rstd_ready = sem("sq_ready"), sem("sq_summed"), sem("rstd_ready")
        x_scaled, h_split, mid_ready = sem("x_scaled"), sem("h_split"), sem("mid_ready")
        attention_sems = [[sem(f"{n}_{i}") for n in ("s_ready", "max_ready", "exp_done", "p_normed", "pt_turned", "pt_ready",
                                                     "pv_done", "o_free", "bias_turned", "bias_ready")] for i in range(2)]
        v_turned, v_ready = sem("v_turned"), sem("v_ready")
        softplus_ready, rate_ready, key_ready, decay_summed = (sem("softplus_ready"), sem("rate_ready"), sem("key_ready"),
                                                               sem("decay_summed"))
        gap_ready, decay_ready, terms_ready, level_scored, level_kept = (
            sem("gap_ready"), sem("decay_ready"), sem("terms_ready"), sem("level_scored"), sem("level_kept"))
        gate_used, gate_scaled, gate_opened = sem("gate_used"), sem("gate_scaled"), sem("gate_opened")
        o_ready, o_taken, o_squared, o_summed, o_rstd, gate_ready = (
            sem("o_ready"), sem("o_taken"), sem("o_squared"), sem("o_summed"), sem("o_rstd"), sem("gate_ready"))
        z_squared, z_summed, z_rstd, z_normed, z_rotated, z_done = (
            sem("z_squared"), sem("z_summed"), sem("z_rstd"), sem("z_normed"), sem("z_rotated"), sem("z_done"))
        conv_in, conv_tapped, conv_summed, conv_mean, conv_squared, conv_var, conv_rstd, conv_gate, conv_pre = (
            sem("conv_in"), sem("conv_tapped"), sem("conv_summed"), sem("conv_mean"), sem("conv_squared"), sem("conv_var"),
            sem("conv_rstd"), sem("conv_gate"), sem("conv_pre"))

        counts = {}

        def link(eng, ins):
            s = dve_chain if eng is nc.vector else act_chain
            key = "dve" if eng is nc.vector else "act"
            counts[key] += 1
            ins.then_inc(s, 1)
            eng.wait_ge(s, counts[key])

        def new_layer():
            counts.update(dve=0, act=0)

        def clear():
            nc.all_engine_barrier()
            nums = sorted(s.num for s in sems)
            assert nums == list(range(nums[0], nums[0] + len(nums)))
            nc.sync.sem_clear(range(nums[0], nums[-1] + 1))
            nc.all_engine_barrier()

        pe, act, dve, pool, sp = nc.tensor, nc.scalar, nc.vector, nc.gpsimd, nc.sync

        LOG_EXP = "natural_log_exp_and_others"

        def split_hi(units, u):
            if u >= len(units):
                return
            _, nk, ntile, _, _ = units[u]
            w = nk * ntile * P
            act.wait_ge(w_loaded[u % 2], 16 * (u // 2 + 1))
            if u >= 2:
                n = units[u - 2][4] + units[u - 2][2] - 1
                act.wait_ge(acc_ready[n % 2], n // 2 + 1)
            act.activation(w_hi[:, u % 2, 0:w], w_raw[:, u % 2, 0:w], ACT.Copy).then_inc(hi_split, 1)

        def load_weights(units, source, L):
            for u, (_, nk, ntile, _, _) in enumerate(units):
                w = nk * ntile * P
                if u >= 2:
                    sp.wait_ge(lo_split, u - 1)
                sp.dma_start(w_raw[:, u % 2, 0:w], source[bass.ds(L, 1), u, :, 0:w].rearrange("a p n -> (a p) n"))\
                    .then_inc(w_loaded[u % 2], 16)

        def split_lo(units):
            for u, (_, nk, ntile, _, _) in enumerate(units):
                w = nk * ntile * P
                pool.wait_ge(hi_split, u + 1)
                pool.tensor_tensor(w_lo[:, u % 2, 0:w], w_raw[:, u % 2, 0:w], w_hi[:, u % 2, 0:w], ALU.subtract)\
                    .then_inc(lo_split, 1)

        class Group:

            def __init__(self, units, group, operands=None):
                self.units, self.operands = units, operands or (lambda nk: (hH, hL))
                self.tiles = [(u, t, x[4] + t) for u, x in enumerate(units) if x[0] == group for t in range(x[2])]
                self.first = self.tiles[0][2]
                self.k = 0

            def products(self, count=None, ready=None, sums=None):
                for _ in range(len(self.tiles) if count is None else min(count, len(self.tiles))):
                    self.part(NK, ready, sums)
                    ready = sums = None

            def part(self, count, ready=None, sums=None):
                if self.tiles:
                    u, t, n = self.tiles[0]
                    _, nk, ntile, _, _ = self.units[u]
                    H, Lo = self.operands(nk)
                    if self.k == 0:
                        pe.wait_ge(lo_split, u + 1)
                        if n >= 2:
                            pe.wait_ge(acc_free[n % 2], n // 2)
                    for k in range(self.k, min(nk, self.k + count)):
                        if ready:
                            ready(k)
                        c = k * ntile * P + t * P
                        wh, wl = w_hi[:, u % 2, c:c + P], w_lo[:, u % 2, c:c + P]
                        pe.matmul(acc[n % 2][:, :], wh, H[:, k, :], start=(k == 0), stop=False)
                        pe.matmul(acc[n % 2][:, :], wl, H[:, k, :], start=False, stop=False)
                        last = pe.matmul(acc[n % 2][:, :], wh, Lo[:, k, :], start=False, stop=(k == nk - 1))
                        if sums:
                            sums(k)
                    self.k = k + 1
                    if self.k == nk:
                        last.then_inc(acc_ready[n % 2], 1)
                        self.tiles.pop(0)
                        self.k = 0

            def evacuate(self, take, count=None):
                for _ in range(len(self.tiles) if count is None else min(count, len(self.tiles))):
                    _, _, n = self.tiles.pop(0)
                    dve.wait_ge(acc_ready[n % 2], n // 2 + 1)
                    take(n - self.first, acc[n % 2], acc_free[n % 2], n // 2 + 1)

            def split_ahead(self, count=None):
                for _ in range(len(self.tiles) if count is None else min(count, len(self.tiles))):
                    u, t, _ = self.tiles.pop(0)
                    if t == self.units[u][2] - 1:
                        split_hi(self.units, u + 2)

        def first_tile_of(units, group):
            return next(x[4] for x in units if x[0] == group)

        def add_to_x(i, a, free, value):
            dve.tensor_tensor(xT[:, i, :], a[:, :], xT[:, i, :], ALU.add).then_inc(free, 1)

        def scale_act(r, gcol, y, sq, before=None):
            act.preload_act_table_set(LOG_EXP)
            for k in range(NK):
                i = NK * r + k
                g = vec[:, gcol + k:gcol + k + 1]
                if before:
                    before(k)
                if i >= 2:
                    act.wait_ge(h_split, i - 1)
                act.activation(y[:, k % 2, :], xT[:, k, :], ACT.Copy, scale=g).then_inc(x_scaled, 1)
                if i >= 2:
                    act.wait_ge(sq_summed, i - 1)
                act.activation(sq[:, k % 2, :], xT[:, k, :], ACT.Square).then_inc(sq_ready, 1)
            act.wait_ge(sq_summed, NK * r + NK)
            link(act, act.activation(rstd[:, :], B[0][:, :], ACT.Ln, bias=EPS, scale=1.0 / D))
            act.activation(rstd[:, :], rstd[:, :], ACT.Exp, scale=-0.5).then_inc(rstd_ready, 1)

        def scale_dve(r, y, hi, lo, k):
            dve.wait_ge(x_scaled, NK * r + k + 1)
            link(dve, dve.tensor_copy(hi[:, k, :], y[:, k % 2, :]))
            dve.tensor_tensor(lo[:, k, :], y[:, k % 2, :], hi[:, k, :], ALU.subtract).then_inc(h_split, 1)

        def out_pe(units, sq):
            out_tiles = Group(units, "out")
            for k in range(NK):
                out_tiles.products(1)
                if k:
                    square_sums(1, sq)(k - 1)
            finish(pe, "out")

        def out_act(units, gcol, y, sq):
            ahead = Group(units, "out")
            first = ahead.first

            def added(k):
                n = first + k
                ahead.split_ahead(1)
                act.wait_ge(acc_free[n % 2], n // 2 + 1)
            scale_act(1, gcol, y, sq, added)
            finish(act, "out")

        def out_dve(units, y, hi, lo):
            out_tiles = Group(units, "out")
            for k in range(NK):
                out_tiles.evacuate(add_to_x, 1)
                if k:
                    scale_dve(1, y, hi, lo, k - 1)
            scale_dve(1, y, hi, lo, NK - 1)
            finish(dve, "out")

        def h_ready(r):
            return lambda k: pe.wait_ge(h_split, NK * r + k + 1)

        def square_sums(r, sq):
            def sums(k):
                pe.wait_ge(sq_ready, NK * r + k + 1)
                pe.matmul(B[0][:, :], ones, sq[:, k % 2, :], start=(k == 0), stop=(k == NK - 1)).then_inc(sq_summed, 1)
            return sums

        def split_dve(hi, lo, src):
            link(dve, dve.tensor_copy(hi, src))
            link(dve, dve.tensor_tensor(lo, src, hi, ALU.subtract))

        def mlp_pe(units, H2, L2, midH, midL, sq):
            for b in range(FB):
                Group(units, f"up{b}", lambda nk: (H2, L2)).products(
                    ready=h_ready(1) if b == 0 else None,
                    sums=(lambda k: square_sums(1, sq)(NK - 1) if k == NK - 2 else None) if b == 0 else None)
                finish(pe, f"up{b}")
                Group(units, f"down{b}", lambda nk: (midH, midL)).products(
                    ready=lambda k, b=b: pe.wait_ge(mid_ready, NK * b + k + 1))
                finish(pe, f"down{b}")

        def mlp_act(units):
            for b in range(FB):
                Group(units, f"up{b}").split_ahead()
                Group(units, f"down{b}").split_ahead()

        def mlp_dve(units, stages, midH, midL, r_sb):
            dve.wait_ge(rstd_ready, 2)

            def hidden(i, a, free, value):
                r = r_sb[:, i % 2, :]
                dve.scalar_tensor_tensor(r, a[:, :], 0.0, rstd[:, :], ALU.max, ALU.mult).then_inc(free, 1)
                dve.wait_ge(free, value)
                link(dve, dve.tensor_tensor(r, r, r, ALU.mult))
                link(dve, dve.tensor_copy(midH[:, i, :], r))
                dve.tensor_tensor(midL[:, i, :], r, midH[:, i, :], ALU.subtract).then_inc(mid_ready, 1)
            for b in range(FB):
                if b:
                    after(dve, stages, f"down{b - 1}", pe_finished)
                Group(units, f"up{b}").evacuate(hidden)
                Group(units, f"down{b}").evacuate(add_to_x)

        def finish(eng, name):
            s = {id(pe): pe_finished, id(act): act_finished, id(dve): dve_finished}[id(eng)]
            eng.drain().then_inc(s, 1)

        def after(eng, stages, name, *who):
            for s in who:
                eng.wait_ge(s, stages.index(name) + 1)

        class Attention:

            def __init__(self, sems_of, passes, P_sb, PT_sb, S_sb, stat, y, extra, gate, out_tile,
                         fill):
                self.fill = fill
                (self.s_ready, self.max_ready, self.exp_done, self.p_normed, self.pt_turned, self.pt_ready, self.pv_done,
                 self.o_free, self.bias_turned, self.bias_ready) = sems_of
                self.passes, self.P, self.PT, self.S, self.stat, self.y = passes, P_sb, PT_sb, S_sb, stat, y
                self.extra, self.gate, self.out_tile = extra, gate, out_tile
                self.base = []
                n = 0
                for p in passes:
                    self.base.append(n)
                    n += self.key_tiles(p)
                self.base.append(n)

            def filled(self, g):
                return max(g, 0) * self.fill // NT

            def ended(self, g):
                return self.filled(g + 1) // NK - self.filled(g) // NK

            @staticmethod
            def key_tiles(p):
                return 1 if p["kind"] == "cmp" else NT

            @staticmethod
            def width(p, qt):
                lo, hi = ranges(p["kind"], qt)
                return 31 if p["kind"] == "cmp" else (hi - lo) * P

            @staticmethod
            def queries(p, kt):
                return [qt for qt in range(NT) if ranges(p["kind"], qt)[0] <= kt < ranges(p["kind"], qt)[1]]

            def pe(self, other=None):
                n = len(self.passes)
                for p in range(n + 1):
                    if p < n:
                        self.pe_scores(p, other)
                    if p >= 1:
                        self.pe_values(p - 1)

            def pe_scores(self, p, other):
                w = self.passes[p]
                kind = w["kind"]
                if kind == "fox":
                    pe.wait_ge(self.bias_ready, p) if p else None
                    pe.matmul(B[5][:, :], w["sel"], w["bias"], start=True, stop=True).then_inc(self.bias_turned, 1)
                for qt in range(NT):
                    g = NT * p + qt
                    if g >= 2:
                        pe.wait_ge(self.exp_done, g - 1)
                    lo, hi = ranges(kind, qt)
                    m = self.width(w, qt)
                    keys = w["k"][:, 0:31] if kind == "cmp" else w["k"][:, lo * P:hi * P]
                    masked = []
                    if kind in ("causal", "window", "fox"):
                        masked.append((causal_neg, (qt - lo) * P))
                    if kind == "window" and qt >= 2:
                        masked.append((window_neg, 0))
                    last = pe.matmul(B[g % 2][:, 0:m], w["q"][:, qt * P:(qt + 1) * P], keys, start=True, stop=True,
                                     skip_group_check=True)
                    for j, (mask, at) in enumerate(masked):
                        last = pe.matmul(B[g % 2][:, at:at + P], identb, mask, start=False, stop=True,
                                         skip_group_check=True)
                    last.then_inc(self.s_ready, 1)
                    if other:
                        self.fill_pe(other, g)

            def fill_pe(self, other, g):
                todo = self.filled(g + 1) - self.filled(g)
                while todo:
                    n = min(todo, NK - other.k)
                    other.part(n)
                    todo -= n

            def pe_values(self, p):
                w = self.passes[p]
                nkt = self.key_tiles(w)
                ob = B[4]
                pe.wait_ge(self.p_normed, NT * (p + 1))
                for kt in range(nkt + 1):
                    if kt < nkt:
                        c = self.base[p] + kt
                        if c >= 2:
                            pe.wait_ge(self.pt_ready, c - 1)
                        rows = 31 if w["kind"] == "cmp" else P
                        for qt in self.queries(w, kt):
                            at = 0 if w["kind"] == "cmp" else (kt - ranges(w["kind"], qt)[0]) * P
                            last = pe.transpose(B[2 + c % 2][0:rows, qt * P:(qt + 1) * P],
                                                self.P[:, p % 2, qt, at:at + rows], ident)
                        last.then_inc(self.pt_turned, 1)
                    if kt >= 1:
                        c = self.base[p] + kt - 1
                        pe.wait_ge(self.pt_ready, c + 1)
                        if kt == 1 and w["opens"] and w["pair"]:
                            pe.wait_ge(self.o_free, w["pair"])
                        qs = self.queries(w, kt - 1)
                        rows = 31 if w["kind"] == "cmp" else P
                        half = HD * w["half"]
                        pe.matmul(ob[half:half + HD, qs[0] * P:(qs[-1] + 1) * P], w["v"](kt - 1),
                                  self.PT[0:rows, c % 2, qs[0] * P:(qs[-1] + 1) * P],
                                  start=(w["opens_head"] and kt == 1), stop=True,
                                  skip_group_check=True).then_inc(self.pv_done, 1)

            def act(self, other=None, side=None):
                n = len(self.passes)
                for p in range(n + 1):
                    if p < n:
                        for qt in range(NT):
                            self.act_exp(p, qt)
                            if other:
                                other.split_ahead(self.ended(NT * p + qt - 1))
                            if side:
                                side(NT * p + qt)
                    if p >= 1:
                        self.act_turn(p - 1)
                if other:
                    other.split_ahead()

            def act_exp(self, p, qt):
                w = self.passes[p]
                g = NT * p + qt
                m = self.width(w, qt)
                act.wait_ge(self.max_ready, g + 1)
                if p >= 2 and qt == 0:
                    act.wait_ge(self.pt_turned, self.base[p - 1])
                src = self.S[:, g % 2, 0:m] if w["kind"] in ("fox", "cmp") else B[g % 2][:, 0:m]
                col = (p % 2) * NT + qt
                act.activation(self.P[:, p % 2, qt, 0:m], src, ACT.Exp, scale=SCALE, bias=self.stat[:, 1, col:col + 1],
                               accum_out=self.stat[:, 2, col:col + 1]).then_inc(self.exp_done, 1)

            def act_turn(self, p):
                w = self.passes[p]
                for kt in range(self.key_tiles(w)):
                    c = self.base[p] + kt
                    act.wait_ge(self.pt_turned, c + 1)
                    if c >= 2:
                        act.wait_ge(self.pv_done, c - 1)
                    qs = self.queries(w, kt)
                    rows = 31 if w["kind"] == "cmp" else P
                    a, b = qs[0] * P, (qs[-1] + 1) * P
                    act.activation(self.PT[0:rows, c % 2, a:b], B[2 + c % 2][0:rows, a:b], ACT.Copy).then_inc(self.pt_ready, 1)

            def dve(self, other=None, take=None, side=None):
                n = len(self.passes)
                for p in range(n + 1):
                    if p < n and self.passes[p]["kind"] == "fox":
                        dve.wait_ge(self.bias_turned, p + 1)
                        ins = dve.tensor_copy(self.extra[:, p % 2, :], B[5][:, :])
                        ins.then_inc(self.bias_ready, 1)
                        dve.wait_ge(self.bias_ready, p + 1)
                    for qt in range(NT):
                        if qt == 2 and p >= 1:
                            self.dve_normalise(p - 1)
                        if p < n:
                            self.dve_max(p, qt)
                            if other:
                                other.evacuate(take, self.ended(NT * p + qt - 1))
                            if side and p < n:
                                side(NT * p + qt)
                    if p >= 1 and self.passes[p - 1]["closes"]:
                        self.dve_output(p - 1)
                    if other and p == n - 1:
                        other.evacuate(take)

            def dve_max(self, p, qt):
                w = self.passes[p]
                g = NT * p + qt
                m = self.width(w, qt)
                col = (p % 2) * NT + qt
                dve.wait_ge(self.s_ready, g + 1)
                if w["kind"] in ("fox", "cmp"):
                    bias = self.extra[:, p % 2, 0:m] if w["kind"] == "fox" else w["bias"][:, qt, 0:m]
                    if g >= 2:
                        dve.wait_ge(self.exp_done, g - 1)
                    link(dve, dve.tensor_tensor_reduce(self.S[:, g % 2, 0:m], B[g % 2][:, 0:m], bias, 1.0, -3e38, ALU.add,
                                                       ALU.max, self.stat[:, 0, col:col + 1]))
                else:
                    link(dve, dve.reduce_max(self.stat[:, 0, col:col + 1], B[g % 2][:, 0:m], AX_X))
                dve.tensor_scalar(self.stat[:, 1, col:col + 1], self.stat[:, 0, col:col + 1], -SCALE, None, ALU.mult)\
                    .then_inc(self.max_ready, 1)

            def dve_normalise(self, p):
                w = self.passes[p]
                a, b = (p % 2) * NT, (p % 2) * NT + NT
                dve.wait_ge(self.exp_done, NT * (p + 1))
                link(dve, dve.reciprocal(self.stat[:, 3, a:b], self.stat[:, 2, a:b]))
                if self.gate is not None:
                    link(dve, dve.tensor_tensor(self.stat[:, 3, a:b], self.stat[:, 3, a:b], self.gate[:, :, w["gate"]],
                                                ALU.mult))
                for qt in range(NT):
                    m = self.width(w, qt)
                    pr = self.P[:, p % 2, qt, 0:m]
                    if w["kind"] == "cmp":
                        dve.scalar_tensor_tensor(pr, pr, self.stat[:, 3, a + qt:a + qt + 1], w["keep"][:, qt, 0:m],
                                                 ALU.mult, ALU.mult).then_inc(self.p_normed, 1)
                    else:
                        dve.tensor_scalar(pr, pr, self.stat[:, 3, a + qt:a + qt + 1], None, ALU.mult).then_inc(self.p_normed, 1)

            def dve_output(self, p):
                w = self.passes[p]
                dve.wait_ge(self.pv_done, self.base[p + 1])
                y = self.y(w["pair"])
                dve.tensor_copy(y, B[4][:, :]).then_inc(self.o_free, 1)
                if self.out_tile:
                    dve.wait_ge(self.o_free, w["pair"] + 1)
                    split_dve(*self.out_tile(w["pair"]), y)

        def make_passes(per_head):
            passes = []
            for h, ps in enumerate(per_head):
                for j, p in enumerate(ps):
                    passes.append(dict(p, pair=h // 2, half=h % 2, opens=(h % 2 == 0 and j == 0),
                                       opens_head=(j == 0), closes_head=(j == len(ps) - 1),
                                       closes=(h % 2 == 1 and j == len(ps) - 1)))
            return passes

        def turn_pe(tiles, base):
            for i, t in enumerate(tiles):
                n = base + i
                if n >= 2:
                    pe.wait_ge(v_ready, n - 1)
                for tt in range(NT):
                    last = pe.transpose(B[n % 2][:, tt * P:(tt + 1) * P], t[:, tt * P:(tt + 1) * P], ident)
                last.then_inc(v_turned, 1)

        def turn_act(outs, base):
            for i, o in enumerate(outs):
                n = base + i
                act.wait_ge(v_turned, n + 1)
                act.activation(o, B[n % 2][:, :].rearrange("p (t f) -> p t f", t=NT), ACT.Copy).then_inc(v_ready, 1)

        class Recurrence:

            def __init__(self, dirs, BB, gap, QL, KL, SS):
                self.dirs, self.BB, self.gap, self.QL, self.KL, self.SS = dirs, BB, gap, QL, KL, SS
                self.steps = [(d, h) for d in range(dirs) for h in [T // 2, T // 4] + LEVELS] + [(0, 0)]
                self.n = len(self.steps)

            def fills(self, s):
                return 1 <= s <= 6

            def scores_of(self, d, h):
                if h == T // 2:
                    return [(0, 2, 2), (1, 2, 2)] if d == 0 else [(2, 0, 2), (3, 0, 2)]
                if h == T // 4:
                    return [(0, 1, 1), (2, 3, 1)] if d == 0 else [(1, 0, 1), (3, 2, 1)]
                return [(t, t, 1) for t in range(NT)]

            @staticmethod
            def block_of(jt, it):
                if jt == it:
                    return jt
                far = (jt < 2) != (it < 2)
                if jt < it:
                    return 4 + 2 * jt + it - 2 if far else 8 + jt // 2
                return 10 + 2 * (jt - 2) + it if far else 14 + it // 2

            def dve(self, run, q, ks, both, other=None, take=None):
                for s in range(self.n + 2):
                    if s < self.n and self.steps[s][1]:
                        d, h = self.steps[s]
                        i = self.n * run + s
                        nb = T // (2 * h)
                        X = self.BB[:, d, 1 - d:1 - d + T].rearrange("p (b w) -> p b w", w=2 * h)
                        ref = self.BB[:, d, 0:T].rearrange("p (b w) -> p b w", w=2 * h)[:, :, h:h + 1]\
                            .to_broadcast([P, nb, h])
                        G = self.gap[:, s % 2, :].rearrange("p (b w) -> p b w", w=2 * h)
                        if s >= 2:
                            dve.wait_ge(terms_ready, self.n * run + s - 1)
                        dve.tensor_tensor(G[:, :, 0:h], ref, X[:, :, 0:h], ALU.subtract)
                        dve.tensor_tensor(G[:, :, h:2 * h], X[:, :, h:2 * h], ref, ALU.subtract).then_inc(gap_ready, 1)
                    if 1 <= s <= self.n:
                        d, h = self.steps[s - 1]
                        if h:
                            dve.wait_ge(decay_ready, (self.n - 1) * run + s)
                            if s >= 3:
                                dve.wait_ge(level_scored, self.n * run + s - 2)
                            E = self.gap[:, (s - 1) % 2, :]
                            dve.tensor_tensor(self.QL[:, (s - 1) % 2, :], q, E, ALU.mult)
                            dve.tensor_tensor(self.KL[:, (s - 1) % 2, :], ks[d], E, ALU.mult).then_inc(terms_ready, 1)
                        elif self.dirs == 2:
                            dve.tensor_tensor(both, ks[0], ks[1], ALU.add).then_inc(terms_ready, 1)
                        else:
                            dve.drain().then_inc(terms_ready, 1)
                    if s >= 2:
                        d, h = self.steps[s - 2]
                        i = self.n * run + s - 2
                        dve.wait_ge(level_scored, i + 1)
                        if i:
                            dve.wait_ge(level_kept, i)
                        for a in range(2):
                            bank = B[2 * (i % 2) + a]
                            if h == T // 2:
                                b = 4 if d == 0 else 10
                                last = dve.tensor_copy(self.SS[:, a, b:b + 4, :],
                                                       bank[:, :].rearrange("p (b f) -> p b f", f=P))
                            elif h == T // 4:
                                b = 8 if d == 0 else 14
                                last = dve.tensor_copy(self.SS[:, a, b:b + 2, :],
                                                       bank[:, 0:2 * P].rearrange("p (b f) -> p b f", f=P))
                            else:
                                m = LEVELS.index(h) + d * len(LEVELS) if h else 2 * len(LEVELS)
                                last = dve.copy_predicated(self.SS[:, a, 0:4, :],
                                                           masks[:, m:m + 1, :].to_broadcast([P, NT, P]),
                                                           bank[:, :].rearrange("p (b f) -> p b f", f=P))
                        last.then_inc(level_kept, 1)
                    if other and s >= 1 and self.fills(s - 1):
                        other.evacuate(take, 1)

            def act(self, run, other=None):
                for s in range(self.n - 1):
                    i = (self.n - 1) * run + s
                    act.wait_ge(gap_ready, i + 1)
                    act.activation(self.gap[:, s % 2, :], self.gap[:, s % 2, :], ACT.Exp).then_inc(decay_ready, 1)
                    if other and s >= 1 and self.fills(s - 1):
                        other.split_ahead(1)

            def pe(self, run, q, both, other=None):
                for s in range(self.n):
                    d, h = self.steps[s]
                    i = self.n * run + s
                    if other and self.fills(s):
                        other.products(1)
                    pe.wait_ge(terms_ready, i + 1)
                    if s >= 2:
                        pe.wait_ge(level_kept, i - 1)
                    QQ, KK = (self.QL[:, s % 2, :], self.KL[:, s % 2, :]) if h else (q, both)
                    for a in range(2):
                        r = slice(HD * a, HD * a + HD)
                        at = 0
                        todo = self.scores_of(d, h)
                        for j, (jt, it, w) in enumerate(todo):
                            last = pe.matmul(B[2 * (i % 2) + a][:, at:at + w * P], KK[r, jt * P:(jt + 1) * P],
                                             QQ[r, it * P:(it + w) * P], start=(j == 0), stop=True,
                                             skip_group_check=True)
                            at += w * P
                    last.then_inc(level_scored, 1)

            def pe_values(self, run, a, v, bank, rows):
                pe.wait_ge(level_kept, self.n * (run + 1))
                pairs = [(jt, it) for it in range(NT) for jt in range(NT) if jt <= it or self.dirs == 2]
                for j, (jt, it) in enumerate(pairs):
                    last = pe.matmul(bank[rows, it * P:(it + 1) * P], v(jt), self.SS[:, a, self.block_of(jt, it), :],
                                     start=(j == 0), stop=True, skip_group_check=True)
                return last

        def softplus_of_minus(dst, src, **kw):
            link(act, act.activation(dst, src, ACT.Abs, **kw))
            link(act, act.activation(dst, dst, ACT.Exp, scale=-1.0))
            return act.activation(dst, dst, ACT.Ln, bias=1.0)

        def load_start():
            scope = ExitStack()
            with scope:
                x_tok = sb("x_tok", [P, NT, D], F32, scope)
                masks_f = sb("masks_f", [P, 2 * len(LEVELS) + 1, P], F32, scope)
                with nc.Block() as block:
                    @block.sync
                    def _(sp):
                        sp.dma_start(C[:, :, :], consts_in).then_inc(consts_loaded, 16)
                        sp.dma_start(x_tok[:, :, :], x_in[0].rearrange("(t p) d -> p t d", p=P)).then_inc(x_loaded, 16)
                        sp.dma_start(masks_f[:, :, :], masks_in).then_inc(consts_loaded, 16)
                        sp.dma_start(cosT[:, :], rope_in[0]).then_inc(consts_loaded, 16)
                        sp.dma_start(sinT[:, :], rope_in[1]).then_inc(consts_loaded, 16)

                    @block.tensor
                    def _(pe):
                        pe.wait_ge(consts_loaded, 64)
                        pe.wait_ge(x_loaded, 16)
                        for k in range(NK):
                            if k >= 2:
                                pe.wait_ge(v_ready, k - 1)
                            for t in range(NT):
                                last = pe.transpose(B[k % 2][:, t * P:(t + 1) * P], x_tok[:, t, k * P:(k + 1) * P], ident)
                            last.then_inc(v_turned, 1)

                    @block.scalar
                    def _(act):
                        for k in range(NK):
                            act.wait_ge(v_turned, k + 1)
                            act.activation(xT[:, k, :], B[k % 2][:, :], ACT.Copy).then_inc(v_ready, 1)

                    @block.vector
                    def _(dve):
                        dve.wait_ge(consts_loaded, 64)
                        dve.tensor_copy(masks[:, :, :], masks_f[:, :, :])
                        dve.tensor_copy(Cb[:, 0, :], C[:, 0, :])
                        dve.tensor_copy(Cb[:, 1:4, :], C[:, 7:10, :])
                        dve.memset(lb_now[:, :, 0], NEG)
                        dve.memset(lb_now[:, :, 1], 0.0)
            clear()

        lb_now = sb("lb_now", [P, 4, 2])
        lb_gap = sb("lb_gap", [P, 2, 4])
        bound_gap, bound_softplus = sem("bound_gap"), sem("bound_softplus")

        def next_bounds_act():
            act.wait_ge(bound_gap, 1)
            softplus_of_minus(lb_gap[:, 1, :], lb_gap[:, 0, :]).then_inc(bound_softplus, 1)

        def next_bounds_dve():
            for d, (first, second) in enumerate((("lb_f0", "lb_f1"), ("lb_b0", "lb_b1"))):
                last = dve.tensor_tensor(lb_gap[:, 0, 2 * d:2 * d + 2], vec[:, V1[second]:V1[second] + 2],
                                         vec[:, V1[first]:V1[first] + 2], ALU.subtract)
            last.then_inc(bound_gap, 1)
            dve.wait_ge(bound_softplus, 1)
            link(dve, dve.scalar_tensor_tensor(lb_now[:, :, 0], lb_gap[:, 0, :], 0.0, lb_gap[:, 1, :],
                                               ALU.min, ALU.subtract))
            dve.tensor_tensor(lb_now[:, :, 1], lb_now[:, :, 0], lb_gap[:, 0, :], ALU.subtract)

        def first_layer(L):
            units, first_unit, first_tile = plan_units(GROUPS1)
            stages = STAGES1
            new_layer()
            scope = ExitStack()
            with scope:
                tmp = sb("tmp", [P, T], F32, scope)
                pair = sb("pair", [P, 2, T], F32, scope)
                pair_r = sb("relu_sb", [P, 2, T], F32, scope)
                yt = sb("yt", [P, 2, T], F32, scope)
                conv_u = sb("conv_u", [P, 2, T + 30], F32, scope)
                conv_c = sb("conv_c", [P, 2, T], F32, scope)
                with ExitStack() as mlp_scope:
                    midH = sb("midH", [P, NK, T], F32R, mlp_scope)
                    midL = sb("midL", [P, NK, T], F32R, mlp_scope)
                    H2 = sb("H2", [P, NK, T], F32R, mlp_scope)
                    L2 = sb("L2", [P, NK, T], F32R, mlp_scope)
                Z = sb("Z", [P, 20, T], F32, scope)
                phases = {}
                with ExitStack() as s1:
                    phases["att"] = dict(P=sb("probs", [P, 2, NT, T], F32, s1), PT=sb("probsT", [P, 2, T], F32, s1),
                                         y=sb("att_y", [P, 4, T], F32, s1), stat=sb("stat", [P, 4, 8], F32, s1))
                with ExitStack() as s1:
                    phases["hgrn"] = dict(BB=sb("cum", [P, 2, T + 1], F32, s1), gap=sb("gap", [P, 2, T], F32, s1),
                                          QL=sb("QL", [P, 2, T], F32, s1),
                                          KL=sb("KL", [P, 2, T], F32, s1), SS=sb("SS", [P, 2, 16, P], F32, s1),
                                          keys=sb("keys", [P, 3, T], F32, s1), t=sb("terms", [P, 3, T], F32, s1))
                with ExitStack() as s1:
                    phases["conv"] = dict(u=conv_u, c=conv_c, s=sb("conv_s", [P, 2, T], F32, s1), m=sb("conv_m", [P, T], F32, s1))
                v_tok = [Z[:, t, :].rearrange("p (t f) -> p t f", t=NT) for t in (5, 8, 9)]
                A, Hg, Cv = phases["att"], phases["hgrn"], phases["conv"]

                passes = make_passes([[dict(kind="full", q=Z[HD * (h // 4):HD * (h // 4) + HD, h % 4, :],
                                            k=Z[HD * (h // 4):HD * (h // 4) + HD, 4, :],
                                            v=(lambda kt, g=h // 4: v_tok[0][:, kt, HD * g:HD * g + HD]))]
                                      for h in range(8)])
                att = Attention(attention_sems[0], passes, A["P"], A["PT"], None, A["stat"], lambda t: A["y"][:, t, :], None,
                                None, None, fill=14)
                rec = Recurrence(2, Hg["BB"], Hg["gap"], Hg["QL"], Hg["KL"], Hg["SS"])

                with nc.Block() as block:
                    @block.sync
                    def _(sp):
                        sp.dma_start(vec[:, 0:NV1], vec1_in[bass.ds(L, 1)].rearrange("a p n -> (a p) n"))\
                            .then_inc(vec_loaded, 16)
                        load_weights(units, w1_in, L)

                    @block.gpsimd
                    def _(pool):
                        split_lo(units)

                    @block.tensor
                    def _(pe):
                        finish(pe, "start")
                        Group(units, "att_in").products(ready=h_ready(0), sums=square_sums(0, pair))
                        finish(pe, "att_in")
                        after(pe, stages, "att_in", dve_finished)
                        for t in range(5):
                            pe.wait_ge(z_squared, t + 1)
                            pe.matmul(B[0][:, :], pair_ones, pair[:, t % 2, :], start=True, stop=True).then_inc(z_summed, 1)
                            pe.wait_ge(z_normed, t + 1)
                            pe.matmul(B[1][:, :], rot1, Z[:, t, :], start=True, stop=True).then_inc(z_rotated, 1)
                        finish(pe, "prep")
                        after(pe, stages, "prep", act_finished, dve_finished)
                        turn_pe([Z[:, 5, :]], 0)
                        pe.wait_ge(v_ready, 1)
                        att.pe(Group(units, "rest_in"))
                        finish(pe, "att")
                        after(pe, stages, "att", act_finished, dve_finished)
                        for r in range(2):
                            turn_pe([Z[:, 8 + r, :]], 1 + r)
                            pe.wait_ge(v_ready, 2 + r)
                            rec.pe(r, Z[:, 6 + r, :], Hg["keys"][:, 2, :])
                            for a in range(2):
                                last = rec.pe_values(r, a, lambda jt: v_tok[1 + r][:, jt, HD * a:HD * a + HD], B[4],
                                                     slice(HD * a, HD * a + HD))
                            last.then_inc(o_ready, 1)
                            pe.wait_ge(o_squared, r + 1)
                            pe.matmul(B[5][:, :], pair_ones, pair[:, 0, :], start=True, stop=True).then_inc(o_summed, 1)
                        finish(pe, "hgrn")
                        after(pe, stages, "hgrn", act_finished, dve_finished)
                        for j in range(2):
                            last = pe.matmul(B[0][:, :], ones, Cv["c"][:, j, :], start=(j == 0), stop=(j == 1))
                        last.then_inc(conv_summed, 1)
                        for j in range(2):
                            pe.wait_ge(conv_squared, j + 1)
                            last = pe.matmul(B[1][:, :], ones, Cv["s"][:, j, :], start=(j == 0), stop=(j == 1))
                        last.then_inc(conv_var, 1)
                        finish(pe, "conv")
                        after(pe, stages, "conv", dve_finished)
                        out_pe(units, pair)
                        mlp_pe(units, H2, L2, midH, midL, pair)

                    @block.scalar
                    def _(act):
                        split_hi(units, 0)
                        split_hi(units, 1)
                        act.wait_ge(vec_loaded, 16)
                        scale_act(0, V1["norm_mix"], yt, pair)
                        finish(act, "start")
                        Group(units, "att_in").split_ahead()
                        finish(act, "att_in")
                        after(act, stages, "att_in", dve_finished)
                        for t in range(5):
                            if t >= 2:
                                act.wait_ge(z_summed, t - 1)
                            act.activation(pair[:, t % 2, :], Z[:, t, :], ACT.Square).then_inc(z_squared, 1)
                            act.wait_ge(z_summed, t + 1)
                            if t:
                                act.wait_ge(z_normed, t)
                            link(act, act.activation(tmp[:, :], B[0][:, :], ACT.Ln, bias=EPS, scale=1.0 / HD))
                            act.activation(tmp[:, :], tmp[:, :], ACT.Exp, scale=-0.5).then_inc(z_rstd, 1)
                        finish(act, "prep")
                        after(act, stages, "prep", pe_finished, dve_finished)
                        turn_act([v_tok[0]], 0)

                        def conv_gates(g):
                            if g == CONV_AT - 1:
                                act.wait_ge(conv_in, 2)
                                for j in range(2):
                                    act.activation(conv_c[:, j, :], Z[:, 18 + j, :], ACT.Sigmoid).then_inc(conv_gate, 1)
                                act.preload_act_table_set(LOG_EXP)
                        att.act(Group(units, "rest_in"), conv_gates)
                        finish(act, "att")
                        after(act, stages, "att", pe_finished, dve_finished)
                        for r in range(2):
                            act.activation(pair[:, r, :], Z[:, 14 + r, :], ACT.Sigmoid).then_inc(gate_ready, 1)
                        act.preload_act_table_set(LOG_EXP)
                        act.wait_ge(gate_used, 1)
                        for r in range(2):
                            turn_act([v_tok[1 + r]], 1 + r)
                            for d in range(2):
                                f = Z[:, 10 + 2 * d + r, :]
                                i = 2 * r + d
                                if i:
                                    act.wait_ge(key_ready, i)
                                link(act, softplus_of_minus(Hg["t"][:, 0, :], f))
                                softplus_of_minus(Hg["t"][:, 1, :], f, scale=-1.0, bias=lb_now[:, 2 * d + r, 0:1])\
                                    .then_inc(softplus_ready, 1)
                                act.wait_ge(rate_ready, i + 1)
                                act.activation(Hg["keys"][:, d, :], Hg["t"][:, 0, :], ACT.Exp,
                                               bias=lb_now[:, 2 * d + r, 1:2]).then_inc(key_ready, 1)
                            rec.act(r)
                            act.wait_ge(o_taken, r + 1)
                            act.activation(pair[:, 0, :], yt[:, 0, :], ACT.Square).then_inc(o_squared, 1)
                            act.wait_ge(o_summed, r + 1)
                            link(act, act.activation(tmp[:, :], B[5][:, :], ACT.Ln, bias=EPS, scale=1.0 / HD))
                            act.activation(tmp[:, :], tmp[:, :], ACT.Exp, scale=-0.5).then_inc(o_rstd, 1)
                        finish(act, "hgrn")
                        after(act, stages, "hgrn", pe_finished, dve_finished)
                        for j in range(2):
                            act.wait_ge(conv_mean, j + 1)
                            act.activation(Cv["s"][:, j, :], Cv["c"][:, j, :], ACT.Square).then_inc(conv_squared, 1)
                        act.wait_ge(conv_var, 1)
                        link(act, act.activation(tmp[:, :], B[1][:, :], ACT.Ln, bias=EPS, scale=1.0 / (2 * P)))
                        act.activation(tmp[:, :], tmp[:, :], ACT.Exp, scale=-0.5).then_inc(conv_rstd, 1)
                        for j in range(2):
                            act.wait_ge(conv_pre, j + 1)
                            act.activation(Cv["s"][:, j, :], Cv["c"][:, j, :], ACT.Sigmoid).then_inc(conv_gate, 1)
                        finish(act, "conv")
                        act.preload_act_table_set(LOG_EXP)
                        next_bounds_act()
                        out_act(units, V1["norm_mlp"], yt, pair)
                        mlp_act(units)

                    @block.vector
                    def _(dve):
                        dve.wait_ge(vec_loaded, 16)
                        for k in range(NK):
                            scale_dve(0, yt, hH, hL, k)
                        finish(dve, "start")
                        dve.wait_ge(rstd_ready, 1)

                        def to_Z(first):
                            def take(i, a, free, value):
                                dve.tensor_tensor(Z[:, first + i, :], a[:, :], rstd[:, :], ALU.mult).then_inc(free, 1)
                            return take
                        Group(units, "att_in").evacuate(to_Z(0))
                        finish(dve, "att_in")
                        for t in range(5):
                            col = V1["q_norm"] if t < 4 else V1["k_norm"]
                            dve.wait_ge(z_rstd, t + 1)
                            ins = dve.scalar_tensor_tensor(Z[:, t, :], Z[:, t, :], vec[:, col:col + 1], tmp[:, :],
                                                           ALU.mult, ALU.mult)
                            ins.then_inc(z_normed, 1)
                            dve.wait_ge(z_normed, t + 1)
                            dve.wait_ge(z_rotated, t + 1)
                            link(dve, dve.tensor_tensor(yt[:, 0, :], B[1][:, :], sinT[:, :], ALU.mult))
                            link(dve, dve.tensor_tensor(yt[:, 1, :], Z[:, t, :], cosT[:, :], ALU.mult))
                            link(dve, dve.tensor_tensor(Z[:, t, :], yt[:, 0, :], yt[:, 1, :], ALU.add))
                        finish(dve, "prep")
                        after(dve, stages, "prep", pe_finished, act_finished)
                        taps = [(tap, j) for tap in range(31) for j in range(2)]
                        slots = NT * len(passes) - CONV_AT

                        def conv_taps(g):
                            if g == CONV_AT:
                                for j in range(2):
                                    dve.memset(conv_u[:, j, 0:15], 0.0)
                                    dve.memset(conv_u[:, j, T + 15:T + 30], 0.0)
                                    dve.wait_ge(conv_gate, j + 1)
                                    link(dve, dve.tensor_tensor(conv_u[:, j, 15:T + 15], Z[:, 16 + j, :], conv_c[:, j, :],
                                                                ALU.mult))
                            s = g - CONV_AT
                            for i in range(max(s, 0) * len(taps) // slots, max(s + 1, 0) * len(taps) // slots):
                                tap, j = taps[i]
                                w, b = V1["conv_w"] + 2 * tap + j, V1["conv_b"] + j
                                src = conv_u[:, j, tap:tap + T]
                                if tap == 0:
                                    ins = dve.tensor_scalar(conv_c[:, j, :], src, vec[:, w:w + 1], vec[:, b:b + 1],
                                                            ALU.mult, ALU.add)
                                else:
                                    dve.wait_ge(conv_tapped, i - 1)
                                    ins = dve.scalar_tensor_tensor(conv_c[:, j, :], src, vec[:, w:w + 1], conv_c[:, j, :],
                                                                   ALU.mult, ALU.add)
                                ins.then_inc(conv_tapped, 1)

                        def rest_to_Z(i, a, free, value):
                            to_Z(16 if i < 4 else 6 - 4)(i, a, free, value)
                            if i in (2, 3):
                                dve.wait_ge(free, value)
                                dve.drain().then_inc(conv_in, 1)
                        att.dve(Group(units, "rest_in"), rest_to_Z, conv_taps)
                        finish(dve, "att")
                        after(dve, stages, "att", pe_finished, act_finished)
                        for t in range(4):
                            split_dve(hH[:, t, :], hL[:, t, :], A["y"][:, t, :])
                        t_, BB, keys = Hg["t"], Hg["BB"], Hg["keys"]
                        for r in range(2):
                            dve.wait_ge(gate_ready, r + 1)
                            last = dve.tensor_tensor(Z[:, 14 + r, :], pair[:, r, :], Z[:, 14 + r, :], ALU.mult)
                        last.then_inc(gate_used, 1)
                        dve.memset(BB[:, :, 0:1], 0.0)
                        dve.memset(Hg["SS"][:, :, :, :], 0.0)
                        for r in range(2):
                            for d in range(2):
                                f = Z[:, 10 + 2 * d + r, :]
                                i = 2 * r + d
                                dve.wait_ge(softplus_ready, i + 1)
                                link(dve, dve.tensor_scalar(t_[:, 2, :], f, -1.0, lb_now[:, 2 * d + r, 0:1], ALU.mult, ALU.add))
                                link(dve, dve.scalar_tensor_tensor(t_[:, 2, :], t_[:, 2, :], 0.0, t_[:, 1, :],
                                                                   ALU.max, ALU.add))
                                link(dve, dve.scalar_tensor_tensor(t_[:, 0, :], f, 0.0, t_[:, 0, :], ALU.min, ALU.subtract))
                                link(dve, dve.tensor_tensor(t_[:, 2, :], t_[:, 2, :], t_[:, 0, :], ALU.add))
                                link(dve, dve.tensor_tensor_scan(BB[:, d, 1:T + 1], ones[:, 0:1].to_broadcast([P, T]),
                                                                 t_[:, 2, :], 0.0, ALU.mult, ALU.add))
                                dve.tensor_tensor(t_[:, 0, :], t_[:, 0, :], f, ALU.subtract).then_inc(rate_ready, 1)
                            dve.wait_ge(key_ready, 2 * r + 2)
                            rec.dve(r, Z[:, 6 + r, :], [keys[:, 0, :], keys[:, 1, :]], keys[:, 2, :])
                            dve.wait_ge(o_ready, r + 1)
                            dve.tensor_copy(yt[:, 0, :], B[4][:, :]).then_inc(o_taken, 1)
                            dve.wait_ge(o_rstd, r + 1)
                            col = V1["hgrn_norm"] + r
                            link(dve, dve.scalar_tensor_tensor(yt[:, 0, :], yt[:, 0, :], vec[:, col:col + 1], tmp[:, :],
                                                               ALU.mult, ALU.mult))
                            link(dve, dve.tensor_tensor(yt[:, 0, :], yt[:, 0, :], Z[:, 14 + r, :], ALU.mult))
                            split_dve(hH[:, 4 + r, :], hL[:, 4 + r, :], yt[:, 0, :])
                        finish(dve, "hgrn")
                        after(dve, stages, "hgrn", pe_finished, act_finished)
                        c, s_ = Cv["c"], Cv["s"]
                        dve.wait_ge(conv_summed, 1)
                        link(dve, dve.tensor_scalar(Cv["m"][:, :], B[0][:, :], 1.0 / (2 * P), None, ALU.mult))
                        for j in range(2):
                            dve.tensor_tensor(c[:, j, :], c[:, j, :], Cv["m"][:, :], ALU.subtract).then_inc(conv_mean, 1)
                        dve.wait_ge(conv_rstd, 1)
                        for j in range(2):
                            g, b = V1["ln_g"] + j, V1["ln_b"] + j
                            link(dve, dve.tensor_tensor(c[:, j, :], c[:, j, :], tmp[:, :], ALU.mult))
                            dve.tensor_scalar(c[:, j, :], c[:, j, :], vec[:, g:g + 1], vec[:, b:b + 1], ALU.mult, ALU.add)\
                                .then_inc(conv_pre, 1)
                        for j in range(2):
                            dve.wait_ge(conv_gate, 3 + j)
                            link(dve, dve.tensor_tensor(c[:, j, :], c[:, j, :], s_[:, j, :], ALU.mult))
                            split_dve(hH[:, 6 + j, :], hL[:, 6 + j, :], c[:, j, :])
                        finish(dve, "conv")
                        next_bounds_dve()
                        out_dve(units, yt, H2, L2)
                        mlp_dve(units, stages, midH, midL, pair_r)
            clear()

        stacked, cmp_loaded, cmp_used, blocks_ready, hidden_ready, hidden_gelu, cmp_made, cmp_taken, cmp_turned = (
            sem(n) for n in ("stacked", "cmp_loaded", "cmp_used", "blocks_ready", "hidden_ready", "hidden_gelu", "cmp_made",
                             "cmp_taken", "cmp_turned"))
        mask_loaded = sem("mask_loaded")
        alpha_loaded, branch_mixed, z_made, sp_part, sp_ready, logit_ready, a_ready, stick_done, stick_taken = (
            sem(n) for n in ("alpha_loaded", "branch_mixed", "z_made", "sp_part", "sp_ready", "logit_ready", "a_ready",
                             "stick_done", "stick_taken"))
        gate_turned, angle_ready, sine_ready, alpha_made, alpha_biased = (
            sem(n) for n in ("gate_turned", "angle_ready", "sine_ready", "alpha_made", "alpha_biased"))

        def start_second():
            new_layer()
            turn = 2 * np.pi
            parts = [6.28125]
            parts.append(float(np.float32(round((turn - parts[0]) * 2 ** 20) / 2 ** 20)))
            parts.append(turn - parts[0] - parts[1])
            to_whole = 1.5 * 2 ** 23
            edge = 3.1415925
            scope = ExitStack()
            with scope:
                pos = sb("pos", [P, T], I32, scope)
                freq = sb("freq", [P, 2], F32, scope)
                ang, n, s2 = (sb(x, [P, T], F32, scope) for x in ("ang", "turns", "s2"))
                with nc.Block() as block:
                    @block.sync
                    def _(sp):
                        sp.dma_start(pos[:, :], pos_in[0:1, :].to_broadcast([P, T])).then_inc(x_loaded, 16)
                        sp.dma_start(freq[:, :], freq_in).then_inc(x_loaded, 16)

                    @block.vector
                    def _(dve):
                        dve.wait_ge(x_loaded, 32)
                        link(dve, dve.tensor_copy(ang[:, :], pos[:, :]))
                        link(dve, dve.tensor_scalar(ang[:, :], ang[:, :], freq[:, 0:1], None, ALU.mult))
                        link(dve, dve.tensor_scalar(n[:, :], ang[:, :], 1.0 / turn, to_whole, ALU.mult, ALU.add))
                        link(dve, dve.tensor_scalar(n[:, :], n[:, :], -to_whole, None, ALU.add))
                        for part in parts:
                            link(dve, dve.scalar_tensor_tensor(ang[:, :], n[:, :], -part, ang[:, :], ALU.mult, ALU.add))
                        dve.tensor_scalar(ang[:, :], ang[:, :], -edge, edge, ALU.max, ALU.min).then_inc(angle_ready, 1)
                        dve.wait_ge(sine_ready, 1)
                        link(dve, dve.tensor_tensor(s2[:, :], s2[:, :], s2[:, :], ALU.mult))
                        dve.tensor_scalar(cosT[:, :], s2[:, :], -2.0, 1.0, ALU.mult, ALU.add)

                    @block.scalar
                    def _(act):
                        act.wait_ge(angle_ready, 1)
                        act.activation(sinT[:, :], ang[:, :], ACT.Sin)
                        act.activation(s2[:, :], ang[:, :], ACT.Sin, scale=0.5).then_inc(sine_ready, 1)
            clear()

        def second_layer(L):
            units, first_unit, first_tile = plan_units(GROUPS2)
            stages = STAGES2
            new_layer()
            scope = ExitStack()
            with scope:
                tmp = sb("tmp2", [P, T], F32, scope)
                pair = sb("pair2", [P, 2, T], F32, scope)
                yt = sb("yt2", [P, 2, T], F32, scope)
                with ExitStack() as s1:
                    midH = sb("midH2", [P, NK, T], F32R, s1)
                    midL = sb("midL2", [P, NK, T], F32R, s1)
                mixed = sb("mixed", [P, NK, T], F32, scope)
                yH = sb("yH", [P, 4, T], F32R, scope)
                yL = sb("yL", [P, 4, T], F32R, scope)
                small = sb("small", [P, T], F32, scope)
                with ExitStack() as s1:
                    H2, L2 = sb("H2_2", [P, NK, T], F32R, s1), sb("L2_2", [P, NK, T], F32R, s1)
                    pair_r = sb("relu2", [P, 2, T], F32, s1)
                Z0 = sb("Z0", [P, 12, T], F32, scope)
                Z1 = sb("Z1", [P, 12, T], F32, scope)
                with ExitStack() as s1:
                    sig = sb("sig", [P, 4, T], F32, s1)
                with ExitStack() as s1:
                    stack = sb("stack", [P, 4, T], F32, s1)
                    blocks_sb = sb("cblocks", [P, 16, 62], F32, s1)
                    cw1 = [sb("cw1", [P, 16, 256], F32, s1)[:, :, :], mixed[:, :, :].rearrange("p k (a c) -> p (k a) c", c=256)]
                kc = Z0[:, 10, 0:31]
                vc = Z0[0:31, 10, 32:160]
                hid = Z0[:, 10, 160:284].rearrange("p (m c) -> p m c", m=2)
                kraw = Z0[:, 10, 288:319]
                cw2 = [z.rearrange("p (m c) -> p m c", m=2) for z in (Z0[:, 10, 320:448], Z0[:, 11, 344:472])]
                kt2 = Z0[:, 10, 448:510]
                gate = Z0[:, 11, 0:96].rearrange("p (t c) -> p t c", t=NT)
                cm = Z0[:, 11, 96:344].rearrange("p (m t c) -> p m t c", m=2, t=NT)
                with ExitStack() as s1:
                    probs = sb("probs2", [P, 2, NT, T], F32, s1)
                    probsT = sb("probsT2", [P, 2, T], F32, s1)
                    S_sb = sb("S_sb", [P, 2, T], F32, s1)
                    stat = sb("stat2", [P, 4, 8], F32, s1)
                    bias_sb = sb("bias_sb", [P, 2, T], F32, s1)
                with ExitStack() as s1:
                    part = sb("sp_part_sb", [P, NT, T], F32, s1)
                    soft = sb("soft_sb", [P, NT, T], F32, s1)
                    aT = sb("aT", [P, NT, T], F32, s1)
                with ExitStack() as s1:
                    BB = sb("cum2", [P, 1, T + 1], F32, s1)
                    gap = sb("gap2", [P, 2, T], F32, s1)
                    QL, KL = sb("QL2", [P, 2, T], F32, s1), sb("KL2", [P, 2, T], F32, s1)
                    SS = sb("SS2", [P, 2, 10, P], F32, s1)
                    alpha = sb("alpha", [P, 256], F32, s1)
                turned0, turned1 = ([z[:, t, :].rearrange("p (t f) -> p t f", t=NT) for t in range(12)] for z in (Z0, Z1))

                def y_tile(t):
                    return yH[:, t, :], yL[:, t, :]

                nsa = []
                for h in range(8):
                    g = h // 4
                    r = slice(HD * g, HD * g + HD)
                    q = Z0[r, h % 4, :]
                    nsa.append([
                        dict(kind="causal", q=q, k=Z0[r, 6, :], v=lambda kt, r=r: turned0[7][:, kt, r], gate=3 * h + 1),
                        dict(kind="window", q=q, k=Z0[r, 8, :], v=lambda kt, r=r: turned0[9][:, kt, r], gate=3 * h + 2),
                        dict(kind="cmp", q=q, k=kc[r, :], v=lambda kt, r=r: vc[:, r], gate=3 * h, bias=cm[:, 0],
                             keep=cm[:, 1])])
                att = Attention(attention_sems[0], make_passes(nsa), probs, probsT, S_sb, stat, lambda t: yt[:, 0, :], None, gate, y_tile,
                                fill=4)
                forget = []
                for h in range(8):
                    r = slice(HD * (h % 2), HD * (h % 2) + HD)
                    forget.append([dict(kind="fox", q=Z1[r, h // 2, :], k=Z1[r, 4 + h // 2, :],
                                        v=lambda kt, r=r, t=8 + h // 2: turned1[t][:, kt, r],
                                        sel=ident[64:96, 64 + h:65 + h].to_broadcast([32, P]), bias=small[64:96, :])])
                fox = Attention(attention_sems[1], make_passes(forget), probs, probsT, S_sb, stat, lambda t: yt[:, 0, :], bias_sb, None,
                                y_tile, fill=8)
                rec = Recurrence(1, BB, gap, QL, KL, SS)

                with nc.Block() as block:
                    @block.sync
                    def _(sp):
                        sp.dma_start(vec[:, 0:NV2], vec2_in[bass.ds(L, 1)].rearrange("a p n -> (a p) n"))\
                            .then_inc(vec_loaded, 16)
                        load_weights(units, w2_in, L)

                    @block.gpsimd
                    def _(pool):
                        split_lo(units)

                    def operands(nk):
                        return (hH, hL) if nk == NK else (yH, yL)

                    @block.tensor
                    def _(pe):
                        finish(pe, "start")
                        Group(units, "nsa_in").products(ready=h_ready(0), sums=square_sums(0, pair))
                        finish(pe, "nsa_in")
                        after(pe, stages, "nsa_in", dve_finished)
                        for i, t in enumerate((0, 1, 2, 3, 6, 8)):
                            if i:
                                pe.wait_ge(z_done, i)
                            pe.matmul(B[0][:, :], rot2, Z0[:, t, :], start=True, stop=True).then_inc(z_rotated, 1)
                        for t in range(NT):
                            last = pe.transpose(B[1][:, t * P:(t + 1) * P], small[:, t * P:(t + 1) * P], ident)
                        last.then_inc(gate_turned, 1)
                        finish(pe, "prep")
                        after(pe, stages, "prep", act_finished, dve_finished)
                        for kv in range(2):
                            pe.wait_ge(blocks_ready, kv + 1)
                            pe.wait_ge(cmp_loaded, 64)
                            for m in range(2):
                                for j in range(16):
                                    last = pe.matmul(B[0][:, m * 62:m * 62 + 62], cw1[kv][:, j, m * P:(m + 1) * P],
                                                     blocks_sb[:, j, :], start=(j == 0 and m == 0), stop=(j == 15 and m == 1),
                                                     skip_group_check=True)
                            last.then_inc(hidden_ready, 1)
                            pe.wait_ge(hidden_gelu, kv + 1)
                            for g in range(2):
                                r = slice(HD * g, HD * g + HD)
                                for m in range(2):
                                    h_ = hid[:, m, 31 * g:31 * g + 31]
                                    if kv == 0:
                                        last = pe.matmul(B[1][r, 0:31], cw2[kv][:, m, :], h_, start=(m == 0), stop=(m == 1))
                                    else:
                                        last = pe.matmul(B[2][0:31, r], h_, cw2[kv][:, m, :], start=(m == 0 and g == 0),
                                                         stop=(m == 1 and g == 1), skip_group_check=True)
                            last.then_inc(cmp_made, 1)
                            if kv == 0:
                                pe.wait_ge(cmp_taken, 1)
                                pe.matmul(B[3][:, 0:31], rot2, kraw, start=True, stop=True).then_inc(cmp_turned, 1)
                        finish(pe, "cmp")
                        after(pe, stages, "cmp", act_finished, dve_finished)
                        turn_pe([Z0[:, 7, :], Z0[:, 9, :]], 0)
                        pe.wait_ge(v_ready, 2)
                        att.pe(Group(units, "stick_in"))
                        finish(pe, "att")
                        gated = Group(units, "mix0", operands)
                        gated.products(4)
                        after(pe, stages, "att", act_finished, dve_finished)
                        gated.products()
                        finish(pe, "mix0")
                        after(pe, stages, "mix0", act_finished, dve_finished)
                        turn_pe([Z1[:, 8 + t, :] for t in range(4)], 2)
                        pe.wait_ge(v_ready, 6)
                        gla_in = Group(units, "gla_in")
                        for h in range(8):
                            r = slice(HD * (h % 2), HD * (h % 2) + HD)
                            if h:
                                pe.wait_ge(a_ready, NT * h)
                            for j in reversed(range(NT)):
                                pe.matmul(B[j][:, 0:T - j * P], Z1[r, 4 + h // 2, j * P:(j + 1) * P], Z1[r, h // 2, j * P:T],
                                          start=True, stop=True).then_inc(z_made, 1)
                            gla_in.products(1)
                            for j in reversed(range(NT)):
                                pe.wait_ge(sp_ready, NT * h + NT - j)
                                pe.matmul(B[j][:, 0:T - j * P], neg_tri, soft[:, j, 0:T - j * P], start=False, stop=True,
                                          skip_group_check=True)
                                for i in range(j + 1, NT):
                                    pe.matmul(B[j][:, (i - j) * P:T - j * P], neg_ones, soft[:, i, 0:T - i * P],
                                              start=False, stop=True, skip_group_check=True)
                                pe.matmul(B[j][:, 0:P], identb, later_neg, start=False, stop=True,
                                          skip_group_check=True).then_inc(logit_ready, 1)
                            gla_in.products(h % 2)
                            if h % 2 == 0 and h:
                                pe.wait_ge(stick_taken, h // 2)
                            pe.wait_ge(a_ready, NT * h + NT)
                            for j in range(NT):
                                last = pe.matmul(B[4][r, j * P:T], turned1[8 + h // 2][:, j, r], aT[:, j, 0:T - j * P],
                                                 start=(j == 0), stop=True, skip_group_check=True)
                            last.then_inc(stick_done, 1)
                        finish(pe, "stick")
                        gated = Group(units, "mix1", operands)
                        gated.products(4)
                        after(pe, stages, "stick", act_finished, dve_finished)
                        gated.products()
                        finish(pe, "mix1")
                        after(pe, stages, "mix1", act_finished, dve_finished)
                        pe.wait_ge(alpha_loaded, 16)
                        fox_in = Group(units, "fox_in")
                        for run in range(2):
                            if run:
                                pe.wait_ge(o_rstd, 2)
                            pe.matmul(B[5][:, :], alpha[32:48, run * P:(run + 1) * P], small[32:48, :], start=True, stop=True)\
                                .then_inc(alpha_made, 1)
                            turn_pe([Z0[:, 4 + 2 * run + a, :] for a in range(2)], 6 + 2 * run)
                            pe.wait_ge(v_ready, 8 + 2 * run)
                            rec.pe(run, Z0[:, run, :], Z0[:, 2 + run, :], fox_in)
                            for a in range(2):
                                rec.pe_values(run, a, lambda jt: turned0[4 + 2 * run + a][:, jt, :], B[4], slice(0, P))\
                                    .then_inc(o_ready, 1)
                                pe.wait_ge(o_squared, 2 * run + a + 1)
                                pe.wait_ge(alpha_biased, run + 1)
                                if a:
                                    pe.wait_ge(o_rstd, 2 * run + 1)
                                pe.matmul(B[5][:, :], ones, pair[:, 0, :], start=True, stop=True).then_inc(o_summed, 1)
                        finish(pe, "recur")
                        gated = Group(units, "mix2", operands)
                        gated.products(4)
                        after(pe, stages, "recur", act_finished, dve_finished)
                        gated.products()
                        finish(pe, "mix2")
                        after(pe, stages, "mix2", act_finished, dve_finished)
                        turn_pe([Z1[:, 8 + t, :] for t in range(4)], 10)
                        pe.wait_ge(v_ready, 14)
                        pe.wait_ge(decay_summed, 1)
                        fox.pe(Group(units, "gate3"))
                        finish(pe, "forget")
                        after(pe, stages, "forget", act_finished, dve_finished)
                        Group(units, "mix3", operands).products()
                        finish(pe, "mix3")
                        after(pe, stages, "mix3", dve_finished)
                        out_pe(units, pair)
                        mlp_pe(units, H2, L2, midH, midL, pair)

                    @block.scalar
                    def _(act):
                        split_hi(units, 0)
                        split_hi(units, 1)
                        act.wait_ge(vec_loaded, 16)
                        for kv in range(2):
                            act.dma_start(cw1[kv].rearrange("p j c -> p (j c)"),
                                          cmpw_in[bass.ds(L, 1), kv].rearrange("a p n -> (a p) n")).then_inc(cmp_loaded, 16)
                            act.dma_start(cw2[kv].rearrange("p m c -> p (m c)"),
                                          cmpw2_in[bass.ds(L, 1), kv].rearrange("a p n -> (a p) n")).then_inc(cmp_loaded, 16)
                        scale_act(0, V2["norm_mix"], yt, pair)
                        finish(act, "start")
                        Group(units, "nsa_in").split_ahead()
                        finish(act, "nsa_in")
                        after(act, stages, "nsa_in", dve_finished)
                        for kv in range(2):
                            for g in range(2):
                                r = slice(HD * g, HD * g + HD)
                                act.dma_start(stack[0:HD, 2 * kv + g, :], Z0[r, 4 + kv, :]).then_inc(stacked, 16)
                                act.dma_start(stack[HD:P, 2 * kv + g, 0:T - 1], Z0[r, 4 + kv, 1:T]).then_inc(stacked, 16)

                        def mix(branch):
                            ahead = Group(units, f"mix{branch}")
                            for half in range(2):
                                for i in range(4):
                                    n = NK * branch + 4 * half + i
                                    ahead.split_ahead(1)
                                    col = V2["b_gate"] + n
                                    act.wait_ge(gate_scaled, n + 1)
                                    act.activation(sig[:, i, :], sig[:, i, :], ACT.Sigmoid, bias=vec[:, col:col + 1])\
                                        .then_inc(gate_opened, 1)
                                ahead.split_ahead(4)
                            act.preload_act_table_set(LOG_EXP)
                            finish(act, f"mix{branch}")

                        act.wait_ge(gate_turned, 1)
                        act.dma_start(cm.rearrange("p m t c -> p (m t c)"), cmpmask_in.rearrange("p m t c -> p (m t c)"))\
                            .then_inc(mask_loaded, 16)
                        act.activation(gate, B[1][:, :].rearrange("p (t f) -> p t f", t=NT)[:, :, 0:24], ACT.Sigmoid)
                        finish(act, "prep")
                        after(act, stages, "prep", pe_finished, dve_finished)
                        for kv in range(2):
                            act.wait_ge(hidden_ready, kv + 1)
                            act.activation(hid, B[0][:, 0:124].rearrange("p (m c) -> p m c", m=2), ACT.Gelu_apprx_tanh)\
                                .then_inc(hidden_gelu, 1)
                        finish(act, "cmp")
                        after(act, stages, "cmp", pe_finished, dve_finished)
                        act.preload_act_table_set(LOG_EXP)
                        turn_act([turned0[7], turned0[9]], 0)
                        att.act(Group(units, "stick_in"))
                        finish(act, "att")
                        after(act, stages, "att", pe_finished, dve_finished)
                        mix(0)
                        after(act, stages, "mix0", pe_finished, dve_finished)
                        turn_act([turned1[8 + t] for t in range(4)], 2)
                        gla_in = Group(units, "gla_in")
                        for h in range(8):
                            for j in reversed(range(NT)):
                                n = NT * h + NT - 1 - j
                                act.wait_ge(z_made, n + 1)
                                if h:
                                    act.wait_ge(sp_ready, n + 1 - NT)
                                softplus_of_minus(part[:, j, 0:T - j * P], B[j][:, 0:T - j * P]).then_inc(sp_part, 1)
                            gla_in.split_ahead(1)
                            if h:
                                act.wait_ge(stick_done, h)
                            for j in reversed(range(NT)):
                                act.wait_ge(logit_ready, NT * h + NT - j)
                                act.activation(aT[:, j, 0:T - j * P], B[j][:, 0:T - j * P], ACT.Exp).then_inc(a_ready, 1)
                            gla_in.split_ahead(h % 2)
                        finish(act, "stick")
                        after(act, stages, "stick", pe_finished, dve_finished)
                        mix(1)
                        after(act, stages, "mix1", pe_finished, dve_finished)
                        act.dma_start(alpha[32:48, :], alpha_in[bass.ds(L, 1)].rearrange("a p n -> (a p) n"))\
                            .then_inc(alpha_loaded, 16)
                        for i in range(4):
                            if i >= 2:
                                act.wait_ge(gate_used, i - 1)
                            act.activation(pair[:, i % 2, :], Z0[:, 8 + i, :], ACT.Sigmoid).then_inc(gate_ready, 1)
                        act.preload_act_table_set(LOG_EXP)
                        act.wait_ge(gate_used, 4)
                        fox_in = Group(units, "fox_in")
                        for run in range(2):
                            turn_act([turned0[4 + 2 * run + a] for a in range(2)], 6 + 2 * run)
                            act.wait_ge(alpha_biased, run + 1)
                            softplus_of_minus(tmp[:, :], yt[:, 0, :]).then_inc(softplus_ready, 1)
                            rec.act(run, fox_in)
                            for a in range(2):
                                i = 2 * run + a
                                act.wait_ge(o_taken, i + 1)
                                act.activation(pair[:, 0, :], yt[:, 0, :], ACT.Square).then_inc(o_squared, 1)
                                act.wait_ge(o_summed, i + 1)
                                link(act, act.activation(tmp[:, :], B[5][:, :], ACT.Ln, bias=EPS, scale=1.0 / P))
                                act.activation(tmp[:, :], tmp[:, :], ACT.Exp, scale=-0.5).then_inc(o_rstd, 1)
                        finish(act, "recur")
                        after(act, stages, "recur", pe_finished, dve_finished)
                        mix(2)
                        after(act, stages, "mix2", pe_finished, dve_finished)
                        act.wait_ge(alpha_biased, 3)
                        softplus_of_minus(tmp[64:96, :], yt[64:96, 0, :]).then_inc(softplus_ready, 1)
                        turn_act([turned1[8 + t] for t in range(4)], 10)
                        fox.act(Group(units, "gate3"))
                        finish(act, "forget")
                        after(act, stages, "forget", pe_finished, dve_finished)
                        ahead = Group(units, "mix3")
                        for n in range(NK):
                            col = V2["b_gate"] + 3 * NK + n
                            act.activation(Z0[:, n, :], Z0[:, n, :], ACT.Sigmoid, bias=vec[:, col:col + 1])\
                                .then_inc(gate_opened, 1)
                            ahead.split_ahead(1)
                        finish(act, "mix3")
                        after(act, stages, "mix3", dve_finished)
                        out_act(units, V2["norm_ff"], yt, pair)
                        mlp_act(units)

                    @block.vector
                    def _(dve):
                        dve.wait_ge(vec_loaded, 16)
                        for k in range(NK):
                            scale_dve(0, yt, hH, hL, k)
                        finish(dve, "start")
                        dve.wait_ge(rstd_ready, 1)

                        def take_to(tile, scaled=0):
                            def take(i, a, free, value):
                                if i < scaled:
                                    ins = dve.scalar_tensor_tensor(tile(i), a[:, :], SCALE, rstd[:, :], ALU.mult, ALU.mult)
                                else:
                                    ins = dve.tensor_tensor(tile(i), a[:, :], rstd[:, :], ALU.mult)
                                ins.then_inc(free, 1)
                            return take

                        to_Z0, to_Z1 = (lambda i: Z0[:, i, :]), (lambda i: Z1[:, i, :])
                        Group(units, "nsa_in").evacuate(take_to(lambda i: Z0[:, i, :] if i < 10 else small[:, :]))
                        finish(dve, "nsa_in")
                        for i, t in enumerate((0, 1, 2, 3, 6, 8)):
                            dve.wait_ge(z_rotated, i + 1)
                            link(dve, dve.tensor_tensor(yt[:, 0, :], B[0][:, :], sinT[:, :], ALU.mult))
                            link(dve, dve.tensor_tensor(yt[:, 1, :], Z0[:, t, :], cosT[:, :], ALU.mult))
                            dve.tensor_tensor(Z0[:, t, :], yt[:, 0, :], yt[:, 1, :], ALU.add).then_inc(z_done, 1)
                        finish(dve, "prep")
                        after(dve, stages, "prep", pe_finished, act_finished)
                        dve.wait_ge(mask_loaded, 16)
                        for kv in range(2):
                            dve.wait_ge(stacked, 128)
                            if kv:
                                dve.wait_ge(hidden_ready, 1)
                            for j in range(16):
                                col = V2["pe_v" if kv else "pe_k"] + j
                                last = dve.tensor_scalar(blocks_sb[:, j, :].rearrange("p (g c) -> p g c", g=2),
                                                         stack[:, 2 * kv:2 * kv + 2, 2 * j:2 * j + 481:16],
                                                         vec[:, col:col + 1], None, ALU.add)
                            last.then_inc(blocks_ready, 1)
                            dve.wait_ge(cmp_made, kv + 1)
                            if kv == 0:
                                ins = dve.tensor_copy(kraw, B[1][:, 0:31])
                                ins.then_inc(cmp_taken, 1)
                                dve.wait_ge(cmp_taken, 1)
                                dve.wait_ge(cmp_turned, 1)
                                dve.tensor_tensor(kt2[:, 0:31], kraw, cosT[:, 31:T:16], ALU.mult)
                                link(dve, dve.tensor_tensor(kt2[:, 31:62], B[3][:, 0:31], sinT[:, 31:T:16], ALU.mult))
                                link(dve, dve.tensor_tensor(kc, kt2[:, 0:31], kt2[:, 31:62], ALU.add))
                            else:
                                dve.tensor_copy(vc, B[2][0:31, 0:P])
                        finish(dve, "cmp")
                        after(dve, stages, "cmp", pe_finished, act_finished)
                        att.dve(Group(units, "stick_in"), take_to(to_Z1, 4))
                        finish(dve, "att")
                        after(dve, stages, "att", pe_finished, act_finished)

                        def mix(branch):
                            def take(t, a, free, value):
                                i, half = t % 4, t // 8
                                n, f = NK * branch + 4 * half + i, 4 * half + i
                                if t % 8 < 4:
                                    if half:
                                        dve.wait_ge(branch_mixed, NK * branch + 4)
                                    dve.tensor_tensor(sig[:, i, :], a[:, :], rstd[:, :], ALU.mult).then_inc(free, 1)
                                    dve.wait_ge(free, value)
                                    dve.drain().then_inc(gate_scaled, 1)
                                    return
                                dve.wait_ge(gate_opened, n + 1)
                                add_branch(branch, f, sig[:, i, :], a, free, value)
                            Group(units, f"mix{branch}").evacuate(take)
                            finish(dve, f"mix{branch}")
                            after(dve, stages, f"mix{branch}", pe_finished, act_finished)

                        def add_branch(branch, f, gates, a, free, value):
                            if branch == 0:
                                link(dve, dve.tensor_tensor(mixed[:, f, :], a[:, :], gates, ALU.mult))
                                dve.drain().then_inc(free, 1)
                                dve.drain().then_inc(branch_mixed, 1)
                            else:
                                dve.tensor_tensor(yt[:, f % 2, :], a[:, :], gates, ALU.mult).then_inc(free, 1)
                                dve.wait_ge(free, value)
                                dve.tensor_tensor(mixed[:, f, :], mixed[:, f, :], yt[:, f % 2, :], ALU.add)\
                                    .then_inc(branch_mixed, 1)

                        mix(0)
                        gla_in = Group(units, "gla_in")
                        for h in range(8):
                            for j in reversed(range(NT)):
                                n = NT * h + NT - 1 - j
                                w = T - j * P
                                dve.wait_ge(sp_part, n + 1)
                                if h:
                                    dve.wait_ge(logit_ready, NT * h)
                                link(dve, dve.scalar_tensor_tensor(soft[:, j, 0:w], B[j][:, 0:w], 0.0, part[:, j, 0:w],
                                                                   ALU.max, ALU.add))
                                dve.tensor_tensor(soft[:, j, 0:P], soft[:, j, 0:P], later_one, ALU.mult).then_inc(sp_ready, 1)
                            gla_in.evacuate(take_to(to_Z0, 2), 1)
                            gla_in.evacuate(take_to(to_Z0, 2), h % 2)
                            if h % 2:
                                dve.wait_ge(stick_done, h + 1)
                                ins = dve.tensor_copy(yt[:, 0, :], B[4][:, :])
                                ins.then_inc(stick_taken, 1)
                                dve.wait_ge(stick_taken, h // 2 + 1)
                                split_dve(yH[:, h // 2, :], yL[:, h // 2, :], yt[:, 0, :])
                        finish(dve, "stick")
                        after(dve, stages, "stick", pe_finished, act_finished)
                        mix(1)
                        for i in range(4):
                            dve.wait_ge(gate_ready, i + 1)
                            dve.tensor_tensor(Z0[:, 8 + i, :], pair[:, i % 2, :], Z0[:, 8 + i, :], ALU.mult).then_inc(gate_used, 1)
                        fox_in = Group(units, "fox_in")
                        dve.memset(BB[:, :, 0:1], 0.0)
                        dve.memset(SS[:, :, :, :], 0.0)
                        for run in range(2):
                            col = V2["b_alpha"] + run
                            dve.wait_ge(alpha_made, run + 1)
                            dve.tensor_scalar(yt[:, 0, :], B[5][:, :], vec[:, col:col + 1], None, ALU.add)\
                                .then_inc(alpha_biased, 1)
                            dve.wait_ge(softplus_ready, run + 1)
                            link(dve, dve.scalar_tensor_tensor(yt[:, 1, :], yt[:, 0, :], 0.0, tmp[:, :], ALU.min, ALU.subtract))
                            link(dve, dve.tensor_scalar(yt[:, 1, :], yt[:, 1, :], 1.0 / 16, None, ALU.mult))
                            link(dve, dve.tensor_tensor_scan(BB[:, 0, 1:T + 1], ones[:, 0:1].to_broadcast([P, T]),
                                                             yt[:, 1, :], 0.0, ALU.mult, ALU.add))
                            rec.dve(run, Z0[:, run, :], [Z0[:, 2 + run, :]], None, fox_in, take_to(to_Z1))
                            for a in range(2):
                                i = 2 * run + a
                                dve.wait_ge(o_ready, i + 1)
                                dve.tensor_copy(yt[:, 0, :], B[4][:, :]).then_inc(o_taken, 1)
                                dve.wait_ge(o_rstd, i + 1)
                                col = V2["gla_norm"]
                                link(dve, dve.scalar_tensor_tensor(yt[:, 0, :], yt[:, 0, :], vec[:, col:col + 1], tmp[:, :],
                                                                   ALU.mult, ALU.mult))
                                link(dve, dve.tensor_tensor(yt[:, 0, :], yt[:, 0, :], Z0[:, 8 + i, :], ALU.mult))
                                split_dve(yH[:, i, :], yL[:, i, :], yt[:, 0, :])
                        finish(dve, "recur")
                        after(dve, stages, "recur", pe_finished, act_finished)
                        mix(2)
                        r = slice(64, 96)
                        col = V2["fox_b"]
                        dve.tensor_scalar(yt[r, 0, :], small[r, :], vec[r, col:col + 1], None, ALU.add)\
                            .then_inc(alpha_biased, 1)
                        dve.wait_ge(softplus_ready, 3)
                        link(dve, dve.scalar_tensor_tensor(yt[r, 1, :], yt[r, 0, :], 0.0, tmp[r, :], ALU.min, ALU.subtract))
                        link(dve, dve.tensor_tensor_scan(yt[r, 0, :], ones[r, 0:1].to_broadcast([32, T]), yt[r, 1, :], 0.0,
                                                         ALU.mult, ALU.add))
                        dve.tensor_scalar(small[r, :], yt[r, 0, :], -1.0 / SCALE, None, ALU.mult).then_inc(decay_summed, 1)
                        fox.dve(Group(units, "gate3"), take_to(to_Z0))
                        finish(dve, "forget")
                        after(dve, stages, "forget", pe_finished, act_finished)

                        def take_last(i, a, free, value):
                            dve.wait_ge(gate_opened, 3 * NK + i + 1)
                            add_branch(3, i, Z0[:, i, :], a, free, value)
                        Group(units, "mix3").evacuate(take_last)
                        for k in range(NK):
                            split_dve(hH[:, k, :], hL[:, k, :], mixed[:, k, :])
                        finish(dve, "mix3")
                        out_dve(units, yt, H2, L2)
                        mlp_dve(units, stages, midH, midL, pair_r)
            clear()

        def store_result(gcol=None):
            new_layer()
            scope = ExitStack()
            with scope:
                tmp = sb("f_tmp", [P, T], F32, scope)
                pair = sb("f_pair", [P, 2, T], F32, scope)
                y = sb("f_y", [P, NK, T], F32, scope)
                x_tok = sb("f_tok", [P, NT, D], F32, scope)
                with nc.Block() as block:
                    @block.tensor
                    def _(pe):
                        for k in range(NK):
                            square_sums(0, pair)(k)
                        for t in range(NT):
                            for half in range(2):
                                n = 2 * t + half
                                if n == 0:
                                    pe.wait_ge(key_ready, 1)
                                if n >= 2:
                                    pe.wait_ge(v_ready, n - 1)
                                for k in range(4):
                                    last = pe.transpose(B[1 + n % 2][:, k * P:(k + 1) * P],
                                                        y[:, 4 * half + k, t * P:(t + 1) * P], ident)
                                last.then_inc(v_turned, 1)

                    @block.scalar
                    def _(act):
                        act.preload_act_table_set(LOG_EXP)
                        for k in range(NK):
                            if k >= 2:
                                act.wait_ge(sq_summed, k - 1)
                            act.activation(pair[:, k % 2, :], xT[:, k, :], ACT.Square).then_inc(sq_ready, 1)
                        act.wait_ge(sq_summed, NK)
                        link(act, act.activation(tmp[:, :], B[0][:, :], ACT.Ln, bias=EPS, scale=1.0 / D))
                        act.activation(tmp[:, :], tmp[:, :], ACT.Exp, scale=-0.5).then_inc(rstd_ready, 1)
                        for n in range(2 * NT):
                            act.wait_ge(v_turned, n + 1)
                            act.activation(x_tok[:, n // 2, (n % 2) * T:(n % 2) * T + T], B[1 + n % 2][:, :], ACT.Copy)\
                                .then_inc(v_ready, 1)

                    @block.vector
                    def _(dve):
                        dve.wait_ge(rstd_ready, 1)
                        for k in range(NK):
                            g = V2["final"] + k
                            last = dve.scalar_tensor_tensor(y[:, k, :], xT[:, k, :], vec[:, g:g + 1], tmp[:, :],
                                                            ALU.mult, ALU.mult)
                        last.then_inc(key_ready, 1)

                    @block.sync
                    def _(sp):
                        for t in range(NT):
                            sp.wait_ge(v_ready, 2 * t + 2)
                            sp.dma_start(out[0, t * P:(t + 1) * P, :], x_tok[:, t, :]).then_inc(stored, 16)
                        sp.wait_ge(stored, 16 * NT)
            clear()

        def probe(i):
            with nc.Block() as block:
                @block.sync
                def _(sp):
                    sp.dma_start(probes[i], xT[:, :, :]).then_inc(stored, 16)
                    sp.wait_ge(stored, 16)
            clear()

        load_start()
        if 1 in blocks:
            with nc.Fori(0, layers) as L:
                first_layer(L)
            if probes is not None:
                probe(0)
        if 2 in blocks:
            start_second()
            with nc.Fori(0, layers) as L:
                second_layer(L)
        if 2 in blocks:
            store_result()


def constants():
    f = np.float32
    i = np.arange(P)
    row, col = i[:, None], i[None, :]
    c = {"ident": np.eye(P), "ones": np.ones((P, P)), "pair_ones": (row // HD == col // HD),
         "neg_tri": -(row >= col).astype(f), "neg_ones": -np.ones((P, P)),
         "causal_neg": np.where(col > row, NEG, 0), "window_neg": np.where(col <= row, NEG, 0),
         "later_neg": np.where(col <= row, NEG, 0), "later_one": col > row}
    for name, half, width, n in (("rot1", 16, 32, HD), ("rot2", 8, 16, 16)):
        R = np.zeros((P, P), f)
        for base in range(0, P, HD):
            for start in range(0, n, width):
                for j in range(half):
                    a, b = base + start + j, base + start + half + j
                    R[b, a], R[a, b] = -1, 1
        c[name] = R
    consts = np.stack([np.asarray(c[k], f) for k in CONSTS], axis=1)
    m = []
    for h in LEVELS:
        m.append((row // (2 * h) == col // (2 * h)) & (row % (2 * h) < h) & (col % (2 * h) >= h))
    m += [x.T for x in m] + [np.eye(P, dtype=bool)]
    t = np.arange(T)
    axis = HD // 2
    inv = (10000.0 ** (-np.arange(0, axis, 2, dtype=f) / axis)).astype(f)
    ang = np.stack([(t // 64).astype(f)[:, None] * inv, (t % 64).astype(f)[:, None] * inv])
    rope = np.zeros((2, P, T), f)
    for p in range(P):
        d = p % HD
        a = ang[d // axis][:, d % (axis // 2)]
        rope[0, p], rope[1, p] = np.cos(a), np.sin(a)
    end = np.arange(31) * 16 + 31
    tok = t.reshape(NT, P).T
    keep = (end[None, None, :] <= tok[:, :, None])
    cmpmask = np.stack([np.where(keep, 0, NEG), keep], axis=1).astype(f)
    sel = np.zeros((32, 8, P), f)
    for h in range(8):
        sel[h, h, :] = 1
    freq = np.zeros((P, 2), f)
    inv2 = (500000.0 ** (-np.arange(0, 16, 2, dtype=f) / 16)).astype(f)
    for p in range(P):
        if p % HD < 16:
            freq[p, 0] = inv2[p % HD % 8]
    return (consts, np.stack(m, axis=1).astype(f), rope, cmpmask, sel, freq)


def columns(a):
    return a.reshape(a.shape[0], -1, P).transpose(0, 2, 1)


def tiles(w, nk, cols):
    return w.reshape(w.shape[0], nk, P, cols).transpose(0, 2, 1, 3).reshape(w.shape[0], P, nk * cols)


def mlp_units(up, down):
    return [u for b in range(FB) for u in cut(up[:, :, b * D:(b + 1) * D]) + cut(down[:, b * D:(b + 1) * D])]


def cut(w):
    return [tiles(w[:, :, j:j + P], NK, P) for j in range(0, w.shape[2], P)]


def head_order(w):
    return w.reshape(w.shape[0], w.shape[1], 2, 4, HD).transpose(0, 1, 3, 2, 4).reshape(w.shape)


def stream1(w_in, w_out, up, down):
    conv = 16 * P
    w = np.concatenate([head_order(w_in[:, :, 0:512]), w_in[:, :, 512:768], w_in[:, :, conv:], w_in[:, :, 768:conv], w_out],
                       axis=2)
    return np.stack(cut(w) + mlp_units(up, down), axis=1)


def stream2(w_in, w_branch, w_out, up, down):
    q, rest = head_order(w_in[:, :, 0:512]), w_in[:, :, 512:1280]
    g, sb_w, gla, lowrank, gla_g = (w_in[:, :, a:b] for a, b in ((1280, 1304), (1304, 2840), (2840, 3864), (3864, 3880),
                                                              (3880, 4392)))
    fox, fox_f, gates = w_in[:, :, 4392:5928], w_in[:, :, 5928:5936], w_in[:, :, 5936:]
    z = lambda n: np.zeros(w_in.shape[:2] + (n,), w_in.dtype)
    small = np.concatenate([g, z(8), lowrank, z(16), fox_f, z(56)], axis=2)
    gate = lambda n: cut(gates[:, :, n * D:(n + 1) * D])
    branch = lambda n: [tiles(w_branch[:, n, :, j:j + 256], 4, 256) for j in range(0, D, 256)]
    mix = lambda n: gate(n)[0:4] + branch(n)[0:2] + gate(n)[4:8] + branch(n)[2:4]
    units = cut(np.concatenate([q, rest, small], axis=2)) + cut(sb_w) + mix(0)
    units += cut(np.concatenate([gla, gla_g], axis=2)) + mix(1) + cut(fox) + mix(2) + gate(3) + branch(3) + cut(w_out)
    return np.stack(units + mlp_units(up, down), axis=1)


def kernel(x, w_in, w_out, norm_mix, norm_mlp, q_norm, k_norm, hgrn_lb_fwd, hgrn_lb_bwd, hgrn_norm, conv_w, conv_b,
           conv_ln_g, conv_ln_b, w_mlp_in, w_mlp_out, positions_2, norm_mix_2, w_in_2, b_gate_2, nsa_cmp_pos_k_2,
           nsa_cmp_pos_v_2, nsa_cmp_wk1_2, nsa_cmp_wk2_2, nsa_cmp_wv1_2, nsa_cmp_wv2_2, gla_w_alpha_2, gla_b_alpha_2,
           gla_norm_2, fox_b_f_2, w_branch_2, w_out_2, norm_ff_2, w_ff1_2, w_ff2_2, norm_final_2):
    import concourse.bacc as bacc
    from concourse.bass_utils import run_bass_kernel_spmd

    a = np.asarray
    both = lambda v: np.concatenate([a(v), a(v)], axis=1)
    lb_f = np.broadcast_to(a(hgrn_lb_fwd).reshape(1, 1, -1), (DEPTH, 1, 2 * 256)).reshape(DEPTH, -1)
    lb_b = np.broadcast_to(a(hgrn_lb_bwd).reshape(1, 1, -1), (DEPTH, 1, 2 * 256)).reshape(DEPTH, -1)
    vec1 = np.concatenate([columns(v) for v in (
        a(norm_mix), a(norm_mlp), both(q_norm), both(k_norm), lb_f, lb_b, a(hgrn_norm), a(conv_b), a(conv_ln_g),
        a(conv_ln_b), a(conv_w).reshape(DEPTH, -1))], axis=2)
    fox_b = np.zeros((DEPTH, P), np.float32)
    fox_b[:, 64:72] = a(fox_b_f_2)
    final = np.broadcast_to(a(norm_final_2)[None], (DEPTH, D))
    vec2 = np.concatenate([columns(v) for v in (
        a(norm_mix_2), a(norm_ff_2), a(b_gate_2), a(nsa_cmp_pos_k_2).reshape(DEPTH, -1),
        a(nsa_cmp_pos_v_2).reshape(DEPTH, -1), a(gla_b_alpha_2), a(gla_norm_2), fox_b, final)], axis=2)
    consts, masks, rope, cmpmask, sel, freq = constants()
    cmpw = np.stack([tiles(a(w), 16, 256) for w in (nsa_cmp_wk1_2, nsa_cmp_wv1_2)], axis=1)
    cmpw2 = np.stack([tiles(a(w), 2, HD) for w in (nsa_cmp_wk2_2, nsa_cmp_wv2_2)], axis=1)
    arrays = {
        "x": a(x), "consts": consts, "masks": masks, "rope": rope, "cmpmask": cmpmask, "sel": sel, "freq": freq,
        "vec1": vec1, "vec2": vec2,
        "stream1": stream1(a(w_in), a(w_out), a(w_mlp_in), a(w_mlp_out)),
        "stream2": stream2(a(w_in_2), a(w_branch_2), a(w_out_2), a(w_ff1_2), a(w_ff2_2)),
        "positions": a(positions_2), "cmpw": cmpw, "cmpw2": cmpw2, "alpha": a(gla_w_alpha_2),
    }
    arrays = {k: np.ascontiguousarray(v) for k, v in arrays.items()}
    nc = bacc.Bacc("TRN2", target_bir_lowering=False, num_devices=1)
    t = {k: nc.dram_tensor(f"in_{k}", v.shape, mybir.dt.from_np(v.dtype), kind="ExternalInput").ap()
         for k, v in arrays.items()}
    out = nc.dram_tensor("out", (1, T, D), F32, kind="ExternalOutput").ap()
    program(nc, t, out)
    r = run_bass_kernel_spmd(nc, [{f"in_{k}": v for k, v in arrays.items()}], core_ids=[0])
    return r.results[0]["out"]
```
